# Optimizing a Trainium2 kernel written in Bass

```python
import jax, jax.numpy as jnp
from jax import lax
import numpy as np

D_MODEL = 1024
BATCH = 1
SEQ = 256
DEPTH = 2

CHUNK = 64
Q_BLOCK = 128
ROPE_BASE = 10000.0
EPS = 1e-6

MLA_HEADS = 8
MLA_NOPE = 64
MLA_ROPE = 32
MLA_V = 64
MLA_Q_LORA = 256
MLA_KV_LORA = 128
FOX_HEADS = 8
FOX_DIM = 64
RET_HEADS = 4
RET_QK = 256
RET_V = 512
N_GROUPS = 4
EXPERTS_PER_GROUP = 8
N_EXPERTS = N_GROUPS * EXPERTS_PER_GROUP
TOP_K = 2
D_EXPERT = 512
MOE_BLOCK = 128

N_EVEN = (DEPTH + 1) // 2
N_ODD = DEPTH // 2
EVEN_IN = MLA_Q_LORA + MLA_KV_LORA + MLA_ROPE + 3 * FOX_HEADS * FOX_DIM + FOX_HEADS
EVEN_MIX = MLA_HEADS * MLA_V + FOX_HEADS * FOX_DIM
ODD_IN = 2 * RET_HEADS * RET_QK + 2 * RET_HEADS * RET_V
ODD_MIX = RET_HEADS * RET_V

kernel_name = 'hybrid_mla_fox_retention_hmoe'

def _rms(x):
    xf = x.astype(jnp.float32)
    return xf * lax.rsqrt(jnp.mean(jnp.square(xf), axis=-1, keepdims=True) + EPS)

def rmsnorm(x, g):
    return (_rms(x) * g.astype(jnp.float32)).astype(x.dtype)

def rope(x):
    s, d = x.shape[1], x.shape[-1]
    half = d // 2
    inv = ROPE_BASE ** (-jnp.arange(half, dtype=jnp.float32) / half)
    ang = jnp.arange(s, dtype=jnp.float32)[:, None] * inv[None, :]
    cos = jnp.cos(ang)[None, :, None, :]
    sin = jnp.sin(ang)[None, :, None, :]
    xf = x.astype(jnp.float32)
    x1, x2 = xf[..., :half], xf[..., half:]
    return jnp.concatenate([x1 * cos - x2 * sin, x1 * sin + x2 * cos], axis=-1).astype(x.dtype)

def block_attention(q_a, k_a, v_a, q_b, k_b, v_b, cum):
    s = q_a.shape[2]
    n_blk = s // Q_BLOCK
    kpos = jnp.arange(s)
    scale_a = (MLA_NOPE + MLA_ROPE) ** -0.5
    scale_b = FOX_DIM ** -0.5

    def one(i):
        start = i * Q_BLOCK
        qpos = start + jnp.arange(Q_BLOCK)
        qa = lax.dynamic_slice_in_dim(q_a, start, Q_BLOCK, axis=2)
        s_a = jnp.einsum('bhqd,bhkd->bhqk', qa, k_a, preferred_element_type=jnp.float32) * scale_a
        chunk_mask = (kpos[None, :] // CHUNK) <= (qpos[:, None] // CHUNK)
        p_a = jax.nn.softmax(jnp.where(chunk_mask, s_a, -jnp.inf), axis=-1)
        o_a = jnp.einsum('bhqk,bhkd->bhqd', p_a.astype(v_a.dtype), v_a)
        qb = lax.dynamic_slice_in_dim(q_b, start, Q_BLOCK, axis=2)
        cq = lax.dynamic_slice_in_dim(cum, start, Q_BLOCK, axis=2)
        s_b = (jnp.einsum('bhqd,bhkd->bhqk', qb, k_b, preferred_element_type=jnp.float32) * scale_b
               + cq[..., :, None] - cum[..., None, :])
        causal = kpos[None, :] <= qpos[:, None]
        p_b = jax.nn.softmax(jnp.where(causal, s_b, -jnp.inf), axis=-1)
        o_b = jnp.einsum('bhqk,bhkd->bhqd', p_b.astype(v_b.dtype), v_b)
        return o_a, o_b

    o_a, o_b = lax.map(one, jnp.arange(n_blk))

    def merge(o):
        nb, b, h, qb_, d = o.shape
        return o.transpose(1, 0, 3, 2, 4).reshape(b, nb * qb_, h * d)

    return merge(o_a), merge(o_b)

def even_mixer(h, w_in, ln_q, w_uq, ln_kv, w_ukv, b_f, w_out):
    b, s, _ = h.shape
    z = h @ w_in
    cuts = np.cumsum([MLA_Q_LORA, MLA_KV_LORA, MLA_ROPE, FOX_HEADS * FOX_DIM,
                      FOX_HEADS * FOX_DIM, FOX_HEADS * FOX_DIM]).tolist()
    c_q, c_kv, k_pe, q_f, k_f, v_f, f_logit = jnp.split(z, cuts, axis=-1)
    q = (rmsnorm(c_q, ln_q) @ w_uq).reshape(b, s, MLA_HEADS, MLA_NOPE + MLA_ROPE)
    q = jnp.concatenate([q[..., :MLA_NOPE], rope(q[..., MLA_NOPE:])], axis=-1)
    kv = (rmsnorm(c_kv, ln_kv) @ w_ukv).reshape(b, s, MLA_HEADS, MLA_NOPE + MLA_V)
    k_pe = jnp.broadcast_to(rope(k_pe[:, :, None, :]), (b, s, MLA_HEADS, MLA_ROPE))
    k = jnp.concatenate([kv[..., :MLA_NOPE], k_pe], axis=-1)
    v = kv[..., MLA_NOPE:]
    log_f = jax.nn.log_sigmoid(f_logit.astype(jnp.float32) + b_f.astype(jnp.float32))
    cum = jnp.cumsum(log_f, axis=1).transpose(0, 2, 1)
    fh = lambda t: t.reshape(b, s, FOX_HEADS, FOX_DIM).transpose(0, 2, 1, 3)
    tr = lambda t: t.transpose(0, 2, 1, 3)
    o_a, o_b = block_attention(tr(q), tr(k), tr(v), fh(q_f), fh(k_f), fh(v_f), cum)
    return jnp.concatenate([o_a, o_b], axis=-1) @ w_out

def retention(q, k, v):
    b, s, h, dk = q.shape
    dv = v.shape[-1]
    n = s // CHUNK
    q, k, v = (t.astype(jnp.float32) for t in (q, k, v))
    log_g = jnp.log(1.0 - jnp.exp2(-5.0 - jnp.arange(h, dtype=jnp.float32)))
    j = jnp.arange(CHUNK, dtype=jnp.float32)
    diff = j[:, None] - j[None, :]
    dmask = jnp.where(diff >= 0, jnp.exp(jnp.maximum(diff, 0.0)[None] * log_g[:, None, None]), 0.0)
    xi = jnp.exp((j[:, None] + 1.0) * log_g[None, :])
    zeta = jnp.exp((CHUNK - 1.0 - j)[:, None] * log_g[None, :])
    g_c = jnp.exp(CHUNK * log_g)
    qc = q.reshape(b, n, CHUNK, h, dk)
    kc = k.reshape(b, n, CHUNK, h, dk)
    vc = v.reshape(b, n, CHUNK, h, dv)
    inner = jnp.einsum('bnchd,bnmhd->bnhcm', qc, kc) * dmask
    o_inner = jnp.einsum('bnhcm,bnmhe->bnche', inner, vc)

    def step(state, xs):
        qn, kn, vn = xs
        cross = jnp.einsum('bchd,bhde->bche', qn, state) * xi[None, :, :, None]
        state = g_c[None, :, None, None] * state + jnp.einsum(
            'bchd,bche->bhde', kn * zeta[None, :, :, None], vn)
        return state, cross

    state0 = jnp.zeros((b, h, dk, dv), jnp.float32)
    lead = lambda t: t.transpose(1, 0, 2, 3, 4)
    _, cross = lax.scan(step, state0, (lead(qc), lead(kc), lead(vc)))
    return (o_inner + lead(cross)).reshape(b, s, h, dv)

def odd_mixer(h, w_in, w_out):
    b, s, _ = h.shape
    z = h @ w_in
    cuts = np.cumsum([RET_HEADS * RET_QK, RET_HEADS * RET_QK, RET_HEADS * RET_V]).tolist()
    q, k, v, g = jnp.split(z, cuts, axis=-1)
    q = rope(q.reshape(b, s, RET_HEADS, RET_QK))
    k = rope(k.reshape(b, s, RET_HEADS, RET_QK)) * (RET_QK ** -0.5)
    v = v.reshape(b, s, RET_HEADS, RET_V)
    o = _rms(retention(q, k, v)).reshape(b, s, ODD_MIX)
    return (o.astype(h.dtype) * jax.nn.silu(g)) @ w_out

def expert_dispatch(xt, eid, gate, w_gate, w_up, w_down):
    t, d = xt.shape
    a = t * TOP_K
    e_flat = eid.reshape(a)
    w_flat = gate.reshape(a)
    tok = jnp.arange(a, dtype=jnp.int32) // TOP_K
    order = jnp.argsort(e_flat)
    e_s, tok_s, w_s = e_flat[order], tok[order], w_flat[order]
    counts = jnp.bincount(e_flat, length=N_EXPERTS)
    start = jnp.cumsum(counts) - counts
    padded = ((counts + MOE_BLOCK - 1) // MOE_BLOCK) * MOE_BLOCK
    pend = jnp.cumsum(padded)
    pstart = pend - padded
    dest = pstart[e_s] + (jnp.arange(a) - start[e_s])
    cap = a + N_EXPERTS * MOE_BLOCK
    n_blk = cap // MOE_BLOCK
    slot_tok = jnp.full((cap,), t, jnp.int32).at[dest].set(tok_s)
    slot_w = jnp.zeros((cap,), jnp.float32).at[dest].set(w_s)
    blk_expert = jnp.minimum(
        jnp.searchsorted(pend, jnp.arange(n_blk) * MOE_BLOCK, side='right'), N_EXPERTS - 1)
    x_pad = jnp.concatenate([xt, jnp.zeros((1, d), xt.dtype)], axis=0)
    xs = x_pad[slot_tok].reshape(n_blk, MOE_BLOCK, d)

    def run(args):
        xb, e = args
        hid = jax.nn.silu(xb @ w_gate[e]) * (xb @ w_up[e])
        return hid @ w_down[e]

    ys = lax.map(run, (xs, blk_expert)).reshape(cap, d)
    out = jax.ops.segment_sum(ys * slot_w[:, None].astype(ys.dtype), slot_tok, num_segments=t + 1)
    return out[:t]

def hier_moe(h, w_rg, b_rg, w_re, b_re, w_gate, w_up, w_down):
    b, s, d = h.shape
    t = b * s
    xt = h.reshape(t, d)
    g_logits = (xt @ w_rg).astype(jnp.float32) + b_rg.astype(jnp.float32)
    g_prob = jax.nn.softmax(g_logits, axis=-1)
    g_sel = jnp.argmax(g_logits, axis=-1).astype(jnp.int32)
    p_g = jnp.take_along_axis(g_prob, g_sel[:, None], axis=-1)
    e_all = ((xt @ w_re).astype(jnp.float32) + b_re.astype(jnp.float32)).reshape(
        t, N_GROUPS, EXPERTS_PER_GROUP)
    e_logits = jnp.take_along_axis(e_all, g_sel[:, None, None], axis=1)[:, 0]
    top_p, top_j = lax.top_k(jax.nn.softmax(e_logits, axis=-1), TOP_K)
    gate = p_g * top_p / jnp.sum(top_p, axis=-1, keepdims=True)
    eid = (g_sel[:, None] * EXPERTS_PER_GROUP + top_j).astype(jnp.int32)
    out = expert_dispatch(xt, eid, gate, w_gate, w_up, w_down)
    return out.reshape(b, s, d)

def setup_inputs(seed: int = 0) -> dict:
    key = jax.random.key(seed)
    ks = jax.random.split(key, 24)
    nrm = lambda k, shape, fan_in: jax.random.normal(k, shape, jnp.float32) * (fan_in ** -0.5)
    gain = lambda k, shape: 1.0 + 0.02 * jax.random.normal(k, shape, jnp.float32)
    return {
        'x': jax.random.normal(ks[0], (BATCH, SEQ, D_MODEL), jnp.float32),
        'ln_mix_e': gain(ks[1], (N_EVEN, D_MODEL)),
        'w_in_e': nrm(ks[2], (N_EVEN, D_MODEL, EVEN_IN), D_MODEL),
        'ln_q_e': gain(ks[3], (N_EVEN, MLA_Q_LORA)),
        'w_uq_e': nrm(ks[4], (N_EVEN, MLA_Q_LORA, MLA_HEADS * (MLA_NOPE + MLA_ROPE)), MLA_Q_LORA),
        'ln_kv_e': gain(ks[5], (N_EVEN, MLA_KV_LORA)),
        'w_ukv_e': nrm(ks[6], (N_EVEN, MLA_KV_LORA, MLA_HEADS * (MLA_NOPE + MLA_V)), MLA_KV_LORA),
        'b_f_e': 3.0 + 0.5 * jax.random.normal(ks[7], (N_EVEN, FOX_HEADS), jnp.float32),
        'w_out_e': nrm(ks[8], (N_EVEN, EVEN_MIX, D_MODEL), EVEN_MIX),
        'ln_mix_o': gain(ks[9], (N_ODD, D_MODEL)),
        'w_in_o': nrm(ks[10], (N_ODD, D_MODEL, ODD_IN), D_MODEL),
        'w_out_o': nrm(ks[11], (N_ODD, ODD_MIX, D_MODEL), ODD_MIX),
        'ln_ffn': gain(ks[12], (DEPTH, D_MODEL)),
        'w_rg': nrm(ks[13], (DEPTH, D_MODEL, N_GROUPS), D_MODEL),
        'b_rg': 0.01 * jax.random.normal(ks[14], (DEPTH, N_GROUPS), jnp.float32),
        'w_re': nrm(ks[15], (DEPTH, D_MODEL, N_EXPERTS), D_MODEL),
        'b_re': 0.01 * jax.random.normal(ks[16], (DEPTH, N_EXPERTS), jnp.float32),
        'w_gate': nrm(ks[17], (DEPTH, N_EXPERTS, D_MODEL, D_EXPERT), D_MODEL),
        'w_up': nrm(ks[18], (DEPTH, N_EXPERTS, D_MODEL, D_EXPERT), D_MODEL),
        'w_down': nrm(ks[19], (DEPTH, N_EXPERTS, D_EXPERT, D_MODEL), D_EXPERT),
        'ln_f': gain(ks[20], (D_MODEL,)),
    }

def reference(x, ln_mix_e, w_in_e, ln_q_e, w_uq_e, ln_kv_e, w_ukv_e, b_f_e, w_out_e,
              ln_mix_o, w_in_o, w_out_o, ln_ffn, w_rg, b_rg, w_re, b_re,
              w_gate, w_up, w_down, ln_f):
    for layer in range(DEPTH):
        i = layer // 2
        if layer % 2 == 0:
            x = x + even_mixer(rmsnorm(x, ln_mix_e[i]), w_in_e[i], ln_q_e[i], w_uq_e[i],
                               ln_kv_e[i], w_ukv_e[i], b_f_e[i], w_out_e[i])
        else:
            x = x + odd_mixer(rmsnorm(x, ln_mix_o[i]), w_in_o[i], w_out_o[i])
        x = x + hier_moe(rmsnorm(x, ln_ffn[layer]), w_rg[layer], b_rg[layer], w_re[layer],
                         b_re[layer], w_gate[layer], w_up[layer], w_down[layer])
    return rmsnorm(x, ln_f)


_drawn_inputs = setup_inputs


def setup_inputs(seed=0):
    import zlib

    import numpy as np

    out = dict(_drawn_inputs(seed))
    spreads = {}
    factors = {'ln_q_e': 3.503, 'ln_f': 8.715, 'b_rg': 3.245, 'b_re': 3.544}
    for name, (base, spread) in spreads.items():
        noise = np.random.default_rng([zlib.crc32(name.encode()), seed]).standard_normal(out[name].shape)
        drawn = base * np.exp(spread * noise) if base else spread * noise
        out[name] = __import__('jax').numpy.asarray(drawn.astype(out[name].dtype))
    for name, factor in factors.items():
        out[name] = (out[name] * factor).astype(out[name].dtype)
    return out
```

```python
import concourse.bass as bass
from concourse import mybir
from contextlib import ExitStack
import numpy as np

F32 = mybir.dt.float32
I32 = mybir.dt.int32
ACT = mybir.ActivationFunctionType
ALU = mybir.AluOpType
AX = mybir.AxisListType

P = 128
SEQ = 256
TC = SEQ // P
D = 1024
DC = D // P
EPS = 1e-6
Q_LORA, KV_LORA, ROPE, NOPE, VD = 256, 128, 32, 64, 64
HEADS = 8
QK = NOPE + ROPE
FOX = 64
FQ = Q_LORA + KV_LORA + ROPE
FW = HEADS * FOX
ZC = FQ + HEADS
RH, RQK, RV = 4, 256, 512
GROUPS, PER, EXPERTS, DE = 4, 8, 32, 512
NR = GROUPS + EXPERTS
SLOTS = 32
ROUNDS = SEQ // SLOTS
RING = 8
UNIT = 4096
EVEN_UNITS, ODD_UNITS = 7, 16
BODY_UNITS = 3 * PER
DEEP = 4
BIG = 1e30
SEG = ((0, 0, 128), (1, 128, 256))

CONSTS = {}
_at = 0
for _n, _w in (("ident", 128), ("tri", 128), ("mla", 384), ("fox", 384), ("cos", 32), ("sin", 32),
               ("iota", 32), ("arg4", 4), ("arg8", 8), ("more", ROUNDS - 1)):
    CONSTS[_n] = (_at, _at + _w)
    _at += _w
NCONST = _at
NODD = 512 + RH * 384


class Steps:

    def __init__(self, names):
        self.names, self.next = list(names), 0

    def done(self, name):
        assert self.names[self.next] == name, (name, self.names[self.next])
        self.next += 1
        return 1

    def at(self, name):
        return self.names.index(name) + 1


def tables():
    c = np.zeros((P, NCONST), np.float32)

    def put(name, a):
        lo, hi = CONSTS[name]
        c[:, lo:hi] = a

    p = np.arange(P)
    put("ident", np.eye(P))
    put("tri", p[:, None] <= p[None, :])
    q0, k0 = p[:, None], p[None, :]
    q1, k1 = P + p[:, None], np.arange(SEQ)[None, :]
    put("mla", np.where(np.concatenate([k0 // 64 <= q0 // 64, k1 // 64 <= q1 // 64], 1), 0.0, -BIG))
    put("fox", np.where(np.concatenate([k0 <= q0, k1 <= q1], 1), 0.0, -BIG))
    pos = np.arange(SEQ, dtype=np.float32)

    def phase(half):
        inv = np.float32(10000.0) ** (-np.arange(half, dtype=np.float32) / np.float32(half))
        return pos[:, None] * inv[None, :]

    a16 = phase(ROPE // 2).reshape(TC, P, 16).transpose(1, 0, 2).reshape(P, 32)
    put("cos", np.cos(a16))
    put("sin", np.sin(a16))
    put("iota", np.arange(SLOTS)[None, :])
    put("arg4", np.arange(GROUPS)[None, :] - GROUPS)
    put("arg8", np.arange(PER)[None, :] - PER)
    put("more", SLOTS * np.arange(1, ROUNDS)[None, :])
    o = np.zeros((P, NODD), np.float32)
    aT = phase(RQK // 2).T
    o[:, 0:256], o[:, 256:512] = np.cos(aT), np.sin(aT)
    for h in range(RH):
        g = np.log(1.0 - 2.0 ** (-5.0 - h))
        t, s = np.arange(SEQ)[None, :], np.arange(SEQ)[:, None]
        dec = np.where(t >= s, np.exp(np.maximum(t - s, 0) * g), 0.0) * RQK ** -0.5
        o[:, 512 + 384 * h:512 + 384 * h + 256] = dec[0:128]
        o[:, 512 + 384 * h + 256:512 + 384 * (h + 1)] = dec[128:256, 128:256]
    return c, o


def build(nc, x_in, ln_mix_e, w_in_e, ln_q_e, w_uq_e, ln_kv_e, w_ukv_e, b_f_e, w_out_e,
          ln_mix_o, w_in_o, w_out_o, ln_ffn, w_rg, b_rg, w_re, b_re, w_gate, w_up, w_down,
          ln_f, consts, consts_odd, out):
    ctx = ExitStack()
    with ctx:
        def sb(name, shape, dt=F32):
            return ctx.enter_context(nc.sbuf_tensor(name, shape, dt))

        def sem(name):
            return ctx.enter_context(nc.semaphore(name))

        ring = sb("ring", [P, RING, UNIT])
        x = sb("x", [P, TC, D])
        xn = sb("xn", [P, TC, DC, P])
        xnT = sb("xnT", [P, DC, SEQ])
        gain = sb("gain", [P, 2, D])
        const = sb("const", [P, NCONST])
        arena = sb("arena", [P, 9984])
        small = sb("small", [P, 1088])
        rounds = sb("rounds", [1, 2], I32)

        def C(name, rows=P):
            return const[0:rows, CONSTS[name][0]:CONSTS[name][1]]

        class Cut:
            def __init__(self, base):
                self.base, self.used = base, 0

            def __call__(self, n, pattern=None, **dims):
                a = self.base[:, self.used:self.used + n]
                self.used += n
                assert self.used <= self.base.shape[1], self.used
                return a.rearrange(pattern, **dims) if pattern else a

        cut = Cut(small)
        wr = cut(2 * DC * NR, "p (l c n) -> p l c n", l=2, c=DC)
        br = cut(2 * NR, "p (l n) -> p l n", l=2)
        ones = cut(P)
        bf = cut(HEADS)
        ss = cut(2)
        ms = cut(2)
        std = cut(2)
        rstd = cut(2)
        s4 = cut(4)
        r4 = cut(4)
        zlog = cut(16, "p (c h) -> p c h", c=TC)
        zabs = cut(16, "p (c h) -> p c h", c=TC)
        zexp = cut(16, "p (c h) -> p c h", c=TC)
        logf = cut(16, "p (c h) -> p c h", c=TC)
        cum = cut(16, "p (c h) -> p c h", c=TC)
        mx = cut(2 * DEEP, "p (b c) -> p b c", b=DEEP)
        nmx = cut(2 * DEEP, "p (b c) -> p b c", b=DEEP)
        sm = cut(2 * DEEP, "p (b c) -> p b c", b=DEEP)
        rsm = cut(2 * DEEP, "p (b c) -> p b c", b=DEEP)
        lg = cut(2 * NR, "p (c n) -> p c n", c=TC)
        oh4 = cut(8, "p (c n) -> p c n", c=TC)
        t4 = cut(8, "p (c n) -> p c n", c=TC)
        oh8 = cut(32, "p (k c n) -> p k c n", k=2, c=TC)
        t8 = cut(16, "p (c n) -> p c n", c=TC)
        el, el2 = zabs, zexp
        rt = cut(36)

        cut = Cut(arena)
        spare = Cut(ring[:, 4, 2 * HEADS * QK + 1024:])
        zc = spare(TC * ZC, "p (c n) -> p c n", c=TC)
        lnqkv = spare(Q_LORA + KV_LORA)
        ropek = spare(256)
        vm = cut(TC * 512, "p (c n) -> p c n", c=TC)
        vf = cut(TC * 512, "p (c n) -> p c n", c=TC)
        q96T = cut(HEADS * SEQ, "p (h t) -> p h t", h=HEADS)
        k96T = cut(HEADS * SEQ, "p (h t) -> p h t", h=HEADS)
        qfT = cut(4 * SEQ, "p (h t) -> p h t", h=4)
        kfT = cut(4 * SEQ, "p (h t) -> p h t", h=4)
        ncT = cut(SEQ)
        shared = cut(768)
        cqT = shared[:, 0:512].rearrange("p (k t) -> p k t", k=2)
        ckvT = shared[:, 512:768]
        probT = cut(2 * 384, "p (b n) -> p b n", b=2)
        q_tok = xn[:, :, :, :].rearrange("p c a b -> p c (a b)")[:, :, 0:HEADS * QK]
        prob = xn[:, :, :, :].rearrange("p c a b -> p (c a b)")[:, 0:DEEP * 384].rearrange(
            "p (b n) -> p b n", b=DEEP)
        oT = xnT

        cut = Cut(arena)
        odd = cut(NODD)
        qT = cut(512, "p (m t) -> p m t", m=2)
        kT = cut(512, "p (m t) -> p m t", m=2)
        ra = cut(512, "p (m t) -> p m t", m=2)
        rb = cut(512, "p (m t) -> p m t", m=2)
        vr = cut(TC * RV, "p (c n) -> p c n", c=TC)
        sg = cut(TC * RV, "p (c n) -> p c n", c=TC)
        yr = cut(TC * RV, "p (c n) -> p c n", c=TC)
        yT = cut(TC * RV, "p (c k t) -> p c k t", c=TC, k=4)
        sT = cut(384)
        junk = cut(TC * RV, "p (c n) -> p c n", c=TC)

        cut = Cut(arena)
        asg = cut(TC * EXPERTS, "p (c g j) -> p c g j", c=TC, g=GROUPS)
        gates = cut(TC * EXPERTS, "p (c e) -> p c e", c=TC)
        place = cut(TC * EXPERTS, "p (c e) -> p c e", c=TC)
        tmp = cut(TC * EXPERTS, "p (c g j) -> p c g j", c=TC, g=GROUPS)
        sel = cut(TC * PER * SLOTS, "p (c e s) -> p c e s", c=TC, e=PER)
        gsel = cut(TC * PER * SLOTS, "p (c e s) -> p c e s", c=TC, e=PER)
        xg = cut(2 * DC * 4 * SLOTS, "p (b c s) -> p b c s", b=2, c=DC)
        act_g = cut(P)
        hid = cut(P)
        hidT = cut(P, "p (k s) -> p k s", k=4)
        ye = cut(256)
        gT = cut(SEQ)
        squares = cut(2 * D, "p (c n) -> p c n", c=TC)

        acc = [ctx.enter_context(nc.psum_tensor(f"acc{i}", [P, 512], F32)) for i in range(4)]
        wk = [ctx.enter_context(nc.psum_tensor(f"wk{i}", [P, 512], F32)) for i in range(4)]

        x_in_sem = sem("x_loaded")
        const_in = sem("consts_loaded")
        gain_in = [sem(f"gain_loaded{b}") for b in range(2)]
        odd_in = sem("odd_consts_loaded")
        small_in = sem("router_and_small_loaded")
        ready = sem("ones_and_router_ready")
        even_here = [sem(f"even_unit{s}_loaded") for s in range(EVEN_UNITS)]
        moe_here = [[sem(f"moe{l}_slot{s}_loaded") for s in range(RING)] for l in range(2)]
        odd_here = [sem(f"odd_slot{s}_loaded") for s in range(RING)]
        even_used = sem("even_units_used")
        moe_used = [sem(f"moe{l}_units_used") for l in range(2)]
        odd_used = sem("odd_units_used")
        pe_s = sem("pe_steps")
        act_s = sem("act_steps")
        dve_s = sem("dve_steps")
        pool_s = sem("pool_steps")
        chain_v = sem("dve_chain")
        chain_a = sem("act_chain")
        rounds_set = [sem(f"rounds{l}_set") for l in range(2)]
        stored = sem("out_stored")

        def moe_sems(l):
            names = ("sel_ready", "sel_spent", "gath_ready", "xg_copied", "gu_ready", "silu_done", "hid_done",
                     "hidT_ready", "hidT_copied", "y_ready", "y_copied", "g_ready", "g_copied", "combined",
                     "moe_done", "place_moved", "gsel_masked")
            return {n: sem(f"m{l}_{n}") for n in names}

        M = [moe_sems(0), moe_sems(1)]
        odd_filled = [sem(f"odd_bank{b}_filled") for b in range(4)]
        odd_drained = [sem(f"odd_bank{b}_drained") for b in range(4)]
        O = {n: sem(f"o_{n}") for n in ("qT_done", "kT_done", "v_done", "sT_done", "sg_done", "y_done", "yT_done",
                                        "scores_done", "o_read", "yT_read", "y_read", "sq_done", "std_done",
                                        "ms_done", "rs_done", "ra_done", "rb_done", "o_all")}

        def norm_steps(e):
            return {"act": [f"{e}:sq", f"{e}:std", f"{e}:xT0", f"{e}:xT2"],
                    "dve": [f"{e}:ms", f"{e}:xn0", f"{e}:xn1", f"{e}:xT1", f"{e}:xT3"],
                    "pe": [f"{e}:xT{i}" for i in range(4)]}

        N = {e: norm_steps(e) for e in ("mix0", "ffn0", "mix1", "ffn1")}
        att_pe = ["S0", "S1", "S2"]
        for a in range(16):
            att_pe += [f"T{a}"] + ([f"S{a + 3}"] if a < 13 else []) + ([f"O{a - 1}"] if a else [])
        att_pe += ["O15"]
        router_pe = lambda l: [f"lg{l}", f"rk{l}"]
        PE = Steps(N["mix0"]["pe"] + ["Z0", "Z1", "QF0", "QF1", "KF0", "KF1", "VF0", "VF1", "CU", "CT", "CQ", "CK",
                                      "QA0", "QB0", "QA1", "QB1", "KN0", "KN1", "KN2", "KN3", "VM0", "VM1",
                                      "QT0", "QT1", "QT2", "QT3"] + att_pe + ["OUT0"]
                   + N["ffn0"]["pe"] + router_pe(0) + N["mix1"]["pe"] + ["OUT1"] + N["ffn1"]["pe"] + router_pe(1))
        att_act = []
        for a in range(16):
            att_act += [f"e{a}"] + ([f"p{a - 2}"] if a > 1 else [])
        att_act += ["p14", "p15"]
        router_act = lambda l: [f"ge{l}", f"ee{l}"]
        A = Steps(N["mix0"]["act"] + ["Z0", "Z1", "sq4", "QF0", "zabs", "zexp", "zln", "std4", "QF1", "VF0", "CT", "CQ", "kpe",
                                      "QA0", "QB0", "QA1", "QB1", "KN0", "KN2", "VM0", "QT0", "QT2"]
                  + att_act + ["x0a", "x0b"] + N["ffn0"]["act"] + router_act(0) + ["y0a", "y0b"] + N["mix1"]["act"]
                  + ["x1a", "x1b"] + N["ffn1"]["act"] + router_act(1) + ["y1a", "y1b", "fin:sq", "fin:std"])
        att_dve = []
        for a in range(16):
            att_dve += [f"s{a}", f"m{a}"] + ([f"r{a - 1}"] if a else []) + ([f"o{a // 2 - 2}"] if a % 2 == 0 and a > 2 else [])
        att_dve += ["r15", "o6", "o7"]
        V = Steps(N["mix0"]["dve"] + ["zlog", "ms4", "KF0", "KF1", "logf", "VF1", "cqn", "kpe", "CU", "CK",
                                      "rope0", "rope1", "KN1", "KN3", "VM1", "QT1", "QT3"] + att_dve
                  + ["x0a", "x0b"] + N["ffn0"]["dve"] + ["gd0", "ed0", "asg0"] + ["y0a", "y0b"]
                  + N["mix1"]["dve"] + ["x1a", "x1b"] + N["ffn1"]["dve"] + ["gd1", "ed1", "asg1"]
                  + ["y1a", "y1b", "fin:ms", "fin0", "fin1"])
        G = Steps([f"n{a}" for a in range(16)])

        def wide(s):
            return ring[:, s, :].rearrange("p (c n) -> p c n", c=DC)

        def tall(s):
            return ring[:, s, :].rearrange("p (c n) -> p c n", c=4)

        z_w = ring[:, 0, 0:DC * ZC].rearrange("p (c n) -> p c n", c=DC)
        uq_w = ring[:, 4, 0:2 * HEADS * QK].rearrange("p (c n) -> p c n", c=2)
        ukv_w = ring[:, 4, 2 * HEADS * QK:2 * HEADS * QK + 1024]

        def moe_slot(idx):
            return (EVEN_UNITS + idx) % RING

        ODD_ORDER = (("qk", 0), ("v", 0), ("g", 0), ("qk", 1), ("wo", 0), ("v", 1), ("g", 1), ("wo", 1))
        odd_slot = {u: moe_slot(i) for i, u in enumerate(ODD_ORDER)}
        ODD_USES = [(n, h) for h, n in ((0, "q"), (0, "k"), (0, "v0"), (0, "v1"), (0, "S0"), (0, "S1"), (0, "g0"), (0, "g1"),
                                        (0, "O0"), (0, "O1"), (1, "q"), (1, "k"), (0, "T0"), (0, "T1"), (1, "v0"), (1, "v1"),
                                        (1, "S0"), (1, "S1"), (1, "g0"), (1, "g1"), (1, "O0"), (1, "O1"), (1, "T0"), (1, "T1"))]

        def odd_use(name, hp):
            u = ODD_USES.index((name, hp))
            return u % 4, u // 4

        block = ctx.enter_context(nc.Block())

        @block.sync
        def _(sp):
            x_v = x_in.rearrange("b (c p) d -> p (b c) d", p=P)
            sp.dma_start(x[:, :, :], x_v).then_inc(x_in_sem, 16)
            w = w_in_e[0].rearrange("(p c) n -> p c n", c=DC)
            sp.dma_start(z_w[:, :, 0:FQ], w[:, :, 0:FQ]).then_inc(even_here[0], 16)
            sp.dma_start(z_w[:, :, FQ:ZC], w[:, :, FQ + 3 * FW:]).then_inc(even_here[0], 16)
            for u in range(3):
                sp.dma_start(wide(1 + u), w[:, :, FQ + u * FW:FQ + (u + 1) * FW]).then_inc(even_here[1 + u], 16)
            sp.dma_start(uq_w, w_uq_e[0].rearrange("(c p) n -> p c n", p=P)).then_inc(even_here[4], 16)
            sp.dma_start(ukv_w, w_ukv_e[0]).then_inc(even_here[4], 16)
            wo = w_out_e[0].rearrange("(u c p) n -> u p c n", u=2, c=4)
            for u in range(2):
                sp.dma_start(tall(5 + u), wo[u]).then_inc(even_here[5 + u], 16)

            gate_v = w_gate.rearrange("l e (p c) n -> (l e) p (c n)", c=DC)
            up_v = w_up.rearrange("l e (p c) n -> (l e) p (c n)", c=DC)
            down_v = w_down.rearrange("l e (c p) n -> (l e) p c n", c=4)

            def load_expert_part(l, group, idx):
                e = group * PER + (l * EXPERTS + idx // 3)
                s = moe_slot(idx)
                if idx % 3 == 2:
                    sp.dma_start(tall(s), down_v[bass.ds(e, 1)].rearrange("e p c n -> p (e c) n")
                                 ).then_inc(moe_here[l][s], 16)
                else:
                    v = (gate_v, up_v)[idx % 3]
                    sp.dma_start(ring[:, s, :], v[bass.ds(e, 1)].rearrange("e p n -> p (e n)")
                                 ).then_inc(moe_here[l][s], 16)

            def first_units(l, free):
                for idx in range(RING):
                    free(idx)
                    load_expert_part(l, 0, idx)

            def rest_of_experts(l):
                sp.sem_inc(moe_used[l], RING)
                with sp.Fori(0, GROUPS - 1) as i:
                    for idx in range(RING, BODY_UNITS):
                        sp.wait_ge(moe_used[l], i * BODY_UNITS + (idx + 1))
                        load_expert_part(l, i, idx)
                    for idx in range(RING):
                        sp.wait_ge(moe_used[l], i * BODY_UNITS + (BODY_UNITS + idx + 1))
                        load_expert_part(l, i + 1, idx)
                for idx in range(RING, BODY_UNITS):
                    sp.wait_ge(moe_used[l], (GROUPS - 1) * BODY_UNITS + idx + 1)
                    load_expert_part(l, GROUPS - 1, idx)
                sp.wait_ge(rounds_set[l], 1)
                n = sp.value_load(rounds[0:1, l:l + 1], min_val=1, max_val=ROUNDS)
                with sp.If(n > 1):
                    with sp.Fori(1, n) as r:
                        with sp.Fori(0, GROUPS) as i:
                            for idx in range(BODY_UNITS):
                                sp.wait_ge(moe_used[l], r * (GROUPS * BODY_UNITS) + i * BODY_UNITS + (idx + 1))
                                load_expert_part(l, i, idx)
                return n

            def after_even(idx):
                if idx:
                    sp.wait_ge(even_used, idx)

            first_units(0, after_even)
            n0 = rest_of_experts(0)

            wi = w_in_o[0].rearrange("(p c) n -> p c n", c=DC)
            wo2 = w_out_o[0].rearrange("(h c p) n -> h p c n", h=RH, c=4)

            def load_odd(i, j):
                kind, hp = ODD_ORDER[j]
                s = odd_slot[(kind, hp)]
                h = i * 2 + hp
                if kind == "qk":
                    for m in range(2):
                        sp.dma_start(wide(s)[:, :, m * RQK:(m + 1) * RQK],
                                     wi[:, :, bass.ds(h * RQK + m * RH * RQK, RQK)]).then_inc(odd_here[s], 16)
                elif kind == "wo":
                    sp.dma_start(tall(s), wo2[bass.ds(h, 1)].rearrange("e p c n -> p (e c) n")).then_inc(odd_here[s], 16)
                else:
                    first = 2 * RH * RQK + (RH * RV if kind == "g" else 0)
                    sp.dma_start(wide(s), wi[:, :, bass.ds(h * RV + first, RV)]).then_inc(odd_here[s], 16)

            for j in range(RING):
                sp.wait_ge(moe_used[0], n0 * (GROUPS * BODY_UNITS) + (j + 1))
                load_odd(0, j)
            for j in range(RING):
                sp.wait_ge(odd_used, j + 1)
                load_odd(1, j)

            def after_odd(idx):
                sp.wait_ge(odd_used, ODD_UNITS - RING + idx + 1)

            first_units(1, after_odd)
            rest_of_experts(1)

            out_v = out.rearrange("b (c p) d -> p (b c) d", p=P)
            for c in range(TC):
                sp.wait_ge(dve_s, V.at(f"fin{c}"))
                sp.dma_start(out_v[:, c, :], x[:, c, :]).then_inc(stored, 16)
            sp.wait_ge(stored, 32)

        @block.gpsimd
        def _(pool):
            def bcast(ap, n):
                return ap.broadcast_to([P, n])

            pool.dma_start(const[:, :], consts).then_inc(const_in, 16)
            pool.dma_start(gain[:, 0, :], bcast(ln_mix_e[0:1, :], D)).then_inc(gain_in[0], 16)
            pool.dma_start(lnqkv[:, 0:Q_LORA], bcast(ln_q_e[0:1, :], Q_LORA)).then_inc(small_in, 16)
            pool.dma_start(lnqkv[:, Q_LORA:], bcast(ln_kv_e[0:1, :], KV_LORA)).then_inc(small_in, 16)
            pool.dma_start(bf, bcast(b_f_e[0:1, :], HEADS)).then_inc(small_in, 16)
            pool.dma_start(gain[:, 1, :], bcast(ln_ffn[0:1, :], D)).then_inc(gain_in[1], 16)
            stage_g = squares[:, 0, 0:2 * DC * GROUPS].rearrange("p (l n) -> p l n", l=2)
            stage_e = squares[:, 1, 0:2 * DC * EXPERTS].rearrange("p (l n) -> p l n", l=2)
            pool.dma_start(br[:, 0, 0:GROUPS], bcast(b_rg[0:1, :], GROUPS)).then_inc(small_in, 16)
            pool.dma_start(br[:, 1, 0:GROUPS], bcast(b_rg[1:2, :], GROUPS)).then_inc(small_in, 16)
            pool.dma_start(br[:, 0, GROUPS:], bcast(b_re[0:1, :], EXPERTS)).then_inc(small_in, 16)
            pool.dma_start(br[:, 1, GROUPS:], bcast(b_re[1:2, :], EXPERTS)).then_inc(small_in, 16)
            nc.gpsimd.memset(ones, 1.0).then_inc(ready, 1)
            for a in range(16):
                pool.wait_ge(act_s, A.at(f"e{a}"))
                pool.wait_ge(dve_s, V.at(f"r{a}"))
                for c, lo, n in SEG:
                    last = nc.gpsimd.tensor_scalar(prob[:, a % DEEP, lo:lo + n], prob[:, a % DEEP, lo:lo + n],
                                                   rsm[:, a % DEEP, c:c + 1], None, ALU.mult)
                last.then_inc(pool_s, G.done(f"n{a}"))
            pool.wait_ge(dve_s, V.at("x0b"))
            pool.wait_ge(act_s, A.at("x0b"))
            for l in range(2):
                pool.dma_start(stage_g[:, l, :], w_rg[l].rearrange("(p c) n -> p (c n)", c=DC)).then_inc(small_in, 16)
                pool.dma_start(stage_e[:, l, :], w_re[l].rearrange("(p c) n -> p (c n)", c=DC)).then_inc(small_in, 16)
            pool.dma_start(gain[:, 0, :], bcast(ln_mix_o[0:1, :], D)).then_inc(gain_in[0], 16)
            pool.wait_ge(small_in, 16 * 11)
            for l in range(2):
                nc.gpsimd.tensor_copy(wr[:, l, :, 0:GROUPS], stage_g[:, l, :].rearrange("p (c n) -> p c n", c=DC)
                                      ).then_inc(ready, 1)
                nc.gpsimd.tensor_copy(wr[:, l, :, GROUPS:], stage_e[:, l, :].rearrange("p (c n) -> p c n", c=DC)
                                      ).then_inc(ready, 1)
            pool.wait_ge(dve_s, V.at("ffn0:xn1"))
            pool.dma_start(gain[:, 1, :], bcast(ln_ffn[1:2, :], D)).then_inc(gain_in[1], 16)
            pool.wait_ge(dve_s, V.at("y0b"))
            pool.wait_ge(act_s, A.at("y0b"))
            pool.dma_start(odd, consts_odd).then_inc(odd_in, 16)
            pool.wait_ge(dve_s, V.at("mix1:xn1"))
            pool.dma_start(gain[:, 0, :], bcast(ln_f[None, :], D)).then_inc(gain_in[0], 16)

        @block.tensor
        def _(pe):
            ident = C("ident")

            def transposed_norm(e):
                pe.wait_ge(dve_s, V.at(f"{e}:xn1"))
                for b in range(4):
                    for i in range(2):
                        for c in range(TC):
                            last = nc.tensor.transpose(wk[b][:, i * SEQ + c * P:i * SEQ + (c + 1) * P],
                                                       xn[:, c, 2 * b + i, :], ident)
                    last.then_inc(pe_s, PE.done(f"{e}:xT{b}"))

            def project(dst, lhs, rhs, n=DC, first=True, last_one=True):
                for k in range(n):
                    last = nc.tensor.matmul(dst, lhs(k), rhs(k), start=(k == 0 and first), stop=(k == n - 1 and last_one))
                return last

            def tok(c):
                return slice(c * P, (c + 1) * P)

            def normed(e):
                pe.wait_ge(act_s, A.at(f"{e}:xT2"))
                pe.wait_ge(dve_s, V.at(f"{e}:xT3"))

            pe.wait_ge(const_in, 16)
            transposed_norm("mix0")
            normed("mix0")
            pe.wait_ge(even_here[0], 32)
            for c in range(TC):
                project(wk[c][:, 0:ZC], lambda k: xnT[:, k, tok(c)], lambda k: z_w[:, k, :]
                        ).then_inc(pe_s, PE.done(f"Z{c}"))
            pe.wait_ge(pe_s, PE.at("Z1"))
            pe.sem_inc(even_used, 1)
            for u, name in ((1, "QF"), (2, "KF")):
                pe.wait_ge(even_here[u], 16)
                for b in range(2):
                    bank = wk[(2 if name == "QF" else 0) + b]
                    if name == "KF":
                        pe.wait_ge(act_s, A.at(f"Z{b}"))
                    for i in range(2):
                        m = 2 * b + i
                        last = project(bank[:, i * SEQ:(i + 1) * SEQ], lambda k: wide(u)[:, k, m * P:(m + 1) * P],
                                       lambda k: xnT[:, k, :])
                    last.then_inc(pe_s, PE.done(f"{name}{b}"))
                pe.wait_ge(pe_s, PE.at(f"{name}1"))
                pe.sem_inc(even_used, 1)
            pe.wait_ge(even_here[3], 16)
            for c in range(TC):
                pe.wait_ge(act_s, A.at(f"QF{c}"))
                project(wk[2 + c][:, :], lambda k: xnT[:, k, tok(c)], lambda k: wide(3)[:, k, :]
                        ).then_inc(pe_s, PE.done(f"VF{c}"))
            pe.wait_ge(pe_s, PE.at("VF1"))
            pe.sem_inc(even_used, 1)
            pe.wait_ge(dve_s, V.at("logf"))
            pe.wait_ge(dve_s, V.at("KF0"))
            pe.wait_ge(ready, 1)
            nc.tensor.matmul(wk[0][:, 0:8], C("tri"), logf[:, 0, :], start=True, stop=True)
            nc.tensor.matmul(wk[0][:, 8:16], C("tri"), logf[:, 1, :], start=True, stop=False)
            nc.tensor.matmul(wk[0][:, 8:16], ones, logf[:, 0, :], start=False, stop=True).then_inc(pe_s, PE.done("CU"))
            pe.wait_ge(dve_s, V.at("CU"))
            for c in range(TC):
                last = nc.tensor.matmul(wk[1][0:8, tok(c)], cum[:, c, :], ident, start=True, stop=True)
            last.then_inc(pe_s, PE.done("CT"))
            for k in range(2):
                for c in range(TC):
                    last = nc.tensor.transpose(wk[0][:, k * SEQ + c * P:k * SEQ + (c + 1) * P],
                                               zc[:, c, k * P:(k + 1) * P], ident)
            last.then_inc(pe_s, PE.done("CQ"))
            pe.wait_ge(act_s, A.at("VF0"))
            for c in range(TC):
                nc.tensor.transpose(wk[2][:, tok(c)], zc[:, c, Q_LORA:Q_LORA + KV_LORA], ident)
            for c in range(TC):
                last = nc.tensor.matmul(wk[2][64:96, SEQ + c * P:SEQ + (c + 1) * P], zc[:, c, FQ - ROPE:FQ], ident,
                                        start=True, stop=True)
            last.then_inc(pe_s, PE.done("CK"))
            pe.wait_ge(even_here[4], 32)
            pe.wait_ge(act_s, A.at("CQ"))
            pe.wait_ge(dve_s, V.at("VF1"))
            banks = {"QA0": 3, "QB0": 0, "QA1": 1, "QB1": 3}
            for c in range(TC):
                for i, name in enumerate(("QA", "QB")):
                    if (c, i) == (1, 1):
                        pe.wait_ge(act_s, A.at("QA0"))
                    b = wk[banks[f"{name}{c}"]]
                    project(b[:, 0:384], lambda k: cqT[:, k, tok(c)], lambda k: uq_w[:, k, i * 384:(i + 1) * 384], n=2
                            ).then_inc(pe_s, PE.done(f"{name}{c}"))
            pe.wait_ge(dve_s, V.at("CK"))
            pe.wait_ge(act_s, A.at("kpe"))
            kn_bank = (2, 0, 1, 3)
            kn_free = (None, "QB0", "QA1", "QB1")
            for m in range(4):
                if kn_free[m]:
                    pe.wait_ge(act_s, A.at(kn_free[m]))
                for i in range(2):
                    h = 2 * m + i
                    last = nc.tensor.matmul(wk[kn_bank[m]][0:64, i * SEQ:(i + 1) * SEQ],
                                            ukv_w[:, h * 128:h * 128 + NOPE], ckvT, start=True, stop=True)
                last.then_inc(pe_s, PE.done(f"KN{m}"))
            uv = ukv_w.rearrange("p (h d) -> p h d", h=HEADS)[:, :, NOPE:]
            for c in range(TC):
                pe.wait_ge(act_s, A.at("KN0")) if c == 0 else pe.wait_ge(dve_s, V.at("KN1"))
                nc.tensor.matmul(wk[2 if c == 0 else 0][:, :], ckvT[:, tok(c)], uv, start=True, stop=True
                                 ).then_inc(pe_s, PE.done(f"VM{c}"))
            pe.wait_ge(pe_s, PE.at("VM1"))
            pe.wait_ge(dve_s, V.at("rope1"))
            pe.sem_inc(even_used, 1)
            qt_bank = (1, 3, 2, 0)
            for m in range(4):
                if m == 0:
                    pe.wait_ge(act_s, A.at("KN2"))
                elif m == 1:
                    pe.wait_ge(dve_s, V.at("KN3"))
                elif m == 2:
                    pe.wait_ge(act_s, A.at("VM0"))
                else:
                    pe.wait_ge(dve_s, V.at("VM1"))
                for i in range(2):
                    h = 2 * m + i
                    for c in range(TC):
                        last = nc.tensor.transpose(wk[qt_bank[m]][0:QK, i * SEQ + c * P:i * SEQ + (c + 1) * P],
                                                   q_tok[:, c, h * QK:(h + 1) * QK], ident)
                last.then_inc(pe_s, PE.done(f"QT{m}"))

            pe.wait_ge(act_s, A.at("QT2"))
            pe.wait_ge(dve_s, V.at("QT3"))
            pe.wait_ge(act_s, A.at("CT"))
            s_bank, t_bank, o_bank = (wk[0], wk[1], acc[2], acc[3]), (wk[2], acc[0]), (wk[3], acc[1])

            def scores(a):
                b = s_bank[a % DEEP]
                if a >= DEEP:
                    pe.wait_ge(dve_s, V.at(f"s{a - DEEP}"))
                for c, lo, n in SEG:
                    if a < 8:
                        last = nc.tensor.matmul(b[:, lo:lo + n], q96T[0:QK, a, tok(c)], k96T[0:QK, a, 0:n],
                                                start=True, stop=True)
                    else:
                        h = a - 8
                        r = 64 * (h % 2)
                        nc.tensor.matmul(b[:, lo:lo + n], qfT[r:r + 64, h // 2, tok(c)], kfT[r:r + 64, h // 2, 0:n],
                                         start=True, stop=False)
                        last = nc.tensor.matmul(b[:, lo:lo + n], C("ident", 8)[:, h:h + 1].broadcast_to([8, P]),
                                                ncT[0:8, 0:n], start=False, stop=True)
                last.then_inc(pe_s, PE.done(f"S{a}"))

            def weigh(a):
                ob = o_bank[a // 2 % 2]
                pe.wait_ge(act_s, A.at(f"p{a}"))
                if a % 2 == 0 and a >= 4:
                    pe.wait_ge(dve_s, V.at(f"o{a // 2 - 2}"))
                h = a % 8
                v = vm if a < 8 else vf
                r = 64 * (a % 2)
                nc.tensor.matmul(ob[r:r + 64, 0:SEQ], v[:, 0, h * 64:(h + 1) * 64], probT[:, a % 2, 0:256],
                                 start=True, stop=False)
                nc.tensor.matmul(ob[r:r + 64, P:SEQ], v[:, 1, h * 64:(h + 1) * 64], probT[:, a % 2, 256:384],
                                 start=False, stop=True).then_inc(pe_s, PE.done(f"O{a}"))

            for a in range(3):
                scores(a)
            for a in range(16):
                tb = t_bank[a % 2]
                pe.wait_ge(pool_s, G.at(f"n{a}"))
                if a >= 2:
                    pe.wait_ge(act_s, A.at(f"p{a - 2}"))
                for k in range(3):
                    last = nc.tensor.transpose(tb[:, k * P:(k + 1) * P], prob[:, a % DEEP, k * P:(k + 1) * P], ident)
                last.then_inc(pe_s, PE.done(f"T{a}"))
                if a < 13:
                    scores(a + 3)
                if a:
                    weigh(a - 1)
            weigh(15)

            def seed_wide():
                for c in range(TC):
                    for hf in range(2):
                        nc.tensor.matmul(acc[2 * c + hf][:, :], ident, x[:, c, hf * 512:(hf + 1) * 512],
                                         start=True, stop=False, skip_group_check=True)

            pe.wait_ge(act_s, A.at("p15"))
            pe.wait_ge(dve_s, V.at("o7"))
            seed_wide()
            for u in range(2):
                pe.wait_ge(even_here[5 + u], 16)
                for c in range(TC):
                    for hf in range(2):
                        for k in range(4):
                            last = nc.tensor.matmul(acc[2 * c + hf][:, :], oT[:, 4 * u + k, tok(c)],
                                                    tall(5 + u)[:, k, hf * 512:(hf + 1) * 512],
                                                    start=False, stop=(u == 1 and k == 3), skip_group_check=True)
                if u == 0:
                    last.then_inc(even_used, 1)
            last.then_inc(pe_s, PE.done("OUT0"))
            pe.wait_ge(pe_s, PE.at("OUT0"))
            pe.sem_inc(even_used, 1)

            def experts(l):
                m = M[l]
                e_ = f"ffn{l}"
                transposed_norm(e_)
                normed(e_)
                pe.wait_ge(ready, 5)
                for c in range(TC):
                    last = project(wk[0][:, c * 64:c * 64 + NR], lambda k: xnT[:, k, tok(c)], lambda k: wr[:, l, k, :])
                last.then_inc(pe_s, PE.done(f"lg{l}"))
                for c in range(TC):
                    for j in range(4):
                        nc.tensor.matmul(acc[j][:, c * 256:(c + 1) * 256], ident, x[:, c, j * 256:(j + 1) * 256],
                                         start=(c == 0), stop=False, skip_group_check=True)
                pe.wait_ge(dve_s, V.at(f"asg{l}"))
                a_ = [asg[:, c, :, :].rearrange("p g j -> p (g j)") for c in range(TC)]
                nc.tensor.matmul(wk[1][:, 0:32], C("tri"), a_[0], start=True, stop=True)
                nc.tensor.matmul(wk[1][:, 32:64], C("tri"), a_[1], start=True, stop=False)
                nc.tensor.matmul(wk[1][:, 32:64], ones, a_[0], start=False, stop=True)
                nc.tensor.matmul(wk[1][:, 64:96], ones, a_[0], start=True, stop=False)
                nc.tensor.matmul(wk[1][:, 64:96], ones, a_[1], start=False, stop=True).then_inc(pe_s, PE.done(f"rk{l}"))
                for n in ("hidT_ready", "y_ready", "combined", "sel_spent"):
                    pe.sem_inc(m[n], 1)
                pe.wait_ge(rounds_set[l], 1)
                nr = pe.value_load(rounds[0:1, l:l + 1], min_val=1, max_val=ROUNDS)
                with pe.Fori(0, nr) as r:
                    with pe.Fori(0, GROUPS) as i:
                        it = r * GROUPS + i

                        def here(idx):
                            pe.wait_ge(moe_here[l][moe_slot(idx)], it * 48 + 16 * (idx // RING + 1))

                        def combine(e):
                            pe.wait_ge(m["y_copied"], it * PER + (e + 1))
                            pe.wait_ge(m["g_copied"], it * PER + (e + 2))
                            for c in range(TC):
                                for j in range(4):
                                    q = slice(32 * j, 32 * j + 32)
                                    last = nc.tensor.matmul(acc[j][:, c * 256:(c + 1) * 256], gT[q, tok(c)], ye[q, :],
                                                            start=False, stop=False, skip_group_check=True,
                                                            tile_position=(32 * j, 0))
                            last.then_inc(m["combined"], 1)

                        pe.wait_ge(m["sel_ready"], it + 1)
                        for e in range(PER):
                            n_ = it * PER + e
                            quad = e // 4
                            if e % 4 == 0:
                                if e:
                                    combine(e - 1)
                                pe.wait_ge(m["g_copied"], n_ + 1)
                                for half in range(2):
                                    b = wk[2 - half]
                                    for k in range(4):
                                        for c in range(TC):
                                            last = nc.tensor.matmul(
                                                b[:, k * P:(k + 1) * P], xn[:, c, 4 * half + k, :],
                                                sel[:, c, 4 * quad:4 * quad + 4, :].rearrange("p e s -> p (e s)"),
                                                start=(c == 0), stop=(c == TC - 1))
                                    last.then_inc(m["gath_ready"], 1)
                                pe.wait_ge(m["xg_copied"], it * 4 + (2 * quad + 2))
                            xe = xg[:, quad, :, (e % 4) * SLOTS:(e % 4 + 1) * SLOTS]


                            def up_or_gate(part):
                                here(3 * e + part)
                                w_ = wide(moe_slot(3 * e + part))
                                for k in range(DC):
                                    for j in range(4):
                                        last = nc.tensor.matmul(wk[0][32 * j:32 * j + 32, part * P:(part + 1) * P],
                                                                xe[:, k, :], w_[:, k, j * P:(j + 1) * P],
                                                                start=(k == 0), stop=(k == DC - 1))
                                return last

                            up_or_gate(0).then_inc(moe_used[l], 1)
                            pe.wait_ge(m["g_copied"], n_ + 1)
                            for c in range(TC):
                                for j in range(4):
                                    last = nc.tensor.matmul(wk[1][32 * j:32 * j + 32, tok(c)], gsel[:, c, e, :],
                                                            ident, start=True, stop=True)
                            last.then_inc(m["g_ready"], 1)
                            up_or_gate(1).then_inc(m["gu_ready"], 1)
                            if e % 4:
                                combine(e - 1)
                            pe.wait_ge(m["hid_done"], n_ + 2)
                            pe.sem_inc(moe_used[l], 1)
                            nc.tensor.transpose(wk[2][:, 0:P], hid, ident).then_inc(m["hidT_ready"], 1)
                            here(3 * e + 2)
                            pe.wait_ge(m["hidT_copied"], n_ + 1)
                            wd = tall(moe_slot(3 * e + 2))
                            for k in range(4):
                                for j in range(4):
                                    last = nc.tensor.matmul(wk[3][32 * j:32 * j + 32, 0:256], hidT[:, k, :],
                                                            wd[:, k, j * 256:(j + 1) * 256],
                                                            start=(k == 0), stop=(k == 3))
                            last.then_inc(m["y_ready"], 1)
                            pe.wait_ge(m["y_ready"], n_ + 2)
                            pe.sem_inc(moe_used[l], 1)
                        combine(PER - 1)
                        pe.wait_ge(m["combined"], it * PER + (PER + 1))
                        pe.sem_inc(m["sel_spent"], 1)
                pe.sem_inc(m["moe_done"], 1)

            experts(0)

            transposed_norm("mix1")
            normed("mix1")
            pe.wait_ge(act_s, A.at("y0b"))
            pe.wait_ge(dve_s, V.at("y0b"))
            seed_wide()
            with pe.Fori(0, RH // 2) as i:
                def fill(name, hp):
                    b, k = odd_use(name, hp)
                    pe.wait_ge(odd_drained[b], i * 6 + (k + 1))
                    return wk[b], odd_filled[b]

                def here(kind, hp):
                    s = odd_slot[(kind, hp)]
                    n = 32 if kind == "qk" else 16
                    pe.wait_ge(odd_here[s], i * n + n)
                    return (tall if kind == "wo" else wide)(s)

                def used(name, hp):
                    b, k = odd_use(name, hp)
                    pe.wait_ge(odd_filled[b], i * 6 + (k + 1))
                    pe.sem_inc(odd_used, 1)

                def qk(hp):
                    w_ = here("qk", hp)
                    for j, name in enumerate("qk"):
                        b, f = fill(name, hp)
                        for m_ in range(2):
                            last = project(b[:, m_ * SEQ:(m_ + 1) * SEQ],
                                           lambda k: w_[:, k, j * RQK + m_ * P:j * RQK + (m_ + 1) * P],
                                           lambda k: xnT[:, k, :])
                        last.then_inc(f, 1)
                    used("k", hp)

                def token_major(kind, hp):
                    w_ = here(kind, hp)
                    for c in range(TC):
                        b, f = fill(f"{kind}{c}", hp)
                        project(b[:, :], lambda k: xnT[:, k, tok(c)], lambda k: w_[:, k, :]).then_inc(f, 1)
                    used(f"{kind}1", hp)

                def ret_scores(hp):
                    pe.wait_ge(O["qT_done"], i * 2 + (hp + 1))
                    pe.wait_ge(O["kT_done"], i * 2 + (hp + 1))
                    for s in range(2):
                        b, f = fill(f"S{s}", hp)
                        for m_ in range(2):
                            last = nc.tensor.matmul(b[:, 0:SEQ - s * P], kT[:, m_, tok(s)], qT[:, m_, s * P:SEQ],
                                                    start=(m_ == 0), stop=(m_ == 1))
                        last.then_inc(f, 1)

                def ret_out(hp):
                    pe.wait_ge(O["sT_done"], i * 4 + (2 * hp + 2))
                    pe.wait_ge(O["v_done"], i * 4 + (2 * hp + 2))
                    b, f = fill("O0", hp)
                    nc.tensor.matmul(b[:, :], sT[:, 0:128], vr[:, 0, :], start=True, stop=True).then_inc(f, 1)
                    b, f = fill("O1", hp)
                    nc.tensor.matmul(b[:, :], sT[:, 128:256], vr[:, 0, :], start=True, stop=False)
                    nc.tensor.matmul(b[:, :], sT[:, 256:384], vr[:, 1, :], start=False, stop=True).then_inc(f, 1)

                def turn(hp):
                    for c in range(TC):
                        pe.wait_ge(O["y_done"], i * 4 + (2 * hp + c + 1))
                        b, f = fill(f"T{c}", hp)
                        for k in range(4):
                            last = nc.tensor.transpose(b[:, k * P:(k + 1) * P], yr[:, c, k * P:(k + 1) * P], ident)
                        last.then_inc(f, 1)

                def out_proj(hp):
                    w_ = here("wo", hp)
                    for c in range(TC):
                        pe.wait_ge(O["yT_done"], i * 4 + (2 * hp + c + 1))
                        for hf in range(2):
                            for k in range(4):
                                last = nc.tensor.matmul(acc[2 * c + hf][:, :], yT[:, c, k, :],
                                                        w_[:, k, hf * 512:(hf + 1) * 512], start=False, stop=False,
                                                        skip_group_check=True)
                    last.then_inc(O["o_all"], 1)
                    pe.wait_ge(O["o_all"], i * 2 + (hp + 1))
                    pe.sem_inc(odd_used, 1)

                qk(0)
                token_major("v", 0)
                ret_scores(0)
                token_major("g", 0)
                ret_out(0)
                qk(1)
                turn(0)
                out_proj(0)
                token_major("v", 1)
                ret_scores(1)
                token_major("g", 1)
                ret_out(1)
                turn(1)
                out_proj(1)
            pe.sem_inc(pe_s, PE.done("OUT1"))
            experts(1)

        @block.scalar
        def _(act):
            links = [0]

            def link(ins):
                links[0] += 1
                ins.then_inc(chain_a, 1)
                act.wait_ge(chain_a, links[0])

            def norm_stats(e, name="std"):
                for c in range(TC):
                    last = nc.scalar.activation(xn[:, c, :, :].rearrange("p a b -> p (a b)"), x[:, c, :], ACT.Square,
                                                accum_out=ss[:, c:c + 1])
                last.then_inc(act_s, A.done(f"{e}:sq"))
                act.wait_ge(dve_s, V.at(f"{e}:ms"))
                nc.scalar.activation(std, ms, ACT.Sqrt).then_inc(act_s, A.done(f"{e}:std"))

            def drain_xT(e):
                for b in (0, 2):
                    act.wait_ge(pe_s, PE.at(f"{e}:xT{b}"))
                    nc.scalar.activation(xnT[:, 2 * b:2 * b + 2, :], wk[b][:, :].rearrange("p (c t) -> p c t", c=2),
                                         ACT.Copy).then_inc(act_s, A.done(f"{e}:xT{b}"))

            act.wait_ge(x_in_sem, 16)
            norm_stats("mix0")
            drain_xT("mix0")
            for c in range(TC):
                act.wait_ge(pe_s, PE.at(f"Z{c}"))
                nc.scalar.activation(zc[:, c, :], wk[c][:, 0:ZC], ACT.Copy).then_inc(act_s, A.done(f"Z{c}"))
            act.wait_ge(act_s, A.at("Z1"))
            for c in range(TC):
                nc.scalar.activation(cqT[:, c, :], zc[:, c, 0:Q_LORA], ACT.Square, accum_out=s4[:, 2 * c:2 * c + 1])
                last = nc.scalar.activation(probT[:, c, 0:KV_LORA], zc[:, c, Q_LORA:Q_LORA + KV_LORA], ACT.Square,
                                            accum_out=s4[:, 2 * c + 1:2 * c + 2])
            last.then_inc(act_s, A.done("sq4"))
            half8 = FOX ** -0.5

            def drain_qf(b):
                act.wait_ge(pe_s, PE.at(f"QF{b}"))
                nc.scalar.activation(qfT[:, 2 * b:2 * b + 2, :], wk[2 + b][:, :].rearrange("p (c t) -> p c t", c=2),
                                     ACT.Copy, scale=half8).then_inc(act_s, A.done(f"QF{b}"))

            drain_qf(0)
            act.wait_ge(dve_s, V.at("zlog"))
            nc.scalar.activation(zabs, zlog, ACT.Abs).then_inc(act_s, A.done("zabs"))
            act.wait_ge(act_s, A.at("zabs"))
            nc.scalar.activation(zexp, zabs, ACT.Exp, scale=-1.0).then_inc(act_s, A.done("zexp"))
            act.wait_ge(act_s, A.at("zexp"))
            act.wait_ge(ready, 1)
            nc.scalar.activation(zabs, zexp, ACT.Ln, bias=ones[:, 0:1]).then_inc(act_s, A.done("zln"))
            act.wait_ge(dve_s, V.at("ms4"))
            nc.scalar.activation(r4, s4, ACT.Sqrt).then_inc(act_s, A.done("std4"))
            drain_qf(1)
            act.wait_ge(pe_s, PE.at("VF0"))
            nc.scalar.activation(vf[:, 0, :], wk[2][:, :], ACT.Copy).then_inc(act_s, A.done("VF0"))
            act.wait_ge(pe_s, PE.at("CT"))
            nc.scalar.activation(ncT[0:8, :], wk[1][0:8, 0:SEQ], ACT.Copy, scale=-1.0).then_inc(act_s, A.done("CT"))
            act.wait_ge(pe_s, PE.at("CQ"))
            nc.scalar.activation(cqT, wk[0][:, :].rearrange("p (c t) -> p c t", c=2), ACT.Copy
                                 ).then_inc(act_s, A.done("CQ"))
            act.wait_ge(pe_s, PE.at("CK"))
            act.wait_ge(dve_s, V.at("CK"))
            nc.scalar.activation(k96T[64:96, :, :], wk[2][64:96, None, SEQ:2 * SEQ].broadcast_to([32, HEADS, SEQ]),
                                 ACT.Copy).then_inc(act_s, A.done("kpe"))
            banks = {"QA0": 3, "QB0": 0, "QA1": 1, "QB1": 3}
            for c in range(TC):
                for i, name in enumerate(("QA", "QB")):
                    act.wait_ge(pe_s, PE.at(f"{name}{c}"))
                    nc.scalar.activation(q_tok[:, c, i * 384:(i + 1) * 384], wk[banks[f"{name}{c}"]][:, 0:384], ACT.Copy,
                                         scale=QK ** -0.5).then_inc(act_s, A.done(f"{name}{c}"))
            for m_, b in ((0, 2), (2, 1)):
                act.wait_ge(pe_s, PE.at(f"KN{m_}"))
                nc.scalar.activation(k96T[0:64, 2 * m_:2 * m_ + 2, :], wk[b][0:64, :].rearrange("p (c t) -> p c t", c=2),
                                     ACT.Copy).then_inc(act_s, A.done(f"KN{m_}"))
            act.wait_ge(pe_s, PE.at("VM0"))
            nc.scalar.activation(vm[:, 0, :], wk[2][:, :], ACT.Copy).then_inc(act_s, A.done("VM0"))
            for m_, b in ((0, 1), (2, 2)):
                act.wait_ge(pe_s, PE.at(f"QT{m_}"))
                nc.scalar.activation(q96T[0:QK, 2 * m_:2 * m_ + 2, :], wk[b][0:QK, :].rearrange("p (c t) -> p c t", c=2),
                                     ACT.Copy).then_inc(act_s, A.done(f"QT{m_}"))

            def drain_probT(a):
                act.wait_ge(pe_s, PE.at(f"T{a}"))
                if a >= 2:
                    act.wait_ge(pe_s, PE.at(f"O{a - 2}"))
                nc.scalar.activation(probT[:, a % 2, :], (wk[2], acc[0])[a % 2][:, 0:384], ACT.Copy
                                     ).then_inc(act_s, A.done(f"p{a}"))

            for a in range(16):
                act.wait_ge(dve_s, V.at(f"m{a}"))
                for c, lo, n in SEG:
                    last = nc.scalar.activation(prob[:, a % DEEP, lo:lo + n], prob[:, a % DEEP, lo:lo + n], ACT.Exp,
                                                bias=nmx[:, a % DEEP, c:c + 1], accum_out=sm[:, a % DEEP, c:c + 1])
                last.then_inc(act_s, A.done(f"e{a}"))
                if a > 1:
                    drain_probT(a - 2)
            drain_probT(14)
            drain_probT(15)

            def drain_wide(name, step):
                act.wait_ge(pe_s, PE.at(name))
                for hf in range(2):
                    nc.scalar.activation(x[:, 0, hf * 512:(hf + 1) * 512], acc[hf][:, :], ACT.Copy
                                         ).then_inc(act_s, A.done(f"{step}{'ab'[hf]}"))
                act.wait_ge(act_s, A.at(f"{step}b"))
                act.wait_ge(dve_s, V.at(f"{step}b"))

            drain_wide("OUT0", "x0")

            def experts(l):
                m = M[l]
                norm_stats(f"ffn{l}")
                drain_xT(f"ffn{l}")
                act.wait_ge(dve_s, V.at(f"gd{l}"))
                nc.scalar.activation(t4, t4, ACT.Exp).then_inc(act_s, A.done(f"ge{l}"))
                act.wait_ge(dve_s, V.at(f"ed{l}"))
                nc.scalar.activation(t8, t8, ACT.Exp)
                nc.scalar.activation(rt[:, 8:10], rt[:, 8:10], ACT.Exp).then_inc(act_s, A.done(f"ee{l}"))
                act.wait_ge(rounds_set[l], 1)
                nr = act.value_load(rounds[0:1, l:l + 1], min_val=1, max_val=ROUNDS)
                with act.Fori(0, nr) as r:
                    with act.Fori(0, GROUPS) as i:
                        it = r * GROUPS + i
                        for e in range(PER):
                            n_ = it * PER + e
                            if e % 4 == 0:
                                act.wait_ge(m["gath_ready"], it * 4 + (e // 2 + 1))
                                nc.scalar.activation(xg[:, e // 4, 0:4, :],
                                                     wk[2][:, :].rearrange("p (c s) -> p c s", c=4), ACT.Copy
                                                     ).then_inc(m["xg_copied"], 1)
                            act.wait_ge(m["gu_ready"], n_ + 1)
                            act.wait_ge(m["hid_done"], n_ + 1)
                            nc.scalar.activation(act_g, wk[0][:, 0:P], ACT.Silu
                                                 ).then_inc(m["silu_done"], 1)
                            act.wait_ge(m["hidT_ready"], n_ + 2)
                            act.wait_ge(m["y_ready"], n_ + 1)
                            nc.scalar.activation(hidT.rearrange("p k s -> p (k s)"), wk[2][:, 0:P], ACT.Copy
                                                 ).then_inc(m["hidT_copied"], 1)
                act.wait_ge(m["moe_done"], 1)
                for j in range(2):
                    nc.scalar.activation(x[:, :, j * 256:(j + 1) * 256],
                                         acc[j][:, :].rearrange("p (c n) -> p c n", c=TC), ACT.Copy
                                         ).then_inc(act_s, A.done(f"y{l}{'ab'[j]}"))
                act.wait_ge(act_s, A.at(f"y{l}b"))
                act.wait_ge(dve_s, V.at(f"y{l}b"))

            experts(0)

            norm_stats("mix1")
            drain_xT("mix1")
            for b in range(4):
                act.sem_inc(odd_drained[b], 1)
            with act.Fori(0, RH // 2) as i:
                def got(name, hp):
                    b, k = odd_use(name, hp)
                    act.wait_ge(odd_filled[b], i * 6 + (k + 1))
                    return wk[b], odd_drained[b]

                def values(hp):
                    for c in range(TC):
                        b, d = got(f"v{c}", hp)
                        ins = nc.scalar.activation(vr[:, c, :], b[:, :], ACT.Copy)
                        ins.then_inc(d, 1)
                    act.wait_ge(d, i * 6 + (odd_use("v1", hp)[1] + 2))
                    act.sem_inc(O["v_done"], 2)

                def gate(hp):
                    for c in range(TC):
                        b, d = got(f"g{c}", hp)
                        nc.scalar.activation(sg[:, c, :], b[:, :], ACT.Silu).then_inc(d, 1)
                    act.wait_ge(d, i * 6 + (odd_use("g1", hp)[1] + 2))
                    act.sem_inc(O["sg_done"], 2)

                def stats(hp):
                    for c in range(TC):
                        b, _ = got(f"O{c}", hp)
                        nc.scalar.activation(junk[:, c, :], b[:, :], ACT.Square, accum_out=ss[:, c:c + 1]
                                             ).then_inc(O["sq_done"], 1)
                    act.wait_ge(O["ms_done"], i * 2 + (hp + 1))
                    nc.scalar.activation(std, ms, ACT.Sqrt).then_inc(O["std_done"], 1)

                def drain_T(hp):
                    for c in range(TC):
                        b, d = got(f"T{c}", hp)
                        nc.scalar.activation(yT[:, c, :, :].rearrange("p k t -> p (k t)"), b[:, :], ACT.Copy).then_inc(d, 1)
                        act.wait_ge(d, i * 6 + (odd_use(f"T{c}", hp)[1] + 2))
                        act.sem_inc(O["yT_done"], 1)

                for hp in range(2):
                    values(hp)
                    gate(hp)
                    stats(hp)
                    drain_T(hp)
            drain_wide("OUT1", "x1")
            experts(1)
            for c in range(TC):
                last = nc.scalar.activation(xn[:, c, :, :].rearrange("p a b -> p (a b)"), x[:, c, :], ACT.Square,
                                            accum_out=ss[:, c:c + 1])
            last.then_inc(act_s, A.done("fin:sq"))
            act.wait_ge(dve_s, V.at("fin:ms"))
            nc.scalar.activation(std, ms, ACT.Sqrt).then_inc(act_s, A.done("fin:std"))

        @block.vector
        def _(dve):
            links = [0]

            def link(ins):
                links[0] += 1
                ins.then_inc(chain_v, 1)
                dve.wait_ge(chain_v, links[0])

            tt, ts, stt = nc.vector.tensor_tensor, nc.vector.tensor_scalar, nc.vector.scalar_tensor_tensor

            def norm(e, slot, loads):
                dve.wait_ge(act_s, A.at(f"{e}:sq"))
                ts(ms, ss, 1.0 / D, EPS, ALU.mult, ALU.add).then_inc(dve_s, V.done(f"{e}:ms"))
                dve.wait_ge(act_s, A.at(f"{e}:std"))
                link(nc.vector.reciprocal(rstd, std))
                dve.wait_ge(gain_in[slot], 16 * loads)
                for c in range(TC):
                    stt(xn[:, c, :, :], x[:, c, :].rearrange("p (a b) -> p b a", b=DC), rstd[:, c:c + 1],
                        gain[:, slot, :].rearrange("p (a b) -> p b a", b=DC), ALU.mult, ALU.mult
                        ).then_inc(dve_s, V.done(f"{e}:xn{c}"))

            def drain_xT(e):
                for b in (1, 3):
                    dve.wait_ge(pe_s, PE.at(f"{e}:xT{b}"))
                    nc.vector.tensor_copy(xnT[:, 2 * b:2 * b + 2, :], wk[b][:, :].rearrange("p (c t) -> p c t", c=2)
                                          ).then_inc(dve_s, V.done(f"{e}:xT{b}"))

            def drain(dst, name, src):
                dve.wait_ge(pe_s, PE.at(name))
                nc.vector.tensor_copy(dst, src).then_inc(dve_s, V.done(name))

            dve.wait_ge(x_in_sem, 16)
            norm("mix0", 0, 1)
            drain_xT("mix0")
            dve.wait_ge(const_in, 16)
            dve.wait_ge(act_s, A.at("Z1"))
            dve.wait_ge(small_in, 16 * 7)
            tt(zlog, zc[:, :, FQ:ZC], bf[:, None, :].broadcast_to([P, TC, HEADS]), ALU.add).then_inc(dve_s, V.done("zlog"))
            dve.wait_ge(act_s, A.at("sq4"))
            lat = s4.rearrange("p (c k) -> p c k", c=TC)
            link(ts(lat[:, :, 0], lat[:, :, 0], 1.0 / Q_LORA, EPS, ALU.mult, ALU.add))
            ts(lat[:, :, 1], lat[:, :, 1], 1.0 / KV_LORA, EPS, ALU.mult, ALU.add).then_inc(dve_s, V.done("ms4"))
            two = lambda b: b[:, :].rearrange("p (c t) -> p c t", c=2)
            drain(kfT[:, 0:2, :], "KF0", two(wk[0]))
            drain(kfT[:, 2:4, :], "KF1", two(wk[1]))
            dve.wait_ge(act_s, A.at("zln"))
            stt(logf, zlog, 0.0, zabs, ALU.min, ALU.subtract).then_inc(dve_s, V.done("logf"))
            drain(vf[:, 1, :], "VF1", wk[3][:, :])
            dve.wait_ge(act_s, A.at("std4"))
            link(nc.vector.reciprocal(r4, r4))
            for c in range(TC):
                stt(zc[:, c, 0:Q_LORA], zc[:, c, 0:Q_LORA], r4[:, 2 * c:2 * c + 1], lnqkv[:, 0:Q_LORA], ALU.mult, ALU.mult)
                last = stt(zc[:, c, Q_LORA:Q_LORA + KV_LORA], zc[:, c, Q_LORA:Q_LORA + KV_LORA],
                           r4[:, 2 * c + 1:2 * c + 2], lnqkv[:, Q_LORA:], ALU.mult, ALU.mult)
            last.then_inc(dve_s, V.done("cqn"))

            def rope(parts, heads, cos, sin, name):
                a = ropek[:, 0:0 + heads * 32]
                bb = tmp_rope[:, 0:heads * 32]
                a4 = a.rearrange("p (h k f) -> p h k f", h=heads, k=2)
                b4 = bb.rearrange("p (h k f) -> p h k f", h=heads, k=2)
                tt(a4, parts, cos, ALU.mult)
                link(tt(b4, parts, sin, ALU.mult))
                tt(parts[:, :, 0, :], a4[:, :, 0, :], b4[:, :, 1, :], ALU.subtract)
                return tt(parts[:, :, 1, :], b4[:, :, 0, :], a4[:, :, 1, :], ALU.add)

            tmp_rope = probT.rearrange("p b n -> p (b n)")

            def phase(name, c=None, heads=HEADS):
                v = C(name).rearrange("p (c f) -> p c f", c=TC)
                if c is None:
                    return v[:, :, None, :].broadcast_to([P, TC, 2, 16])
                return v[:, c:c + 1, None, :].broadcast_to([P, heads, 2, 16])

            rope(zc[:, :, FQ - ROPE:FQ].rearrange("p c (k f) -> p c k f", k=2), TC, phase("cos"), phase("sin"), "kpe"
                 ).then_inc(dve_s, V.done("kpe"))
            dve.wait_ge(dve_s, V.at("kpe"))
            dve.wait_ge(pe_s, PE.at("CU"))
            nc.vector.tensor_copy(cum.rearrange("p c h -> p (c h)"), wk[0][:, 0:16]).then_inc(dve_s, V.done("CU"))
            drain(ckvT, "CK", wk[2][:, 0:SEQ])
            for c in range(TC):
                dve.wait_ge(act_s, A.at(f"QB{c}"))
                parts = q_tok[:, c, :].rearrange("p (h n) -> p h n", h=HEADS)[:, :, NOPE:].rearrange(
                    "p h (k f) -> p h k f", k=2)
                rope(parts, HEADS, phase("cos", c), phase("sin", c), f"rope{c}").then_inc(dve_s, V.done(f"rope{c}"))
                dve.wait_ge(dve_s, V.at(f"rope{c}"))
            drain(k96T[0:64, 2:4, :], "KN1", two(wk[0])[0:64])
            drain(k96T[0:64, 6:8, :], "KN3", two(wk[3])[0:64])
            drain(vm[:, 1, :], "VM1", wk[0][:, :])
            drain(q96T[0:QK, 2:4, :], "QT1", two(wk[3])[0:QK])
            drain(q96T[0:QK, 6:8, :], "QT3", two(wk[0])[0:QK])

            def drain_o(pair):
                dve.wait_ge(pe_s, PE.at(f"O{2 * pair + 1}"))
                nc.vector.tensor_copy(oT[:, pair, :], (wk[3], acc[1])[pair % 2][:, 0:SEQ]
                                      ).then_inc(dve_s, V.done(f"o{pair}"))

            def invert(a):
                dve.wait_ge(act_s, A.at(f"e{a}"))
                nc.vector.reciprocal(rsm[:, a % DEEP, :], sm[:, a % DEEP, :]).then_inc(dve_s, V.done(f"r{a}"))

            for a in range(16):
                dve.wait_ge(pe_s, PE.at(f"S{a}"))
                sc = (wk[0], wk[1], acc[2], acc[3])[a % DEEP]
                pr = prob[:, a % DEEP, :]
                if a >= DEEP:
                    dve.wait_ge(pe_s, PE.at(f"T{a - DEEP}"))
                if a < 8:
                    ins = tt(pr, sc[:, 0:384], C("mla"), ALU.add)
                else:
                    for c, lo, n in SEG:
                        ins = stt(pr[:, lo:lo + n], sc[:, lo:lo + n], cum[:, c, a - 8:a - 7],
                                  C("fox")[:, lo:lo + n], ALU.add, ALU.add)
                ins.then_inc(dve_s, V.done(f"s{a}"))
                dve.wait_ge(dve_s, V.at(f"s{a}"))
                for c, lo, n in SEG:
                    ins = nc.vector.reduce_max(mx[:, a % DEEP, c:c + 1], pr[:, lo:lo + n], AX.X)
                link(ins)
                ts(nmx[:, a % DEEP, :], mx[:, a % DEEP, :], -1.0, None, ALU.mult).then_inc(dve_s, V.done(f"m{a}"))
                if a:
                    invert(a - 1)
                if a % 2 == 0 and a > 2:
                    drain_o(a // 2 - 2)
            invert(15)
            drain_o(6)
            drain_o(7)

            def drain_wide(name, step):
                dve.wait_ge(pe_s, PE.at(name))
                for hf in range(2):
                    nc.vector.tensor_copy(x[:, 1, hf * 512:(hf + 1) * 512], acc[2 + hf][:, :]
                                          ).then_inc(dve_s, V.done(f"{step}{'ab'[hf]}"))
                dve.wait_ge(dve_s, V.at(f"{step}b"))
                dve.wait_ge(act_s, A.at(f"{step}b"))

            drain_wide("OUT0", "x0")

            def experts(l):
                m = M[l]
                norm(f"ffn{l}", 1, l + 1)
                drain_xT(f"ffn{l}")
                dve.wait_ge(pe_s, PE.at(f"lg{l}"))
                logits = wk[0][:, 0:128].rearrange("p (c n) -> p c n", c=TC)[:, :, 0:NR]
                link(tt(lg, logits, br[:, l:l + 1, :].broadcast_to([P, TC, NR]), ALU.add))
                gl = lg[:, :, 0:GROUPS]
                gmax, pg, first, m1, p2, s8, pr1, pr2, den, ga, gb = (rt[:, 2 * k:2 * k + 2] for k in
                                                                     (0, 1, 2, 3, 4, 5, 6, 7, 8, 9, 10))
                m2, base, mc = rt[:, 22:24], rt[:, 24:26], rt[:, 26:27]

                def wide_of(s, n):
                    return s[:, :, None].broadcast_to([P, TC, n])

                def first_max(dst, vals, best, arg, n, t):
                    link(tt(t, vals, wide_of(best, n), ALU.is_equal))
                    ar = C(arg)[:, None, :].broadcast_to([P, TC, n])
                    link(tt(t, t, ar, ALU.mult))
                    link(nc.vector.tensor_reduce(first, t, AX.X, ALU.min))
                    link(tt(dst, ar, wide_of(first, n), ALU.is_equal))

                link(nc.vector.reduce_max(gmax, gl, AX.X))
                first_max(oh4, gl, gmax, "arg4", GROUPS, t4)
                tt(t4, gl, wide_of(gmax, GROUPS), ALU.subtract).then_inc(dve_s, V.done(f"gd{l}"))
                ea = lg[:, :, GROUPS:].rearrange("p c (g j) -> p c g j", g=GROUPS)
                link(tt(tmp, ea, oh4[:, :, :, None].broadcast_to([P, TC, GROUPS, PER]), ALU.mult))
                link(nc.vector.reduce_sum(el, tmp.rearrange("p c g j -> p c j g"), AX.X))
                link(nc.vector.reduce_max(m1, el, AX.X))
                first_max(oh8[:, 0], el, m1, "arg8", PER, t8)
                link(stt(el2, oh8[:, 0], -BIG, el, ALU.mult, ALU.add))
                link(nc.vector.reduce_max(m2, el2, AX.X))
                first_max(oh8[:, 1], el2, m2, "arg8", PER, t8)
                tt(t8, el, wide_of(m1, PER), ALU.subtract)
                tt(p2, m2, m1, ALU.subtract).then_inc(dve_s, V.done(f"ed{l}"))
                dve.wait_ge(act_s, A.at(f"ge{l}"))
                link(nc.vector.reduce_sum(pg, t4, AX.X))
                dve.wait_ge(act_s, A.at(f"ee{l}"))
                link(nc.vector.reduce_sum(s8, t8, AX.X))
                link(nc.vector.reciprocal(pg, pg))
                link(nc.vector.reciprocal(pr1, s8))
                link(tt(pr2, p2, pr1, ALU.mult))
                link(tt(den, pr1, pr2, ALU.add))
                link(nc.vector.reciprocal(den, den))
                link(tt(base, pg, den, ALU.mult))
                tt(ga, base, pr1, ALU.mult)
                link(tt(gb, base, pr2, ALU.mult))
                link(tt(t8, oh8[:, 0], oh8[:, 1], ALU.add))
                four = lambda v: v[:, :, None, :].broadcast_to([P, TC, GROUPS, PER])
                grp = oh4[:, :, :, None].broadcast_to([P, TC, GROUPS, PER])
                tt(asg, four(t8), grp, ALU.mult).then_inc(dve_s, V.done(f"asg{l}"))
                link(tt(el, oh8[:, 0], wide_of(ga, PER), ALU.mult))
                link(tt(el2, oh8[:, 1], wide_of(gb, PER), ALU.mult))
                link(tt(el, el, el2, ALU.add))
                link(tt(gates.rearrange("p c (g j) -> p c g j", g=GROUPS), four(el), grp, ALU.mult))
                dve.wait_ge(pe_s, PE.at(f"rk{l}"))
                rank = wk[1][:, 0:64].rearrange("p (c e) -> p c e", c=TC)
                link(tt(place, rank, asg.rearrange("p c g j -> p c (g j)"), ALU.mult))
                link(ts(place, place, 1.0, None, ALU.subtract))
                link(nc.vector.reduce_max(mc, wk[1][:, 64:96], AX.X))
                link(ts(rt[0:1, 28:28 + ROUNDS - 1], C("more", 1), mc[0:1, :], None, ALU.is_lt))
                link(nc.vector.reduce_sum(rt[0:1, 27:28], rt[0:1, 28:28 + ROUNDS - 1], AX.X))
                ts(rounds[0:1, l:l + 1], rt[0:1, 27:28], 1.0, None, ALU.add).then_inc(rounds_set[l], 1)
                dve.wait_ge(rounds_set[l], 1)
                for n in ("hid_done", "g_copied"):
                    dve.sem_inc(m[n], 1)
                nr = dve.value_load(rounds[0:1, l:l + 1], min_val=1, max_val=ROUNDS)
                with dve.Fori(0, nr) as r:
                    with dve.Fori(0, GROUPS) as i:
                        it = r * GROUPS + i
                        dve.wait_ge(m["sel_spent"], it + 1)
                        slots = C("iota")[:, None, :].broadcast_to([P, PER, SLOTS])
                        for c in range(TC):
                            pl = place[:, c, bass.ds(i * PER, PER)][:, :, None].broadcast_to([P, PER, SLOTS])
                            ins = tt(sel[:, c], pl, slots, ALU.is_equal)
                        ins.then_inc(m["gsel_masked"], 1)
                        dve.wait_ge(m["gsel_masked"], it + 1)
                        for c in range(TC):
                            gt = gates[:, c, bass.ds(i * PER, PER)][:, :, None].broadcast_to([P, PER, SLOTS])
                            ins = tt(gsel[:, c], sel[:, c], gt, ALU.mult)
                        ins.then_inc(m["sel_ready"], 1)
                        for e in range(PER):
                            n_ = it * PER + e
                            if e % 4 == 0:
                                dve.wait_ge(m["gath_ready"], it * 4 + (e // 2 + 2))
                                nc.vector.tensor_copy(xg[:, e // 4, 4:8, :],
                                                      wk[1][:, :].rearrange("p (c s) -> p c s", c=4)
                                                      ).then_inc(m["xg_copied"], 1)
                            dve.wait_ge(m["silu_done"], n_ + 1)
                            dve.wait_ge(m["hidT_ready"], n_ + 1)
                            tt(hid, wk[0][:, P:2 * P], act_g, ALU.mult).then_inc(m["hid_done"], 1)
                            dve.wait_ge(m["g_ready"], n_ + 1)
                            dve.wait_ge(m["combined"], n_ + 1)
                            nc.vector.tensor_copy(gT, wk[1][:, 0:SEQ]).then_inc(m["g_copied"], 1)
                            dve.wait_ge(m["y_ready"], n_ + 2)
                            nc.vector.tensor_copy(ye, wk[3][:, 0:256]).then_inc(m["y_copied"], 1)
                    ts(place, place, float(SLOTS), None, ALU.subtract).then_inc(m["place_moved"], 1)
                    dve.wait_ge(m["place_moved"], r + 1)
                dve.wait_ge(m["moe_done"], 1)
                for j in range(2, 4):
                    nc.vector.tensor_copy(x[:, :, j * 256:(j + 1) * 256],
                                          acc[j][:, :].rearrange("p (c n) -> p c n", c=TC)
                                          ).then_inc(dve_s, V.done(f"y{l}{'ab'[j - 2]}"))
                dve.wait_ge(dve_s, V.at(f"y{l}b"))
                dve.wait_ge(act_s, A.at(f"y{l}b"))

            experts(0)

            norm("mix1", 0, 2)
            drain_xT("mix1")
            dve.wait_ge(odd_in, 16)
            cosT = odd[:, 0:256][:, None, :].broadcast_to([P, 2, SEQ])
            sinT = odd[:, 256:512][:, None, :].broadcast_to([P, 2, SEQ])
            with dve.Fori(0, RH // 2) as i:
                def got(name, hp):
                    b, k = odd_use(name, hp)
                    dve.wait_ge(odd_filled[b], i * 6 + (k + 1))
                    return wk[b], odd_drained[b]

                def rotate(hp):
                    for j, (name, dst) in enumerate((("q", qT), ("k", kT))):
                        b, d = got(name, hp)
                        src = b[:, :].rearrange("p (m t) -> p m t", m=2)
                        tt(ra, src, cosT, ALU.mult).then_inc(O["ra_done"], 1)
                        tt(rb, src, sinT, ALU.mult).then_inc(d, 1)
                        k = odd_use(name, hp)[1]
                        dve.wait_ge(O["ra_done"], i * 4 + (2 * hp + j + 1))
                        dve.wait_ge(d, i * 6 + (k + 2))
                        tt(dst[:, 0, :], ra[:, 0, :], rb[:, 1, :], ALU.subtract)
                        tt(dst[:, 1, :], rb[:, 0, :], ra[:, 1, :], ALU.add).then_inc(O[f"{name}T_done"], 1)
                        dve.wait_ge(O[f"{name}T_done"], i * 2 + (hp + 1))

                def decay(hp):
                    dec = odd[:, bass.ds(i * 768 + (512 + 384 * hp), 384)]
                    for s in range(2):
                        b, d = got(f"S{s}", hp)
                        w_ = SEQ - s * P
                        tt(sT[:, s * SEQ:s * SEQ + w_], b[:, 0:w_], dec[:, s * SEQ:s * SEQ + w_], ALU.mult).then_inc(d, 1)
                        dve.wait_ge(d, i * 6 + (odd_use(f"S{s}", hp)[1] + 2))
                        dve.sem_inc(O["sT_done"], 1)

                def finish(hp):
                    dve.wait_ge(O["sq_done"], i * 4 + (2 * hp + 2))
                    ts(ms, ss, 1.0 / RV, EPS, ALU.mult, ALU.add).then_inc(O["ms_done"], 1)
                    dve.wait_ge(O["std_done"], i * 2 + (hp + 1))
                    nc.vector.reciprocal(rstd, std).then_inc(O["rs_done"], 1)
                    dve.wait_ge(O["rs_done"], i * 2 + (hp + 1))
                    dve.wait_ge(O["sg_done"], i * 4 + (2 * hp + 2))
                    for c in range(TC):
                        b, d = got(f"O{c}", hp)
                        stt(yr[:, c, :], b[:, :], rstd[:, c:c + 1], sg[:, c, :], ALU.mult, ALU.mult).then_inc(d, 1)
                        dve.wait_ge(d, i * 6 + (odd_use(f"O{c}", hp)[1] + 2))
                        dve.sem_inc(O["y_done"], 1)

                for hp in range(2):
                    rotate(hp)
                    decay(hp)
                    finish(hp)
            drain_wide("OUT1", "x1")
            experts(1)
            dve.wait_ge(act_s, A.at("fin:sq"))
            ts(ms, ss, 1.0 / D, EPS, ALU.mult, ALU.add).then_inc(dve_s, V.done("fin:ms"))
            dve.wait_ge(act_s, A.at("fin:std"))
            link(nc.vector.reciprocal(rstd, std))
            dve.wait_ge(gain_in[0], 48)
            for c in range(TC):
                stt(x[:, c, :], x[:, c, :], rstd[:, c:c + 1], gain[:, 0, :], ALU.mult, ALU.mult
                    ).then_inc(dve_s, V.done(f"fin{c}"))


_INS = ['x', 'ln_mix_e', 'w_in_e', 'ln_q_e', 'w_uq_e', 'ln_kv_e', 'w_ukv_e', 'b_f_e', 'w_out_e', 'ln_mix_o', 'w_in_o',
        'w_out_o', 'ln_ffn', 'w_rg', 'b_rg', 'w_re', 'b_re', 'w_gate', 'w_up', 'w_down', 'ln_f']


def kernel(**inputs):
    import concourse.bacc as _bacc
    from concourse.bass_utils import run_bass_kernel_spmd as _run

    nc = _bacc.Bacc("TRN2", target_bir_lowering=False, num_devices=1)
    arrays, args = {}, []
    c, o = tables()
    for name, a in [(n, inputs[n]) for n in _INS] + [("consts", c), ("consts_odd", o)]:
        a = np.ascontiguousarray(a)
        arrays[f"in_{name}"] = a
        args.append(nc.dram_tensor(f"in_{name}", a.shape, mybir.dt.from_np(a.dtype), kind="ExternalInput").ap())
    args.append(nc.dram_tensor("out_0", (1, SEQ, D), F32, kind="ExternalOutput").ap())
    build(nc, *args)
    return _run(nc, [arrays], core_ids=[0]).results[0]["out_0"]
```

```python
import concourse.bass as bass
from concourse import mybir
from contextlib import ExitStack
import numpy as np

F32 = mybir.dt.float32
F32R = mybir.dt.float32r
I32 = mybir.dt.int32
ACT = mybir.ActivationFunctionType
ALU = mybir.AluOpType
AX = mybir.AxisListType

P = 128
SEQ = 256
TC = SEQ // P
D = 1024
DC = D // P
EPS = 1e-6
Q_LORA, KV_LORA, ROPE, NOPE, VD = 256, 128, 32, 64, 64
HEADS = 8
QK = NOPE + ROPE
FOX = 64
FQ = Q_LORA + KV_LORA + ROPE
FW = HEADS * FOX
ZC = FQ + HEADS
RH, RQK, RV = 4, 256, 512
GROUPS, PER, EXPERTS, DE = 4, 8, 32, 512
NR = GROUPS + EXPERTS
SLOTS = 32
ROUNDS = SEQ // SLOTS
RING = 8
UNIT = 4096
EVEN_UNITS, ODD_UNITS = 7, 16
BODY_UNITS = 3 * PER
DEEP = 4
BIG = 1e30
SEG = ((0, 0, 128), (1, 128, 256))

CONSTS = {}
_at = 0
for _n, _w in (("ident", 128), ("tri", 128), ("mla", 384), ("fox", 384), ("cos", 32), ("sin", 32),
               ("iota", 32), ("arg4", 4), ("arg8", 8), ("more", ROUNDS - 1)):
    CONSTS[_n] = (_at, _at + _w)
    _at += _w
NCONST = _at
NODD = 512 + RH * 384


class Steps:

    def __init__(self, names):
        self.names, self.next = list(names), 0

    def done(self, name):
        assert self.names[self.next] == name, (name, self.names[self.next])
        self.next += 1
        return 1

    def at(self, name):
        return self.names.index(name) + 1


def tables():
    c = np.zeros((P, NCONST), np.float32)

    def put(name, a):
        lo, hi = CONSTS[name]
        c[:, lo:hi] = a

    p = np.arange(P)
    put("ident", np.eye(P))
    put("tri", p[:, None] <= p[None, :])
    q0, k0 = p[:, None], p[None, :]
    q1, k1 = P + p[:, None], np.arange(SEQ)[None, :]
    put("mla", np.where(np.concatenate([k0 // 64 <= q0 // 64, k1 // 64 <= q1 // 64], 1), 0.0, -BIG))
    put("fox", np.where(np.concatenate([k0 <= q0, k1 <= q1], 1), 0.0, -BIG))
    pos = np.arange(SEQ, dtype=np.float32)

    def phase(half):
        inv = np.float32(10000.0) ** (-np.arange(half, dtype=np.float32) / np.float32(half))
        return pos[:, None] * inv[None, :]

    a16 = phase(ROPE // 2).reshape(TC, P, 16).transpose(1, 0, 2).reshape(P, 32)
    put("cos", np.cos(a16))
    put("sin", np.sin(a16))
    put("iota", np.arange(SLOTS)[None, :])
    put("arg4", np.arange(GROUPS)[None, :] - GROUPS)
    put("arg8", np.arange(PER)[None, :] - PER)
    put("more", SLOTS * np.arange(1, ROUNDS)[None, :])
    o = np.zeros((P, NODD), np.float32)
    aT = phase(RQK // 2).T
    o[:, 0:256], o[:, 256:512] = np.cos(aT), np.sin(aT)
    for h in range(RH):
        g = np.log(1.0 - 2.0 ** (-5.0 - h))
        t, s = np.arange(SEQ)[None, :], np.arange(SEQ)[:, None]
        dec = np.where(t >= s, np.exp(np.maximum(t - s, 0) * g), 0.0) * RQK ** -0.5
        o[:, 512 + 384 * h:512 + 384 * h + 256] = dec[0:128]
        o[:, 512 + 384 * h + 256:512 + 384 * (h + 1)] = dec[128:256, 128:256]
    return c, o


def build(nc, x_in, ln_mix_e, w_in_e, ln_q_e, w_uq_e, ln_kv_e, w_ukv_e, b_f_e, w_out_e,
          ln_mix_o, w_in_o, w_out_o, ln_ffn, w_rg, b_rg, w_re, b_re, w_gate, w_up, w_down,
          ln_f, consts, consts_odd, out):
    ctx = ExitStack()
    with ctx:
        def sb(name, shape, dt=F32):
            return ctx.enter_context(nc.sbuf_tensor(name, shape, dt))

        def sem(name):
            return ctx.enter_context(nc.semaphore(name))

        base = (nc.sbuf_base + 31) // 32 * 32
        ring = sb("ring", [P, RING, UNIT])
        x = sb("x", [P, TC, D])
        xn = sb("xn", [P, TC, DC, P])
        xnT = sb("xnT", [P, DC, SEQ])
        gain = sb("gain", [P, 2, D])
        arena = sb("arena", [P, 9984])
        const = sb("const", [P, NCONST])
        small = sb("small", [P, 1104])
        rounds = sb("rounds", [1, 2], I32)

        def C(name, rows=P):
            return const[0:rows, CONSTS[name][0]:CONSTS[name][1]]

        class Cut:
            def __init__(self, base):
                self.base, self.used = base, 0

            def __call__(self, n, pattern=None, **dims):
                a = self.base[:, self.used:self.used + n]
                self.used += n
                assert self.used <= self.base.shape[1], self.used
                return a.rearrange(pattern, **dims) if pattern else a

        def over(name, shape, floats):
            return nc.alloc_sbuf_tensor_at(name, shape, F32R, offset=base + 4 * floats)

        AT_X = RING * UNIT
        AT_XN, AT_XNT, AT_ARENA = AT_X + TC * D, AT_X + 2 * TC * D, AT_X + 3 * TC * D + 2 * D
        part = [over(f"slot{s}_parts", [P, UNIT], s * UNIT) for s in range(RING)]
        xh = over("x_high", [P, DC, SEQ], AT_XNT)
        xl = over("x_low", [P, TC, DC, P], AT_XN)
        yh = over("y_high", [P, TC, 4, P], AT_ARENA + 7680)
        yl = over("y_low", [P, TC, 4, P], AT_ARENA + 7680 + TC * RV)

        cut = Cut(small)
        wr = cut(2 * DC * NR, "p (l c n) -> p l c n", l=2, c=DC)
        br = cut(2 * NR, "p (l n) -> p l n", l=2)
        ones = cut(P)
        bf = cut(HEADS)
        ss = cut(2)
        s2 = cut(2)
        ms = cut(2)
        warm = cut(12)
        std = cut(2)
        rstd = cut(2)
        s4 = cut(4)
        r4 = cut(4)
        zlog = cut(16, "p (c h) -> p c h", c=TC)
        zabs = cut(16, "p (c h) -> p c h", c=TC)
        zexp = cut(16, "p (c h) -> p c h", c=TC)
        logf = cut(16, "p (c h) -> p c h", c=TC)
        cum = cut(16, "p (c h) -> p c h", c=TC)
        mx = cut(2 * DEEP, "p (b c) -> p b c", b=DEEP)
        nmx = cut(2 * DEEP, "p (b c) -> p b c", b=DEEP)
        sm = cut(2 * DEEP, "p (b c) -> p b c", b=DEEP)
        rsm = cut(2 * DEEP, "p (b c) -> p b c", b=DEEP)
        lg = cut(2 * NR, "p (c n) -> p c n", c=TC)
        oh4 = cut(8, "p (c n) -> p c n", c=TC)
        t4 = cut(8, "p (c n) -> p c n", c=TC)
        oh8 = cut(32, "p (k c n) -> p k c n", k=2, c=TC)
        t8 = cut(16, "p (c n) -> p c n", c=TC)
        el, el2 = zabs, zexp
        rt = cut(36)

        cut = Cut(arena)
        spare = Cut(ring[:, 4, 2 * HEADS * QK + 1024:])
        zc = spare(TC * ZC, "p (c n) -> p c n", c=TC)
        lnqkv = spare(Q_LORA + KV_LORA)
        ropek = spare(256)
        vm = cut(TC * 512, "p (c n) -> p c n", c=TC)
        vf = cut(TC * 512, "p (c n) -> p c n", c=TC)
        q96T = cut(HEADS * SEQ, "p (h t) -> p h t", h=HEADS)
        k96T = cut(HEADS * SEQ, "p (h t) -> p h t", h=HEADS)
        qfT = cut(4 * SEQ, "p (h t) -> p h t", h=4)
        kfT = cut(4 * SEQ, "p (h t) -> p h t", h=4)
        ncT = cut(SEQ)
        shared = cut(768)
        cqT = shared[:, 0:512].rearrange("p (k t) -> p k t", k=2)
        ckvT = shared[:, 512:768]
        probT = cut(2 * 384, "p (b n) -> p b n", b=2)
        q_tok = xn[:, :, :, :].rearrange("p c a b -> p c (a b)")[:, :, 0:HEADS * QK]
        prob = xn[:, :, :, :].rearrange("p c a b -> p (c a b)")[:, 0:DEEP * 384].rearrange(
            "p (b n) -> p b n", b=DEEP)
        oT = xnT

        cut = Cut(arena)
        odd = cut(NODD)
        qT = cut(512, "p (m t) -> p m t", m=2)
        kT = cut(512, "p (m t) -> p m t", m=2)
        ra = cut(512, "p (m t) -> p m t", m=2)
        rb = cut(512, "p (m t) -> p m t", m=2)
        vr = cut(TC * RV, "p (c n) -> p c n", c=TC)
        sg = cut(TC * RV, "p (c n) -> p c n", c=TC)
        yr = cut(TC * RV, "p (c n) -> p c n", c=TC)
        sT = cut(384)
        assert cut.used <= 7680

        cut = Cut(arena)
        asg = cut(TC * EXPERTS, "p (c g j) -> p c g j", c=TC, g=GROUPS)
        gates = cut(TC * EXPERTS, "p (c e) -> p c e", c=TC)
        place = cut(TC * EXPERTS, "p (c e) -> p c e", c=TC)
        tmp = cut(TC * EXPERTS, "p (c g j) -> p c g j", c=TC, g=GROUPS)
        sel = cut(TC * PER * SLOTS, "p (c e s) -> p c e s", c=TC, e=PER)
        gsel = cut(TC * PER * SLOTS, "p (c e s) -> p c e s", c=TC, e=PER)
        xg = cut(2 * DC * 4 * SLOTS, "p (b c s) -> p b c s", b=2, c=DC)
        act_g = cut(P)
        hid = cut(P)
        hidT = cut(P, "p (k s) -> p k s", k=4)
        ye = cut(D)
        gT = cut(SEQ)

        acc = [ctx.enter_context(nc.psum_tensor(f"acc{i}", [P, 512], F32)) for i in range(4)]
        wk = [ctx.enter_context(nc.psum_tensor(f"wk{i}", [P, 512], F32)) for i in range(4)]

        x_in_sem = [sem(f"x_chunk{c}_loaded") for c in range(TC)]
        const_in = sem("consts_loaded")
        first_gain_in = sem("first_gain_loaded")
        gain_in = [sem(f"gain{b}_loaded") for b in range(2)]
        odd_in = sem("odd_consts_loaded")
        small_in = sem("small_loaded")
        router_in = sem("router_loaded")
        ready = sem("ones_and_router_ready")
        even_here = [sem(f"even_unit{s}_loaded") for s in range(EVEN_UNITS)]
        moe_here = [[sem(f"moe{l}_slot{s}_loaded") for s in range(RING)] for l in range(2)]
        odd_here = [sem(f"odd_slot{s}_loaded") for s in range(RING)]
        even_used = sem("even_units_used")
        moe_used = [sem(f"moe{l}_units_used") for l in range(2)]
        odd_used = sem("odd_units_used")
        odd_high, odd_low = sem("odd_high_parts"), sem("odd_low_parts")
        pe_s = sem("pe_steps")
        act_s = sem("act_steps")
        dve_s = sem("dve_steps")
        pool_s = sem("pool_steps")
        chain_v = sem("dve_chain")
        chain_a = sem("act_chain")
        rounds_set = [sem(f"rounds{l}_set") for l in range(2)]
        stored = sem("out_stored")

        def moe_sems(l):
            names = ("sel_ready", "gath_ready", "xg_copied", "gu_ready", "silu_done", "hid_done",
                     "hidT_ready", "hidT_copied", "y_ready", "y_copied", "g_ready", "g_copied", "combined0",
                     "combined", "place_moved", "gsel_masked")
            return {n: sem(f"m{l}_{n}") for n in names}

        M = [moe_sems(0), moe_sems(1)]
        odd_filled = [sem(f"odd_bank{b}_filled") for b in range(4)]
        odd_drained = [sem(f"odd_bank{b}_drained") for b in range(4)]
        O = {n: sem(f"o_{n}") for n in ("qT_done", "kT_done", "v_done", "sT_done", "sg_done", "y_done", "yT_done",
                                        "sq_done", "std_done",
                                        "ms_done", "rs_done", "ra_done", "yh_done", "out0", "out1")}

        SUMMED = ("ffn0", "mix1", "ffn1")

        def norm_steps(e):
            chunks = range(TC)
            act = sum([([f"{e}:sb{c}"] if e != "mix0" else []) + [f"{e}:sa{c}", f"{e}:std{c}"] for c in chunks], [])
            copy = lambda name: [f"{e}:{name}"] if e in SUMMED else []
            dve = sum([copy(f"xa{c}") + [f"{e}:b{c}"] + copy(f"x{c}") + [f"{e}:xn{c}"] for c in chunks], [])
            if e == "fin":
                return {"act": act, "dve": dve}
            if e == "mix1":
                drains = [[f"{e}:x{k}{b}" for b in range(4)] for k in "hl"]
            else:
                drains = [[f"{e}:xT{b}" for b in range(k, 4, 2)] for k in range(2)]
            return {"act": act + drains[0], "dve": dve + drains[1], "pe": [f"{e}:xT{i}" for i in range(4)]}

        N = {e: norm_steps(e) for e in ("mix0", "ffn0", "mix1", "ffn1", "fin")}
        att_pe = ["S0", "S1", "S2"]
        for a in range(16):
            att_pe += [f"T{a}"] + ([f"S{a + 3}"] if a < 13 else []) + ([f"O{a - 1}"] if a else [])
        att_pe += ["O15"]
        router_pe = lambda l: [f"lg{l}", f"rk{l}"]
        PE = Steps(N["mix0"]["pe"] + ["Z0", "Z1", "QF0", "QF1", "KF0", "KF1", "VF0", "VF1", "CU", "CT", "CQ", "CK",
                                      "QA0", "QB0", "QA1", "QB1", "KN0", "KN1", "KN2", "KN3", "VM0", "VM1",
                                      "QT0", "QT1", "QT2", "QT3"] + att_pe + ["OUT0:0", "OUT0:1"]
                   + N["ffn0"]["pe"] + router_pe(0) + N["mix1"]["pe"] + N["ffn1"]["pe"] + router_pe(1))
        att_act = []
        for a in range(16):
            att_act += [f"e{a}"] + ([f"p{a - 2}"] if a > 1 else [])
        att_act += ["p14", "p15"]
        router_act = lambda l: [f"ge{l}", f"ee{l}"]
        A = Steps(N["mix0"]["act"] + ["Z0", "Z1", "sq4", "QF0", "zabs", "zexp", "zln", "std4", "QF1", "VF0", "CT", "CQ", "kpe",
                                      "QA0", "QB0", "QA1", "QB1", "KN0", "KN2", "VM0", "QT0", "QT2"]
                  + att_act + N["ffn0"]["act"] + router_act(0) + N["mix1"]["act"] + N["ffn1"]["act"] + router_act(1)
                  + N["fin"]["act"])
        att_dve = []
        for a in range(16):
            att_dve += [f"s{a}", f"m{a}"] + ([f"r{a - 1}"] if a else []) + ([f"o{a // 2 - 2}"] if a % 2 == 0 and a > 2 else [])
        att_dve += ["r15", "o6", "o7"]
        V = Steps(N["mix0"]["dve"] + ["zlog", "ms4", "KF0", "KF1", "logf", "VF1", "cqn", "kpe", "CU", "CK",
                                      "rope0", "rope1", "KN1", "KN3", "VM1", "QT1", "QT3"] + att_dve
                  + N["ffn0"]["dve"] + ["gd0", "ed0", "asg0"] + N["mix1"]["dve"]
                  + N["ffn1"]["dve"] + ["gd1", "ed1", "asg1"] + N["fin"]["dve"])
        G = Steps([f"n{a}" for a in range(16)])

        def wide(s):
            return ring[:, s, :].rearrange("p (c n) -> p c n", c=DC)

        def tall(s):
            return ring[:, s, :].rearrange("p (c n) -> p c n", c=4)

        z_w = ring[:, 0, 0:DC * ZC].rearrange("p (c n) -> p c n", c=DC)

        def odd_parts(j):
            return 3 + j % 2, (7 + j % 4) % RING

        def shaped(t, n, c):
            return t[:, 0:n].rearrange("p (c n) -> p c n", c=c)

        uq_w = ring[:, 4, 0:2 * HEADS * QK].rearrange("p (c n) -> p c n", c=2)
        ukv_w = ring[:, 4, 2 * HEADS * QK:2 * HEADS * QK + 1024]

        def moe_slot(l, idx):
            return ((7, 5)[l] + idx) % RING

        ODD_ORDER = (("qk", 0), ("v", 0), ("g", 0), ("qk", 1), ("wo", 0), ("v", 1), ("g", 1), ("wo", 1))
        ODD_USES = [(n, h) for h, n in ((0, "q"), (0, "k"), (0, "v0"), (0, "v1"), (0, "S0"), (0, "S1"), (0, "g0"), (0, "g1"),
                                        (0, "O0"), (0, "O1"), (1, "q"), (1, "k"), (0, "T0"), (0, "T1"), (1, "v0"), (1, "v1"),
                                        (1, "S0"), (1, "S1"), (1, "g0"), (1, "g1"), (1, "O0"), (1, "O1"), (1, "T0"), (1, "T1"))]

        def odd_use(name, hp):
            u = ODD_USES.index((name, hp))
            return u % 4, u // 4

        block = ctx.enter_context(nc.Block())

        @block.sync
        def _(sp):
            x_v = x_in.rearrange("b (c p) d -> p (b c) d", p=P)
            for c in range(TC):
                sp.dma_start(x[:, c, :], x_v[:, c, :]).then_inc(x_in_sem[c], 16)
            sp.dma_start(gain[:, 0, :], ln_mix_e[0:1, :].broadcast_to([P, D])).then_inc(first_gain_in, 16)
            sp.dma_start(const[:, :], consts).then_inc(const_in, 16)
            w = w_in_e[0].rearrange("(p c) n -> p c n", c=DC)
            sp.dma_start(z_w[:, :, 0:FQ], w[:, :, 0:FQ]).then_inc(even_here[0], 16)
            sp.dma_start(z_w[:, :, FQ:ZC], w[:, :, FQ + 3 * FW:]).then_inc(even_here[0], 16)
            for u in range(3):
                sp.dma_start(wide(1 + u), w[:, :, FQ + u * FW:FQ + (u + 1) * FW]).then_inc(even_here[1 + u], 16)
            sp.dma_start(uq_w, w_uq_e[0].rearrange("(c p) n -> p c n", p=P)).then_inc(even_here[4], 16)
            sp.dma_start(ukv_w, w_ukv_e[0]).then_inc(even_here[4], 16)
            wo = w_out_e[0].rearrange("(u c p) n -> u p c n", u=2, c=4)
            for u in range(2):
                sp.dma_start(tall(5 + u), wo[u]).then_inc(even_here[5 + u], 16)

            gate_v = w_gate.rearrange("l e (p c) n -> (l e) p (c n)", c=DC)
            up_v = w_up.rearrange("l e (p c) n -> (l e) p (c n)", c=DC)
            down_v = w_down.rearrange("l e (c p) n -> (l e) p c n", c=4)

            def load_expert_part(l, group, idx):
                e = group * PER + (l * EXPERTS + idx // 3)
                s = moe_slot(l, idx)
                if idx % 3 == 2:
                    sp.dma_start(tall(s), down_v[bass.ds(e, 1)].rearrange("e p c n -> p (e c) n")
                                 ).then_inc(moe_here[l][s], 16)
                else:
                    v = (gate_v, up_v)[idx % 3]
                    sp.dma_start(ring[:, s, :], v[bass.ds(e, 1)].rearrange("e p n -> p (e n)")
                                 ).then_inc(moe_here[l][s], 16)

            def first_units(l, free):
                for idx in range(RING):
                    free(idx)
                    load_expert_part(l, 0, idx)

            def rest_of_experts(l):
                sp.sem_inc(moe_used[l], RING)
                with sp.Fori(0, GROUPS - 1) as i:
                    for idx in range(RING, BODY_UNITS):
                        sp.wait_ge(moe_used[l], i * BODY_UNITS + (idx + 1))
                        load_expert_part(l, i, idx)
                    for idx in range(RING):
                        sp.wait_ge(moe_used[l], i * BODY_UNITS + (BODY_UNITS + idx + 1))
                        load_expert_part(l, i + 1, idx)
                for idx in range(RING, BODY_UNITS):
                    sp.wait_ge(moe_used[l], (GROUPS - 1) * BODY_UNITS + idx + 1)
                    load_expert_part(l, GROUPS - 1, idx)
                sp.wait_ge(rounds_set[l], 1)
                n = sp.value_load(rounds[0:1, l:l + 1], min_val=1, max_val=ROUNDS)
                with sp.If(n > 1):
                    with sp.Fori(1, n) as r:
                        with sp.Fori(0, GROUPS) as i:
                            for idx in range(BODY_UNITS):
                                sp.wait_ge(moe_used[l], r * (GROUPS * BODY_UNITS) + i * BODY_UNITS + (idx + 1))
                                load_expert_part(l, i, idx)
                return n

            def after_even(idx):
                if idx:
                    sp.wait_ge(even_used, idx)
                if idx == 1:
                    sp.wait_ge(ready, 5)

            first_units(0, after_even)
            n0 = rest_of_experts(0)

            wi = w_in_o[0].rearrange("(p c) n -> p c n", c=DC)
            wo2 = w_out_o[0].rearrange("(h c p) n -> h p c n", h=RH, c=4)

            def load_odd(i, j):
                kind, hp = ODD_ORDER[j]
                s = odd_parts(j)[1]
                h = i * 2 + hp
                if kind == "qk":
                    for m in range(2):
                        sp.dma_start(wide(s)[:, :, m * RQK:(m + 1) * RQK],
                                     wi[:, :, bass.ds(h * RQK + m * RH * RQK, RQK)]).then_inc(odd_here[s], 16)
                elif kind == "wo":
                    sp.dma_start(tall(s), wo2[bass.ds(h, 1)].rearrange("e p c n -> p (e c) n")).then_inc(odd_here[s], 16)
                else:
                    first = 2 * RH * RQK + (RH * RV if kind == "g" else 0)
                    sp.dma_start(wide(s), wi[:, :, bass.ds(h * RV + first, RV)]).then_inc(odd_here[s], 16)

            for j in range(4):
                sp.wait_ge(moe_used[0], n0 * (GROUPS * BODY_UNITS) + (j + 1))
                load_odd(0, j)
            for j in range(4, RING):
                sp.wait_ge(odd_used, 2 + j - 3)
                load_odd(0, j)
            for j in range(RING):
                sp.wait_ge(odd_used, 2 + RING + j - 3)
                load_odd(1, j)
                if j == 0:
                    sp.wait_ge(moe_used[0], n0 * (GROUPS * BODY_UNITS) + RING)
                    for idx in range(2):
                        load_expert_part(1, 0, idx)
            for idx in range(2, RING):
                sp.wait_ge(odd_used, 2 + (11 + idx if idx < 6 else ODD_UNITS))
                load_expert_part(1, 0, idx)
            rest_of_experts(1)

            out_v = out.rearrange("b (c p) d -> p (b c) d", p=P)
            for c in range(TC):
                sp.wait_ge(dve_s, V.at(f"fin:xn{c}"))
                sp.dma_start(out_v[:, c, :], x[:, c, :]).then_inc(stored, 16)
            sp.wait_ge(stored, 32)

        @block.gpsimd
        def _(pool):
            def bcast(ap, n):
                return ap.broadcast_to([P, n])

            pool.dma_start(lnqkv[:, 0:Q_LORA], bcast(ln_q_e[0:1, :], Q_LORA)).then_inc(small_in, 16)
            pool.dma_start(lnqkv[:, Q_LORA:], bcast(ln_kv_e[0:1, :], KV_LORA)).then_inc(small_in, 16)
            pool.dma_start(bf, bcast(b_f_e[0:1, :], HEADS)).then_inc(small_in, 16)
            pool.dma_start(gain[:, 1, :], bcast(ln_ffn[0:1, :], D)).then_inc(gain_in[1], 16)
            stage_g = ring[:, 0, DC * ZC:DC * (ZC + 2 * GROUPS)].rearrange("p (l n) -> p l n", l=2)
            stage_e = ring[:, 0, DC * (ZC + 2 * GROUPS):DC * (ZC + 2 * NR)].rearrange("p (l n) -> p l n", l=2)
            pool.dma_start(br[:, 0, 0:GROUPS], bcast(b_rg[0:1, :], GROUPS)).then_inc(small_in, 16)
            pool.dma_start(br[:, 1, 0:GROUPS], bcast(b_rg[1:2, :], GROUPS)).then_inc(small_in, 16)
            pool.dma_start(br[:, 0, GROUPS:], bcast(b_re[0:1, :], EXPERTS)).then_inc(small_in, 16)
            pool.dma_start(br[:, 1, GROUPS:], bcast(b_re[1:2, :], EXPERTS)).then_inc(small_in, 16)
            nc.gpsimd.memset(warm, 1.0)
            nc.gpsimd.memset(ones, 1.0).then_inc(ready, 1)
            for l in range(2):
                pool.dma_start(stage_g[:, l, :], w_rg[l].rearrange("(p c) n -> p (c n)", c=DC)).then_inc(router_in, 16)
                pool.dma_start(stage_e[:, l, :], w_re[l].rearrange("(p c) n -> p (c n)", c=DC)).then_inc(router_in, 16)
            pool.wait_ge(router_in, 64)
            for l in range(2):
                nc.gpsimd.tensor_copy(wr[:, l, :, 0:GROUPS], stage_g[:, l, :].rearrange("p (c n) -> p c n", c=DC)
                                      ).then_inc(ready, 1)
                nc.gpsimd.tensor_copy(wr[:, l, :, GROUPS:], stage_e[:, l, :].rearrange("p (c n) -> p c n", c=DC)
                                      ).then_inc(ready, 1)
            pool.wait_ge(dve_s, V.at("mix0:xn1"))
            pool.dma_start(gain[:, 0, :], bcast(ln_mix_o[0:1, :], D)).then_inc(gain_in[0], 16)
            for a in range(16):
                pool.wait_ge(act_s, A.at(f"e{a}"))
                pool.wait_ge(dve_s, V.at(f"r{a}"))
                for c, lo, n in SEG:
                    last = nc.gpsimd.tensor_scalar(prob[:, a % DEEP, lo:lo + n], prob[:, a % DEEP, lo:lo + n],
                                                   rsm[:, a % DEEP, c:c + 1], None, ALU.mult)
                last.then_inc(pool_s, G.done(f"n{a}"))
            pool.wait_ge(dve_s, V.at("ffn0:xn1"))
            pool.dma_start(gain[:, 1, :], bcast(ln_ffn[1:2, :], D)).then_inc(gain_in[1], 16)
            pool.wait_ge(dve_s, V.at("mix1:x1"))
            pool.dma_start(odd, consts_odd).then_inc(odd_in, 16)
            pool.wait_ge(dve_s, V.at("mix1:xn1"))
            pool.dma_start(gain[:, 0, :], bcast(ln_f[None, :], D)).then_inc(gain_in[0], 16)

        @block.tensor
        def _(pe):
            ident = C("ident")

            def transposed_norm(e):
                for c in range(TC):
                    pe.wait_ge(dve_s, V.at(f"{e}:xn{c}"))
                    for half in range(2):
                        for i in range(4):
                            last = nc.tensor.transpose(wk[2 * c + half][:, i * P:(i + 1) * P],
                                                       xn[:, c, 4 * half + i, :], ident)
                        last.then_inc(pe_s, PE.done(f"{e}:xT{2 * c + half}"))

            def project(dst, lhs, rhs, n=DC, first=True, last_one=True):
                for k in range(n):
                    last = nc.tensor.matmul(dst, lhs(k), rhs(k), start=(k == 0 and first), stop=(k == n - 1 and last_one))
                return last

            def tok(c):
                return slice(c * P, (c + 1) * P)

            def split_project(dst, stat, mov, halves=None, n=DC, first=True, last_one=True):
                for k in range(n):
                    if halves and k % (n // 2) == 0:
                        halves(k // (n // 2))
                    sh, sl = stat(k)
                    mh, ml = mov(k)
                    nc.tensor.matmul(dst, sh, mh, start=(k == 0 and first), stop=False, skip_group_check=True)
                    nc.tensor.matmul(dst, sh, ml, start=False, stop=False, skip_group_check=True)
                    last = nc.tensor.matmul(dst, sl, mh, start=False, stop=(k == n - 1 and last_one),
                                            skip_group_check=True)
                return last

            def x_tok(c):
                return lambda k: (xh[:, k, tok(c)], xl[:, c, k, :])

            def x_all(k):
                return xh[:, k, :].rearrange("p (c t) -> p c t", c=TC), xl[:, :, k, :]

            def normed(e, c):
                pe.wait_ge(act_s, A.at(f"{e}:xT{2 * c}"))
                pe.wait_ge(dve_s, V.at(f"{e}:xT{2 * c + 1}"))

            pe.wait_ge(const_in, 16)
            transposed_norm("mix0")
            pe.wait_ge(even_here[0], 32)
            for c in range(TC):
                normed("mix0", c)
                project(wk[c][:, 0:ZC], lambda k: xnT[:, k, tok(c)], lambda k: z_w[:, k, :]
                        ).then_inc(pe_s, PE.done(f"Z{c}"))
            pe.wait_ge(pe_s, PE.at("Z1"))
            pe.sem_inc(even_used, 1)
            for u, name in ((1, "QF"), (2, "KF")):
                pe.wait_ge(even_here[u], 16)
                for b in range(2):
                    bank = wk[(2 if name == "QF" else 0) + b]
                    if name == "KF":
                        pe.wait_ge(act_s, A.at(f"Z{b}"))
                    for i in range(2):
                        m = 2 * b + i
                        last = project(bank[:, i * SEQ:(i + 1) * SEQ], lambda k: wide(u)[:, k, m * P:(m + 1) * P],
                                       lambda k: xnT[:, k, :])
                    last.then_inc(pe_s, PE.done(f"{name}{b}"))
                pe.wait_ge(pe_s, PE.at(f"{name}1"))
                pe.sem_inc(even_used, 1)
            pe.wait_ge(even_here[3], 16)
            for c in range(TC):
                pe.wait_ge(act_s, A.at(f"QF{c}"))
                project(wk[2 + c][:, :], lambda k: xnT[:, k, tok(c)], lambda k: wide(3)[:, k, :]
                        ).then_inc(pe_s, PE.done(f"VF{c}"))
            pe.wait_ge(pe_s, PE.at("VF1"))
            pe.sem_inc(even_used, 1)
            pe.wait_ge(dve_s, V.at("logf"))
            pe.wait_ge(dve_s, V.at("KF0"))
            pe.wait_ge(ready, 1)
            nc.tensor.matmul(wk[0][:, 0:8], C("tri"), logf[:, 0, :], start=True, stop=True)
            nc.tensor.matmul(wk[0][:, 8:16], C("tri"), logf[:, 1, :], start=True, stop=False)
            nc.tensor.matmul(wk[0][:, 8:16], ones, logf[:, 0, :], start=False, stop=True).then_inc(pe_s, PE.done("CU"))
            pe.wait_ge(dve_s, V.at("CU"))
            for c in range(TC):
                last = nc.tensor.matmul(wk[1][0:8, tok(c)], cum[:, c, :], ident, start=True, stop=True)
            last.then_inc(pe_s, PE.done("CT"))
            for k in range(2):
                for c in range(TC):
                    last = nc.tensor.transpose(wk[0][:, k * SEQ + c * P:k * SEQ + (c + 1) * P],
                                               zc[:, c, k * P:(k + 1) * P], ident)
            last.then_inc(pe_s, PE.done("CQ"))
            pe.wait_ge(act_s, A.at("VF0"))
            for c in range(TC):
                nc.tensor.transpose(wk[2][:, tok(c)], zc[:, c, Q_LORA:Q_LORA + KV_LORA], ident)
            for c in range(TC):
                last = nc.tensor.matmul(wk[2][64:96, SEQ + c * P:SEQ + (c + 1) * P], zc[:, c, FQ - ROPE:FQ], ident,
                                        start=True, stop=True)
            last.then_inc(pe_s, PE.done("CK"))
            pe.wait_ge(even_here[4], 32)
            pe.wait_ge(act_s, A.at("CQ"))
            pe.wait_ge(dve_s, V.at("VF1"))
            banks = {"QA0": 3, "QB0": 0, "QA1": 1, "QB1": 3}
            for c in range(TC):
                for i, name in enumerate(("QA", "QB")):
                    if (c, i) == (1, 1):
                        pe.wait_ge(act_s, A.at("QA0"))
                    b = wk[banks[f"{name}{c}"]]
                    project(b[:, 0:384], lambda k: cqT[:, k, tok(c)], lambda k: uq_w[:, k, i * 384:(i + 1) * 384], n=2
                            ).then_inc(pe_s, PE.done(f"{name}{c}"))
            pe.wait_ge(dve_s, V.at("CK"))
            pe.wait_ge(act_s, A.at("kpe"))
            kn_bank = (2, 0, 1, 3)
            kn_free = (None, "QB0", "QA1", "QB1")
            for m in range(4):
                if kn_free[m]:
                    pe.wait_ge(act_s, A.at(kn_free[m]))
                for i in range(2):
                    h = 2 * m + i
                    last = nc.tensor.matmul(wk[kn_bank[m]][0:64, i * SEQ:(i + 1) * SEQ],
                                            ukv_w[:, h * 128:h * 128 + NOPE], ckvT, start=True, stop=True)
                last.then_inc(pe_s, PE.done(f"KN{m}"))
            uv = ukv_w.rearrange("p (h d) -> p h d", h=HEADS)[:, :, NOPE:]
            for c in range(TC):
                pe.wait_ge(act_s, A.at("KN0")) if c == 0 else pe.wait_ge(dve_s, V.at("KN1"))
                nc.tensor.matmul(wk[2 if c == 0 else 0][:, :], ckvT[:, tok(c)], uv, start=True, stop=True
                                 ).then_inc(pe_s, PE.done(f"VM{c}"))
            pe.wait_ge(pe_s, PE.at("VM1"))
            pe.wait_ge(dve_s, V.at("rope1"))
            pe.sem_inc(even_used, 1)
            qt_bank = (1, 3, 2, 0)
            for m in range(4):
                if m == 0:
                    pe.wait_ge(act_s, A.at("KN2"))
                elif m == 1:
                    pe.wait_ge(dve_s, V.at("KN3"))
                elif m == 2:
                    pe.wait_ge(act_s, A.at("VM0"))
                else:
                    pe.wait_ge(dve_s, V.at("VM1"))
                for i in range(2):
                    h = 2 * m + i
                    for c in range(TC):
                        last = nc.tensor.transpose(wk[qt_bank[m]][0:QK, i * SEQ + c * P:i * SEQ + (c + 1) * P],
                                                   q_tok[:, c, h * QK:(h + 1) * QK], ident)
                last.then_inc(pe_s, PE.done(f"QT{m}"))

            pe.wait_ge(act_s, A.at("QT2"))
            pe.wait_ge(dve_s, V.at("QT3"))
            pe.wait_ge(act_s, A.at("CT"))
            s_bank, t_bank, o_bank = (wk[0], wk[1], acc[2], acc[3]), (wk[2], acc[0]), (wk[3], acc[1])

            def scores(a):
                b = s_bank[a % DEEP]
                if a >= DEEP:
                    pe.wait_ge(dve_s, V.at(f"s{a - DEEP}"))
                for c, lo, n in SEG:
                    if a < 8:
                        last = nc.tensor.matmul(b[:, lo:lo + n], q96T[0:QK, a, tok(c)], k96T[0:QK, a, 0:n],
                                                start=True, stop=True)
                    else:
                        h = a - 8
                        r = 64 * (h % 2)
                        nc.tensor.matmul(b[:, lo:lo + n], qfT[r:r + 64, h // 2, tok(c)], kfT[r:r + 64, h // 2, 0:n],
                                         start=True, stop=False)
                        last = nc.tensor.matmul(b[:, lo:lo + n], C("ident", 8)[:, h:h + 1].broadcast_to([8, P]),
                                                ncT[0:8, 0:n], start=False, stop=True)
                last.then_inc(pe_s, PE.done(f"S{a}"))

            def weigh(a):
                ob = o_bank[a // 2 % 2]
                pe.wait_ge(act_s, A.at(f"p{a}"))
                if a % 2 == 0 and a >= 4:
                    pe.wait_ge(dve_s, V.at(f"o{a // 2 - 2}"))
                h = a % 8
                v = vm if a < 8 else vf
                r = 64 * (a % 2)
                nc.tensor.matmul(ob[r:r + 64, 0:SEQ], v[:, 0, h * 64:(h + 1) * 64], probT[:, a % 2, 0:256],
                                 start=True, stop=False)
                nc.tensor.matmul(ob[r:r + 64, P:SEQ], v[:, 1, h * 64:(h + 1) * 64], probT[:, a % 2, 256:384],
                                 start=False, stop=True).then_inc(pe_s, PE.done(f"O{a}"))

            for a in range(3):
                scores(a)
            for a in range(16):
                tb = t_bank[a % 2]
                pe.wait_ge(pool_s, G.at(f"n{a}"))
                if a >= 2:
                    pe.wait_ge(act_s, A.at(f"p{a - 2}"))
                for k in range(3):
                    last = nc.tensor.transpose(tb[:, k * P:(k + 1) * P], prob[:, a % DEEP, k * P:(k + 1) * P], ident)
                last.then_inc(pe_s, PE.done(f"T{a}"))
                if a < 13:
                    scores(a + 3)
                if a:
                    weigh(a - 1)
            weigh(15)

            def seed_wide():
                for c in range(TC):
                    for hf in range(2):
                        nc.tensor.matmul(acc[2 * c + hf][:, :], ident, x[:, c, hf * 512:(hf + 1) * 512],
                                         start=True, stop=False, skip_group_check=True)

            pe.wait_ge(act_s, A.at("p15"))
            pe.wait_ge(dve_s, V.at("o7"))
            seed_wide()
            for u in range(2):
                pe.wait_ge(even_here[5 + u], 16)
                for c in range(TC):
                    for hf in range(2):
                        for k in range(4):
                            last = nc.tensor.matmul(acc[2 * c + hf][:, :], oT[:, 4 * u + k, tok(c)],
                                                    tall(5 + u)[:, k, hf * 512:(hf + 1) * 512],
                                                    start=False, stop=(u == 1 and k == 3), skip_group_check=True)
                    if u == 1:
                        last.then_inc(pe_s, PE.done(f"OUT0:{c}"))
                if u == 0:
                    last.then_inc(even_used, 1)
            pe.wait_ge(pe_s, PE.at("OUT0:1"))
            pe.sem_inc(even_used, 1)

            def experts(l):
                m = M[l]
                e_ = f"ffn{l}"
                transposed_norm(e_)
                pe.wait_ge(ready, 5)
                for c in range(TC):
                    normed(e_, c)
                    last = project(wk[0][:, c * 64:c * 64 + NR], lambda k: xnT[:, k, tok(c)], lambda k: wr[:, l, k, :])
                last.then_inc(pe_s, PE.done(f"lg{l}"))
                seed_wide()
                pe.wait_ge(dve_s, V.at(f"asg{l}"))
                a_ = [asg[:, c, :, :].rearrange("p g j -> p (g j)") for c in range(TC)]
                nc.tensor.matmul(wk[1][:, 0:32], C("tri"), a_[0], start=True, stop=True)
                nc.tensor.matmul(wk[1][:, 32:64], C("tri"), a_[1], start=True, stop=False)
                nc.tensor.matmul(wk[1][:, 32:64], ones, a_[0], start=False, stop=True)
                nc.tensor.matmul(wk[1][:, 64:96], ones, a_[0], start=True, stop=False)
                nc.tensor.matmul(wk[1][:, 64:96], ones, a_[1], start=False, stop=True).then_inc(pe_s, PE.done(f"rk{l}"))
                for n in ("hidT_ready", "y_ready", "combined"):
                    pe.sem_inc(m[n], 1)
                pe.wait_ge(rounds_set[l], 1)
                nr = pe.value_load(rounds[0:1, l:l + 1], min_val=1, max_val=ROUNDS)
                with pe.Fori(0, nr) as r:
                    with pe.Fori(0, GROUPS) as i:
                        it = r * GROUPS + i

                        def here(idx):
                            pe.wait_ge(moe_here[l][moe_slot(l, idx)], it * 48 + 16 * (idx // RING + 1))

                        def combine(quad):
                            pe.wait_ge(m["y_copied"], (it * PER + 4 * quad) * 2 + 9)
                            pe.wait_ge(m["g_copied"], it * 2 + (quad + 2))
                            for c in range(TC):
                                for hf in range(2):
                                    last = nc.tensor.matmul(acc[2 * c + hf][:, :], gT[:, tok(c)],
                                                            ye[:, hf * 512:(hf + 1) * 512],
                                                            start=False, stop=False, skip_group_check=True)
                                last.then_inc(m["combined0" if c == 0 else "combined"], 1)

                        pe.wait_ge(m["sel_ready"], it + 1)
                        for e in range(PER):
                            n_ = it * PER + e
                            quad = e // 4
                            if e % 4 == 0:
                                pe.wait_ge(m["g_copied"], it * 2 + (quad + 1))
                                for half in range(2):
                                    b = wk[2 - half]
                                    for k in range(4):
                                        for c in range(TC):
                                            last = nc.tensor.matmul(
                                                b[:, k * P:(k + 1) * P], xn[:, c, 4 * half + k, :],
                                                sel[:, c, 4 * quad:4 * quad + 4, :].rearrange("p e s -> p (e s)"),
                                                start=(c == 0), stop=(c == TC - 1))
                                    last.then_inc(m["gath_ready"], 1)
                                pe.wait_ge(m["xg_copied"], it * 4 + (2 * quad + 2))
                            xe = xg[:, quad, :, (e % 4) * SLOTS:(e % 4 + 1) * SLOTS]

                            def up_or_gate(part):
                                here(3 * e + part)
                                w_ = wide(moe_slot(l, 3 * e + part))
                                for k in range(DC):
                                    for j in range(4):
                                        last = nc.tensor.matmul(wk[0][32 * j:32 * j + 32, part * P:(part + 1) * P],
                                                                xe[:, k, :], w_[:, k, j * P:(j + 1) * P],
                                                                start=(k == 0), stop=(k == DC - 1))
                                return last

                            up_or_gate(0).then_inc(moe_used[l], 1)
                            if e % 4 == 0:
                                for c in range(TC):
                                    last = nc.tensor.matmul(
                                        wk[1][:, tok(c)], gsel[:, c, e:e + 4, :].rearrange("p e s -> p (e s)"),
                                        ident, start=True, stop=True)
                                last.then_inc(m["g_ready"], 1)
                            up_or_gate(1).then_inc(m["gu_ready"], 1)
                            if e == 4:
                                combine(0)
                            pe.wait_ge(m["hid_done"], n_ + 2)
                            pe.sem_inc(moe_used[l], 1)
                            nc.tensor.transpose(wk[2][:, 0:P], hid, ident).then_inc(m["hidT_ready"], 1)
                            here(3 * e + 2)
                            pe.wait_ge(m["hidT_copied"], n_ + 1)
                            pe.wait_ge(m["y_copied"], n_ * 2 + 1)
                            wd = tall(moe_slot(l, 3 * e + 2))
                            for k in range(4):
                                for j in range(4):
                                    last = nc.tensor.matmul(wk[3][32 * j:32 * j + 32, 0:256], hidT[:, k, :],
                                                            wd[:, k, j * 256:(j + 1) * 256],
                                                            start=(k == 0), stop=(k == 3))
                            last.then_inc(m["y_ready"], 1)
                            pe.wait_ge(m["y_ready"], n_ + 2)
                            pe.sem_inc(moe_used[l], 1)
                        combine(1)

            experts(0)

            transposed_norm("mix1")
            pe.wait_ge(dve_s, V.at("mix1:x1"))
            pe.wait_ge(act_s, A.at("mix1:sa1"))
            seed_wide()
            pe.wait_ge(dve_s, V.at("mix1:xl3"))
            pe.sem_inc(odd_used, 2)
            with pe.Fori(0, RH // 2) as i:
                def fill(name, hp):
                    b, k = odd_use(name, hp)
                    pe.wait_ge(odd_drained[b], i * 6 + (k + 1))
                    return wk[b], odd_filled[b]

                def parts(kind, hp):
                    j = ODD_ORDER.index((kind, hp))
                    hi, lo = (shaped(part[s_], UNIT, 4 if kind == "wo" else DC) for s_ in odd_parts(j))

                    def half(n):
                        pe.wait_ge(odd_low, i * 16 + (2 * j + n + 1))
                    return hi, lo, half

                def used(name, hp):
                    b, k = odd_use(name, hp)
                    pe.wait_ge(odd_filled[b], i * 6 + (k + 1))
                    pe.sem_inc(odd_used, 1)

                def qk(hp):
                    hi, lo, half = parts("qk", hp)
                    for j, name in enumerate("qk"):
                        b, f = fill(name, hp)
                        for m_ in range(2):
                            cols = slice(j * RQK + m_ * P, j * RQK + (m_ + 1) * P)
                            last = split_project(b[:, m_ * SEQ:(m_ + 1) * SEQ],
                                                 lambda k: (hi[:, k, cols], lo[:, k, cols]), x_all, half)
                        last.then_inc(f, 1)
                    used("k", hp)

                def token_major(kind, hp):
                    hi, lo, half = parts(kind, hp)
                    for c in range(TC):
                        b, f = fill(f"{kind}{c}", hp)
                        split_project(b[:, :], x_tok(c), lambda k: (hi[:, k, :], lo[:, k, :]), half).then_inc(f, 1)
                    used(f"{kind}1", hp)

                def ret_scores(hp):
                    pe.wait_ge(O["qT_done"], i * 2 + (hp + 1))
                    pe.wait_ge(O["kT_done"], i * 2 + (hp + 1))
                    for s in range(2):
                        b, f = fill(f"S{s}", hp)
                        for m_ in range(2):
                            last = nc.tensor.matmul(b[:, 0:SEQ - s * P], kT[:, m_, tok(s)], qT[:, m_, s * P:SEQ],
                                                    start=(m_ == 0), stop=(m_ == 1))
                        last.then_inc(f, 1)

                def ret_out(hp):
                    pe.wait_ge(O["sT_done"], i * 4 + (2 * hp + 2))
                    pe.wait_ge(O["v_done"], i * 4 + (2 * hp + 2))
                    b, f = fill("O0", hp)
                    nc.tensor.matmul(b[:, :], sT[:, 0:128], vr[:, 0, :], start=True, stop=True).then_inc(f, 1)
                    b, f = fill("O1", hp)
                    nc.tensor.matmul(b[:, :], sT[:, 128:256], vr[:, 0, :], start=True, stop=False)
                    nc.tensor.matmul(b[:, :], sT[:, 256:384], vr[:, 1, :], start=False, stop=True).then_inc(f, 1)

                def turn(hp):
                    for c in range(TC):
                        pe.wait_ge(O["y_done"], i * 4 + (2 * hp + c + 1))
                        b, f = fill(f"T{c}", hp)
                        for k in range(4):
                            last = nc.tensor.transpose(b[:, k * P:(k + 1) * P], yr[:, c, k * P:(k + 1) * P], ident)
                        last.then_inc(f, 1)

                def out_proj(hp):
                    hi, lo, half = parts("wo", hp)
                    for c in range(TC):
                        pe.wait_ge(O["yT_done"], i * 4 + (2 * hp + c + 1))
                        for hf in range(2):
                            cols = slice(hf * 512, (hf + 1) * 512)
                            last = split_project(acc[2 * c + hf][:, :], lambda k: (yh[:, c, k, :], yl[:, c, k, :]),
                                                 lambda k: (hi[:, k, cols], lo[:, k, cols]), half,
                                                 n=4, first=False, last_one=False)
                        last.then_inc(O[f"out{c}"], 1)
                    pe.wait_ge(O["out1"], i * 2 + (hp + 1))
                    pe.sem_inc(odd_used, 1)

                qk(0)
                token_major("v", 0)
                ret_scores(0)
                token_major("g", 0)
                ret_out(0)
                qk(1)
                turn(0)
                out_proj(0)
                token_major("v", 1)
                ret_scores(1)
                token_major("g", 1)
                ret_out(1)
                turn(1)
                out_proj(1)
            experts(1)

        @block.scalar
        def _(act):
            links = [0]

            def link(ins):
                links[0] += 1
                ins.then_inc(chain_a, 1)
                act.wait_ge(chain_a, links[0])

            warmed = [0]

            def preload(function):
                k = warmed[0]
                warmed[0] += 1
                nc.scalar.activation(warm[:, 1 + k:2 + k], warm[:, 0:1], function)

            def norm_stats(e, arrived):
                for c in range(TC):
                    arrived(c)

                    def squares(half, sums):
                        src = x[:, c, half * 512:(half + 1) * 512] if e == "mix0" else acc[2 * c + half][:, :]
                        return nc.scalar.activation(xn[:, c, 4 * half:4 * half + 4, :].rearrange("p a b -> p (a b)"),
                                                    src, ACT.Square, accum_out=sums[:, c:c + 1])

                    if e != "mix0":
                        squares(1, s2).then_inc(act_s, A.done(f"{e}:sb{c}"))
                    if e in SUMMED:
                        act.wait_ge(dve_s, V.at(f"{e}:xa{c}"))
                    squares(0, ss).then_inc(act_s, A.done(f"{e}:sa{c}"))
                    act.wait_ge(act_s, A.at(f"{e}:sa{c}"))
                    act.wait_ge(dve_s, V.at(f"{e}:b{c}"))
                    nc.scalar.activation(std[:, c:c + 1], ss[:, c:c + 1], ACT.Sqrt, scale=1.0 / D,
                                         bias=ms[:, c:c + 1]).then_inc(act_s, A.done(f"{e}:std{c}"))

            def drain_xT(e):
                for c in range(TC):
                    act.wait_ge(pe_s, PE.at(f"{e}:xT{2 * c}"))
                    nc.scalar.activation(xnT[:, 0:4, c * P:(c + 1) * P],
                                         wk[2 * c][:, :].rearrange("p (k t) -> p k t", k=4),
                                         ACT.Copy).then_inc(act_s, A.done(f"{e}:xT{2 * c}"))

            def high(u_slot, h_slot, n, first, done):
                for i in range(2):
                    if i == 0:
                        first()
                    cols = slice(i * n // 2, (i + 1) * n // 2)
                    nc.scalar.activation(part[h_slot][:, cols], ring[:, u_slot, cols], ACT.Copy).then_inc(done, 1)

            def high_xT(e):
                for b in range(4):
                    act.wait_ge(pe_s, PE.at(f"{e}:xT{b}"))
                    c, half = b // 2, b % 2
                    nc.scalar.activation(xh[:, 4 * half:4 * half + 4, c * P:(c + 1) * P],
                                         wk[b][:, :].rearrange("p (k t) -> p k t", k=4),
                                         ACT.Copy).then_inc(act_s, A.done(f"{e}:xh{b}"))

            act.wait_ge(ready, 1)
            preload(ACT.Sqrt)
            norm_stats("mix0", lambda c: act.wait_ge(x_in_sem[c], 16))
            drain_xT("mix0")
            for c in range(TC):
                act.wait_ge(pe_s, PE.at(f"Z{c}"))
                nc.scalar.activation(zc[:, c, :], wk[c][:, 0:ZC], ACT.Copy).then_inc(act_s, A.done(f"Z{c}"))
            act.wait_ge(act_s, A.at("Z1"))
            for c in range(TC):
                nc.scalar.activation(cqT[:, c, :], zc[:, c, 0:Q_LORA], ACT.Square, accum_out=s4[:, 2 * c:2 * c + 1])
                last = nc.scalar.activation(probT[:, c, 0:KV_LORA], zc[:, c, Q_LORA:Q_LORA + KV_LORA], ACT.Square,
                                            accum_out=s4[:, 2 * c + 1:2 * c + 2])
            last.then_inc(act_s, A.done("sq4"))
            half8 = FOX ** -0.5

            def drain_qf(b):
                act.wait_ge(pe_s, PE.at(f"QF{b}"))
                nc.scalar.activation(qfT[:, 2 * b:2 * b + 2, :], wk[2 + b][:, :].rearrange("p (c t) -> p c t", c=2),
                                     ACT.Copy, scale=half8).then_inc(act_s, A.done(f"QF{b}"))

            drain_qf(0)
            act.wait_ge(dve_s, V.at("zlog"))
            nc.scalar.activation(zabs, zlog, ACT.Abs).then_inc(act_s, A.done("zabs"))
            act.wait_ge(act_s, A.at("zabs"))
            nc.scalar.activation(zexp, zabs, ACT.Exp, scale=-1.0).then_inc(act_s, A.done("zexp"))
            act.wait_ge(act_s, A.at("zexp"))
            nc.scalar.activation(zabs, zexp, ACT.Ln, bias=ones[:, 0:1]).then_inc(act_s, A.done("zln"))
            act.wait_ge(dve_s, V.at("ms4"))
            nc.scalar.activation(r4, s4, ACT.Sqrt).then_inc(act_s, A.done("std4"))
            preload(ACT.Exp)
            drain_qf(1)
            act.wait_ge(pe_s, PE.at("VF0"))
            nc.scalar.activation(vf[:, 0, :], wk[2][:, :], ACT.Copy).then_inc(act_s, A.done("VF0"))
            act.wait_ge(pe_s, PE.at("CT"))
            nc.scalar.activation(ncT[0:8, :], wk[1][0:8, 0:SEQ], ACT.Copy, scale=-1.0).then_inc(act_s, A.done("CT"))
            act.wait_ge(pe_s, PE.at("CQ"))
            nc.scalar.activation(cqT, wk[0][:, :].rearrange("p (c t) -> p c t", c=2), ACT.Copy
                                 ).then_inc(act_s, A.done("CQ"))
            act.wait_ge(pe_s, PE.at("CK"))
            act.wait_ge(dve_s, V.at("CK"))
            nc.scalar.activation(k96T[64:96, :, :], wk[2][64:96, None, SEQ:2 * SEQ].broadcast_to([32, HEADS, SEQ]),
                                 ACT.Copy).then_inc(act_s, A.done("kpe"))
            banks = {"QA0": 3, "QB0": 0, "QA1": 1, "QB1": 3}
            for c in range(TC):
                for i, name in enumerate(("QA", "QB")):
                    act.wait_ge(pe_s, PE.at(f"{name}{c}"))
                    nc.scalar.activation(q_tok[:, c, i * 384:(i + 1) * 384], wk[banks[f"{name}{c}"]][:, 0:384], ACT.Copy,
                                         scale=QK ** -0.5).then_inc(act_s, A.done(f"{name}{c}"))
            for m_, b in ((0, 2), (2, 1)):
                act.wait_ge(pe_s, PE.at(f"KN{m_}"))
                nc.scalar.activation(k96T[0:64, 2 * m_:2 * m_ + 2, :], wk[b][0:64, :].rearrange("p (c t) -> p c t", c=2),
                                     ACT.Copy).then_inc(act_s, A.done(f"KN{m_}"))
            act.wait_ge(pe_s, PE.at("VM0"))
            nc.scalar.activation(vm[:, 0, :], wk[2][:, :], ACT.Copy).then_inc(act_s, A.done("VM0"))
            for m_, b in ((0, 1), (2, 2)):
                act.wait_ge(pe_s, PE.at(f"QT{m_}"))
                nc.scalar.activation(q96T[0:QK, 2 * m_:2 * m_ + 2, :], wk[b][0:QK, :].rearrange("p (c t) -> p c t", c=2),
                                     ACT.Copy).then_inc(act_s, A.done(f"QT{m_}"))

            def drain_probT(a):
                act.wait_ge(pe_s, PE.at(f"T{a}"))
                if a >= 2:
                    act.wait_ge(pe_s, PE.at(f"O{a - 2}"))
                nc.scalar.activation(probT[:, a % 2, :], (wk[2], acc[0])[a % 2][:, 0:384], ACT.Copy
                                     ).then_inc(act_s, A.done(f"p{a}"))

            for a in range(16):
                act.wait_ge(dve_s, V.at(f"m{a}"))
                for c, lo, n in SEG:
                    last = nc.scalar.activation(prob[:, a % DEEP, lo:lo + n], prob[:, a % DEEP, lo:lo + n], ACT.Exp,
                                                bias=nmx[:, a % DEEP, c:c + 1], accum_out=sm[:, a % DEEP, c:c + 1])
                last.then_inc(act_s, A.done(f"e{a}"))
                if a > 1:
                    drain_probT(a - 2)
            drain_probT(14)
            drain_probT(15)

            preload(ACT.Sqrt)
            def experts(l, arrived):
                m = M[l]
                norm_stats(f"ffn{l}", arrived)
                preload(ACT.Exp)
                drain_xT(f"ffn{l}")
                act.wait_ge(dve_s, V.at(f"gd{l}"))
                nc.scalar.activation(t4, t4, ACT.Exp).then_inc(act_s, A.done(f"ge{l}"))
                act.wait_ge(dve_s, V.at(f"ed{l}"))
                nc.scalar.activation(t8, t8, ACT.Exp)
                nc.scalar.activation(rt[:, 8:10], rt[:, 8:10], ACT.Exp).then_inc(act_s, A.done(f"ee{l}"))
                preload(ACT.Silu)
                act.wait_ge(rounds_set[l], 1)
                nr = act.value_load(rounds[0:1, l:l + 1], min_val=1, max_val=ROUNDS)
                with act.Fori(0, nr) as r:
                    with act.Fori(0, GROUPS) as i:
                        it = r * GROUPS + i
                        for e in range(PER):
                            n_ = it * PER + e
                            if e % 4 == 0:
                                act.wait_ge(m["gath_ready"], it * 4 + (e // 2 + 1))
                                nc.scalar.activation(xg[:, e // 4, 0:4, :],
                                                     wk[2][:, :].rearrange("p (c s) -> p c s", c=4), ACT.Copy
                                                     ).then_inc(m["xg_copied"], 1)
                            act.wait_ge(m["gu_ready"], n_ + 1)
                            act.wait_ge(m["hid_done"], n_ + 1)
                            nc.scalar.activation(act_g, wk[0][:, 0:P], ACT.Silu
                                                 ).then_inc(m["silu_done"], 1)
                            act.wait_ge(m["hidT_ready"], n_ + 2)
                            act.wait_ge(m["y_ready"], n_ + 1)
                            nc.scalar.activation(hidT.rearrange("p k s -> p (k s)"), wk[2][:, 0:P], ACT.Copy
                                                 ).then_inc(m["hidT_copied"], 1)
                            act.wait_ge(m["y_ready"], n_ + 2)
                            if e % 4 == 0:
                                act.wait_ge(m["combined"], it * 2 + (e // 4 + 1))
                            q = slice(32 * (e % 4), 32 * (e % 4) + 32)
                            for j in range(2):
                                last = nc.scalar.activation(ye[q, j * 256:(j + 1) * 256],
                                                            wk[3][32 * j:32 * j + 32, 0:256], ACT.Copy)
                            last.then_inc(m["y_copied"], 1)
                preload(ACT.Sqrt)
                return lambda c: act.wait_ge(m["combined0" if c == 0 else "combined"], nr * (GROUPS * 2) + c)

            summed = experts(0, lambda c: act.wait_ge(pe_s, PE.at(f"OUT0:{c}")))

            norm_stats("mix1", summed)
            preload(ACT.Silu)
            high_xT("mix1")
            for b in range(4):
                act.sem_inc(odd_drained[b], 1)
            with act.Fori(0, RH // 2) as i:
                def got(name, hp):
                    b, k = odd_use(name, hp)
                    act.wait_ge(odd_filled[b], i * 6 + (k + 1))
                    return wk[b], odd_drained[b]

                def values(hp):
                    for c in range(TC):
                        b, d = got(f"v{c}", hp)
                        ins = nc.scalar.activation(vr[:, c, :], b[:, :], ACT.Copy)
                        ins.then_inc(d, 1)
                    act.wait_ge(d, i * 6 + (odd_use("v1", hp)[1] + 2))
                    act.sem_inc(O["v_done"], 2)

                def gate(hp):
                    for c in range(TC):
                        b, d = got(f"g{c}", hp)
                        nc.scalar.activation(sg[:, c, :], b[:, :], ACT.Silu).then_inc(d, 1)
                    act.wait_ge(d, i * 6 + (odd_use("g1", hp)[1] + 2))
                    act.sem_inc(O["sg_done"], 2)

                def stats(hp):
                    for c in range(TC):
                        b, _ = got(f"O{c}", hp)
                        nc.scalar.activation(yr[:, c, :], b[:, :], ACT.Square, accum_out=ss[:, c:c + 1]
                                             ).then_inc(O["sq_done"], 1)
                    act.wait_ge(O["ms_done"], i * 2 + (hp + 1))
                    nc.scalar.activation(std, ms, ACT.Sqrt).then_inc(O["std_done"], 1)

                def high_T(hp):
                    for c in range(TC):
                        b, _ = got(f"T{c}", hp)
                        nc.scalar.activation(yh[:, c, :, :].rearrange("p k t -> p (k t)"), b[:, :], ACT.Copy
                                             ).then_inc(O["yh_done"], 1)

                def odd_high_of(j):
                    kind = ODD_ORDER[j][0]
                    h_slot, s_ = odd_parts(j)

                    def first():
                        per = 48 if j % 4 in (0, 3) else 32
                        act.wait_ge(odd_here[s_], i * per + (per if j >= 4 else (32 if kind == "qk" else 16)))
                        act.wait_ge(odd_used, i * RING + (j + 1))
                    high(s_, h_slot, UNIT, first, odd_high)

                odd_high_of(0)
                odd_high_of(1)
                odd_high_of(2)
                values(0)
                odd_high_of(3)
                gate(0)
                odd_high_of(4)
                stats(0)
                high_T(0)
                odd_high_of(5)
                odd_high_of(6)
                values(1)
                odd_high_of(7)
                gate(1)
                stats(1)
                high_T(1)
            preload(ACT.Sqrt)
            summed = experts(1, lambda c: act.wait_ge(O[f"out{c}"], RH))
            norm_stats("fin", summed)

        @block.vector
        def _(dve):
            links = [0]

            def link(ins):
                links[0] += 1
                ins.then_inc(chain_v, 1)
                dve.wait_ge(chain_v, links[0])

            tt, ts, stt = nc.vector.tensor_tensor, nc.vector.tensor_scalar, nc.vector.scalar_tensor_tensor

            def norm(e, arrived, slot, gain_loaded, loads=1):
                for c in range(TC):
                    arrived(c)
                    if e in SUMMED:
                        nc.vector.tensor_copy(x[:, c, 0:512], acc[2 * c][:, :]).then_inc(dve_s, V.done(f"{e}:xa{c}"))
                    if e == "mix0":
                        link(stt(xn[:, c, 4:8, :].rearrange("p a b -> p (a b)"), x[:, c, 512:], 1.0, x[:, c, 512:],
                                 ALU.mult, ALU.mult, accum_out=s2[:, c:c + 1]))
                    else:
                        dve.wait_ge(act_s, A.at(f"{e}:sb{c}"))
                    ts(ms[:, c:c + 1], s2[:, c:c + 1], 1.0 / D, EPS, ALU.mult, ALU.add
                       ).then_inc(dve_s, V.done(f"{e}:b{c}"))
                    if e in SUMMED:
                        nc.vector.tensor_copy(x[:, c, 512:], acc[2 * c + 1][:, :]).then_inc(dve_s, V.done(f"{e}:x{c}"))
                        dve.wait_ge(dve_s, V.at(f"{e}:x{c}"))
                    dve.wait_ge(act_s, A.at(f"{e}:std{c}"))
                    link(nc.vector.reciprocal(rstd[:, c:c + 1], std[:, c:c + 1]))
                    if c == 0:
                        dve.wait_ge(gain_loaded, 16 * loads)
                    if e == "fin":
                        for hf in range(2):
                            cols = slice(hf * 512, (hf + 1) * 512)
                            last = stt(x[:, c, cols], acc[2 * c + hf][:, :], rstd[:, c:c + 1], gain[:, slot, cols],
                                       ALU.mult, ALU.mult)
                        last.then_inc(dve_s, V.done(f"{e}:xn{c}"))
                    else:
                        stt(xn[:, c, :, :], x[:, c, :].rearrange("p (a b) -> p b a", b=DC), rstd[:, c:c + 1],
                            gain[:, slot, :].rearrange("p (a b) -> p b a", b=DC), ALU.mult, ALU.mult
                            ).then_inc(dve_s, V.done(f"{e}:xn{c}"))

            def drain_xT(e):
                for c in range(TC):
                    dve.wait_ge(pe_s, PE.at(f"{e}:xT{2 * c + 1}"))
                    nc.vector.tensor_copy(xnT[:, 4:8, c * P:(c + 1) * P],
                                          wk[2 * c + 1][:, :].rearrange("p (k t) -> p k t", k=4)
                                          ).then_inc(dve_s, V.done(f"{e}:xT{2 * c + 1}"))

            def drain(dst, name, src):
                dve.wait_ge(pe_s, PE.at(name))
                nc.vector.tensor_copy(dst, src).then_inc(dve_s, V.done(name))

            def low(u_slot, h_slot, n, highs, done):
                for i in range(2):
                    cols = slice(i * n // 2, (i + 1) * n // 2)
                    highs(i)
                    tt(part[u_slot][:, cols], ring[:, u_slot, cols], part[h_slot][:, cols].bitcast(F32), ALU.subtract
                       ).then_inc(done, 1)

            def low_xT(e):
                for b in range(4):
                    dve.wait_ge(act_s, A.at(f"{e}:xh{b}"))
                    c, half = b // 2, b % 2
                    if half == 0:
                        dve.wait_ge(pe_s, PE.at(f"{e}:xT{2 * c + 1}"))
                    tt(xl[:, c, 4 * half:4 * half + 4, :], wk[b][:, :].rearrange("p (k t) -> p k t", k=4),
                       xh[:, 4 * half:4 * half + 4, c * P:(c + 1) * P].bitcast(F32), ALU.subtract
                       ).then_inc(dve_s, V.done(f"{e}:xl{b}"))

            norm("mix0", lambda c: dve.wait_ge(x_in_sem[c], 16), 0, first_gain_in)
            drain_xT("mix0")
            dve.wait_ge(const_in, 16)
            dve.wait_ge(act_s, A.at("Z1"))
            dve.wait_ge(small_in, 16 * 7)
            tt(zlog, zc[:, :, FQ:ZC], bf[:, None, :].broadcast_to([P, TC, HEADS]), ALU.add).then_inc(dve_s, V.done("zlog"))
            dve.wait_ge(act_s, A.at("sq4"))
            lat = s4.rearrange("p (c k) -> p c k", c=TC)
            link(ts(lat[:, :, 0], lat[:, :, 0], 1.0 / Q_LORA, EPS, ALU.mult, ALU.add))
            ts(lat[:, :, 1], lat[:, :, 1], 1.0 / KV_LORA, EPS, ALU.mult, ALU.add).then_inc(dve_s, V.done("ms4"))
            two = lambda b: b[:, :].rearrange("p (c t) -> p c t", c=2)
            drain(kfT[:, 0:2, :], "KF0", two(wk[0]))
            drain(kfT[:, 2:4, :], "KF1", two(wk[1]))
            dve.wait_ge(act_s, A.at("zln"))
            stt(logf, zlog, 0.0, zabs, ALU.min, ALU.subtract).then_inc(dve_s, V.done("logf"))
            drain(vf[:, 1, :], "VF1", wk[3][:, :])
            dve.wait_ge(act_s, A.at("std4"))
            link(nc.vector.reciprocal(r4, r4))
            for c in range(TC):
                stt(zc[:, c, 0:Q_LORA], zc[:, c, 0:Q_LORA], r4[:, 2 * c:2 * c + 1], lnqkv[:, 0:Q_LORA], ALU.mult, ALU.mult)
                last = stt(zc[:, c, Q_LORA:Q_LORA + KV_LORA], zc[:, c, Q_LORA:Q_LORA + KV_LORA],
                           r4[:, 2 * c + 1:2 * c + 2], lnqkv[:, Q_LORA:], ALU.mult, ALU.mult)
            last.then_inc(dve_s, V.done("cqn"))

            def rope(parts, heads, cos, sin, name):
                a = ropek[:, 0:0 + heads * 32]
                bb = tmp_rope[:, 0:heads * 32]
                a4 = a.rearrange("p (h k f) -> p h k f", h=heads, k=2)
                b4 = bb.rearrange("p (h k f) -> p h k f", h=heads, k=2)
                tt(a4, parts, cos, ALU.mult)
                link(tt(b4, parts, sin, ALU.mult))
                tt(parts[:, :, 0, :], a4[:, :, 0, :], b4[:, :, 1, :], ALU.subtract)
                return tt(parts[:, :, 1, :], b4[:, :, 0, :], a4[:, :, 1, :], ALU.add)

            tmp_rope = probT.rearrange("p b n -> p (b n)")

            def phase(name, c=None, heads=HEADS):
                v = C(name).rearrange("p (c f) -> p c f", c=TC)
                if c is None:
                    return v[:, :, None, :].broadcast_to([P, TC, 2, 16])
                return v[:, c:c + 1, None, :].broadcast_to([P, heads, 2, 16])

            rope(zc[:, :, FQ - ROPE:FQ].rearrange("p c (k f) -> p c k f", k=2), TC, phase("cos"), phase("sin"), "kpe"
                 ).then_inc(dve_s, V.done("kpe"))
            dve.wait_ge(dve_s, V.at("kpe"))
            dve.wait_ge(pe_s, PE.at("CU"))
            nc.vector.tensor_copy(cum.rearrange("p c h -> p (c h)"), wk[0][:, 0:16]).then_inc(dve_s, V.done("CU"))
            drain(ckvT, "CK", wk[2][:, 0:SEQ])
            for c in range(TC):
                dve.wait_ge(act_s, A.at(f"QB{c}"))
                parts = q_tok[:, c, :].rearrange("p (h n) -> p h n", h=HEADS)[:, :, NOPE:].rearrange(
                    "p h (k f) -> p h k f", k=2)
                rope(parts, HEADS, phase("cos", c), phase("sin", c), f"rope{c}").then_inc(dve_s, V.done(f"rope{c}"))
                dve.wait_ge(dve_s, V.at(f"rope{c}"))
            drain(k96T[0:64, 2:4, :], "KN1", two(wk[0])[0:64])
            drain(k96T[0:64, 6:8, :], "KN3", two(wk[3])[0:64])
            drain(vm[:, 1, :], "VM1", wk[0][:, :])
            drain(q96T[0:QK, 2:4, :], "QT1", two(wk[3])[0:QK])
            drain(q96T[0:QK, 6:8, :], "QT3", two(wk[0])[0:QK])

            def drain_o(pair):
                dve.wait_ge(pe_s, PE.at(f"O{2 * pair + 1}"))
                nc.vector.tensor_copy(oT[:, pair, :], (wk[3], acc[1])[pair % 2][:, 0:SEQ]
                                      ).then_inc(dve_s, V.done(f"o{pair}"))

            def invert(a):
                dve.wait_ge(act_s, A.at(f"e{a}"))
                nc.vector.reciprocal(rsm[:, a % DEEP, :], sm[:, a % DEEP, :]).then_inc(dve_s, V.done(f"r{a}"))

            for a in range(16):
                dve.wait_ge(pe_s, PE.at(f"S{a}"))
                sc = (wk[0], wk[1], acc[2], acc[3])[a % DEEP]
                pr = prob[:, a % DEEP, :]
                if a >= DEEP:
                    dve.wait_ge(pe_s, PE.at(f"T{a - DEEP}"))
                if a < 8:
                    ins = tt(pr, sc[:, 0:384], C("mla"), ALU.add)
                else:
                    for c, lo, n in SEG:
                        ins = stt(pr[:, lo:lo + n], sc[:, lo:lo + n], cum[:, c, a - 8:a - 7],
                                  C("fox")[:, lo:lo + n], ALU.add, ALU.add)
                ins.then_inc(dve_s, V.done(f"s{a}"))
                dve.wait_ge(dve_s, V.at(f"s{a}"))
                for c, lo, n in SEG:
                    ins = nc.vector.reduce_max(mx[:, a % DEEP, c:c + 1], pr[:, lo:lo + n], AX.X)
                link(ins)
                ts(nmx[:, a % DEEP, :], mx[:, a % DEEP, :], -1.0, None, ALU.mult).then_inc(dve_s, V.done(f"m{a}"))
                if a:
                    invert(a - 1)
                if a % 2 == 0 and a > 2:
                    drain_o(a // 2 - 2)
            invert(15)
            drain_o(6)
            drain_o(7)

            def experts(l, arrived):
                m = M[l]
                norm(f"ffn{l}", arrived, 1, gain_in[1], l + 1)
                drain_xT(f"ffn{l}")
                dve.wait_ge(pe_s, PE.at(f"lg{l}"))
                logits = wk[0][:, 0:128].rearrange("p (c n) -> p c n", c=TC)[:, :, 0:NR]
                link(tt(lg, logits, br[:, l:l + 1, :].broadcast_to([P, TC, NR]), ALU.add))
                gl = lg[:, :, 0:GROUPS]
                gmax, pg, first, m1, p2, s8, pr1, pr2, den, ga, gb = (rt[:, 2 * k:2 * k + 2] for k in
                                                                     (0, 1, 2, 3, 4, 5, 6, 7, 8, 9, 10))
                m2, base, mc = rt[:, 22:24], rt[:, 24:26], rt[:, 26:27]

                def wide_of(s, n):
                    return s[:, :, None].broadcast_to([P, TC, n])

                def first_max(dst, vals, best, arg, n, t):
                    link(tt(t, vals, wide_of(best, n), ALU.is_equal))
                    ar = C(arg)[:, None, :].broadcast_to([P, TC, n])
                    link(tt(t, t, ar, ALU.mult))
                    link(nc.vector.tensor_reduce(first, t, AX.X, ALU.min))
                    link(tt(dst, ar, wide_of(first, n), ALU.is_equal))

                link(nc.vector.reduce_max(gmax, gl, AX.X))
                first_max(oh4, gl, gmax, "arg4", GROUPS, t4)
                tt(t4, gl, wide_of(gmax, GROUPS), ALU.subtract).then_inc(dve_s, V.done(f"gd{l}"))
                ea = lg[:, :, GROUPS:].rearrange("p c (g j) -> p c g j", g=GROUPS)
                link(tt(tmp, ea, oh4[:, :, :, None].broadcast_to([P, TC, GROUPS, PER]), ALU.mult))
                link(nc.vector.reduce_sum(el, tmp.rearrange("p c g j -> p c j g"), AX.X))
                link(nc.vector.reduce_max(m1, el, AX.X))
                first_max(oh8[:, 0], el, m1, "arg8", PER, t8)
                link(stt(el2, oh8[:, 0], -BIG, el, ALU.mult, ALU.add))
                link(nc.vector.reduce_max(m2, el2, AX.X))
                first_max(oh8[:, 1], el2, m2, "arg8", PER, t8)
                tt(t8, el, wide_of(m1, PER), ALU.subtract)
                tt(p2, m2, m1, ALU.subtract).then_inc(dve_s, V.done(f"ed{l}"))
                dve.wait_ge(act_s, A.at(f"ge{l}"))
                link(nc.vector.reduce_sum(pg, t4, AX.X))
                dve.wait_ge(act_s, A.at(f"ee{l}"))
                link(nc.vector.reduce_sum(s8, t8, AX.X))
                link(nc.vector.reciprocal(pg, pg))
                link(nc.vector.reciprocal(pr1, s8))
                link(tt(pr2, p2, pr1, ALU.mult))
                link(tt(den, pr1, pr2, ALU.add))
                link(nc.vector.reciprocal(den, den))
                link(tt(base, pg, den, ALU.mult))
                tt(ga, base, pr1, ALU.mult)
                link(tt(gb, base, pr2, ALU.mult))
                link(tt(t8, oh8[:, 0], oh8[:, 1], ALU.add))
                four = lambda v: v[:, :, None, :].broadcast_to([P, TC, GROUPS, PER])
                grp = oh4[:, :, :, None].broadcast_to([P, TC, GROUPS, PER])
                tt(asg, four(t8), grp, ALU.mult).then_inc(dve_s, V.done(f"asg{l}"))
                link(tt(el, oh8[:, 0], wide_of(ga, PER), ALU.mult))
                link(tt(el2, oh8[:, 1], wide_of(gb, PER), ALU.mult))
                link(tt(el, el, el2, ALU.add))
                link(tt(gates.rearrange("p c (g j) -> p c g j", g=GROUPS), four(el), grp, ALU.mult))
                dve.wait_ge(pe_s, PE.at(f"rk{l}"))
                rank = wk[1][:, 0:64].rearrange("p (c e) -> p c e", c=TC)
                link(tt(place, rank, asg.rearrange("p c g j -> p c (g j)"), ALU.mult))
                link(ts(place, place, 1.0, None, ALU.subtract))
                link(nc.vector.reduce_max(mc, wk[1][:, 64:96], AX.X))
                link(ts(rt[0:1, 28:28 + ROUNDS - 1], C("more", 1), mc[0:1, :], None, ALU.is_lt))
                link(nc.vector.reduce_sum(rt[0:1, 27:28], rt[0:1, 28:28 + ROUNDS - 1], AX.X))
                ts(rounds[0:1, l:l + 1], rt[0:1, 27:28], 1.0, None, ALU.add).then_inc(rounds_set[l], 1)
                dve.wait_ge(rounds_set[l], 1)
                for n in ("hid_done", "g_copied", "y_copied"):
                    dve.sem_inc(m[n], 1)
                nr = dve.value_load(rounds[0:1, l:l + 1], min_val=1, max_val=ROUNDS)
                with dve.Fori(0, nr) as r:
                    with dve.Fori(0, GROUPS) as i:
                        it = r * GROUPS + i
                        slots = C("iota")[:, None, :].broadcast_to([P, PER, SLOTS])
                        for c in range(TC):
                            pl = place[:, c, bass.ds(i * PER, PER)][:, :, None].broadcast_to([P, PER, SLOTS])
                            ins = tt(sel[:, c], pl, slots, ALU.is_equal)
                        ins.then_inc(m["gsel_masked"], 1)
                        dve.wait_ge(m["gsel_masked"], it + 1)
                        for c in range(TC):
                            gt = gates[:, c, bass.ds(i * PER, PER)][:, :, None].broadcast_to([P, PER, SLOTS])
                            ins = tt(gsel[:, c], sel[:, c], gt, ALU.mult)
                        ins.then_inc(m["sel_ready"], 1)
                        for e in range(PER):
                            n_ = it * PER + e
                            if e % 4 == 0:
                                dve.wait_ge(m["gath_ready"], it * 4 + (e // 2 + 2))
                                nc.vector.tensor_copy(xg[:, e // 4, 4:8, :],
                                                      wk[1][:, :].rearrange("p (c s) -> p c s", c=4)
                                                      ).then_inc(m["xg_copied"], 1)
                            dve.wait_ge(m["silu_done"], n_ + 1)
                            dve.wait_ge(m["hidT_ready"], n_ + 1)
                            tt(hid, wk[0][:, P:2 * P], act_g, ALU.mult).then_inc(m["hid_done"], 1)
                            if e % 4 == 0:
                                dve.wait_ge(m["g_ready"], it * 2 + (e // 4 + 1))
                                dve.wait_ge(m["combined"], it * 2 + (e // 4 + 1))
                                nc.vector.tensor_copy(gT, wk[1][:, 0:SEQ]).then_inc(m["g_copied"], 1)
                            dve.wait_ge(m["y_ready"], n_ + 2)
                            q = slice(32 * (e % 4), 32 * (e % 4) + 32)
                            for j in range(2, 4):
                                last = nc.vector.tensor_copy(ye[q, j * 256:(j + 1) * 256],
                                                             wk[3][32 * j:32 * j + 32, 0:256])
                            last.then_inc(m["y_copied"], 1)
                    ts(place, place, float(SLOTS), None, ALU.subtract).then_inc(m["place_moved"], 1)
                    dve.wait_ge(m["place_moved"], r + 1)
                return lambda c: dve.wait_ge(m["combined0" if c == 0 else "combined"], nr * (GROUPS * 2) + c)

            summed = experts(0, lambda c: dve.wait_ge(pe_s, PE.at(f"OUT0:{c}")))

            norm("mix1", summed, 0, gain_in[0])
            low_xT("mix1")
            dve.wait_ge(odd_in, 16)
            cosT = odd[:, 0:256][:, None, :].broadcast_to([P, 2, SEQ])
            sinT = odd[:, 256:512][:, None, :].broadcast_to([P, 2, SEQ])
            with dve.Fori(0, RH // 2) as i:
                def got(name, hp):
                    b, k = odd_use(name, hp)
                    dve.wait_ge(odd_filled[b], i * 6 + (k + 1))
                    return wk[b], odd_drained[b]

                def rotate(hp):
                    for j, (name, dst) in enumerate((("q", qT), ("k", kT))):
                        b, d = got(name, hp)
                        src = b[:, :].rearrange("p (m t) -> p m t", m=2)
                        tt(ra, src, cosT, ALU.mult).then_inc(O["ra_done"], 1)
                        tt(rb, src, sinT, ALU.mult).then_inc(d, 1)
                        k = odd_use(name, hp)[1]
                        dve.wait_ge(O["ra_done"], i * 4 + (2 * hp + j + 1))
                        dve.wait_ge(d, i * 6 + (k + 2))
                        tt(dst[:, 0, :], ra[:, 0, :], rb[:, 1, :], ALU.subtract)
                        tt(dst[:, 1, :], rb[:, 0, :], ra[:, 1, :], ALU.add).then_inc(O[f"{name}T_done"], 1)
                        dve.wait_ge(O[f"{name}T_done"], i * 2 + (hp + 1))

                def decay(hp):
                    dec = odd[:, bass.ds(i * 768 + (512 + 384 * hp), 384)]
                    for s in range(2):
                        b, d = got(f"S{s}", hp)
                        w_ = SEQ - s * P
                        tt(sT[:, s * SEQ:s * SEQ + w_], b[:, 0:w_], dec[:, s * SEQ:s * SEQ + w_], ALU.mult).then_inc(d, 1)
                        dve.wait_ge(d, i * 6 + (odd_use(f"S{s}", hp)[1] + 2))
                        dve.sem_inc(O["sT_done"], 1)

                def finish(hp):
                    dve.wait_ge(O["sq_done"], i * 4 + (2 * hp + 2))
                    ts(ms, ss, 1.0 / RV, EPS, ALU.mult, ALU.add).then_inc(O["ms_done"], 1)
                    dve.wait_ge(O["std_done"], i * 2 + (hp + 1))
                    nc.vector.reciprocal(rstd, std).then_inc(O["rs_done"], 1)
                    dve.wait_ge(O["rs_done"], i * 2 + (hp + 1))
                    dve.wait_ge(O["sg_done"], i * 4 + (2 * hp + 2))
                    for c in range(TC):
                        b, d = got(f"O{c}", hp)
                        stt(yr[:, c, :], b[:, :], rstd[:, c:c + 1], sg[:, c, :], ALU.mult, ALU.mult).then_inc(d, 1)
                        dve.wait_ge(d, i * 6 + (odd_use(f"O{c}", hp)[1] + 2))
                        dve.sem_inc(O["y_done"], 1)

                def low_T(hp):
                    for c in range(TC):
                        b, d = got(f"T{c}", hp)
                        dve.wait_ge(O["yh_done"], i * 4 + (2 * hp + c + 1))
                        tt(yl[:, c, :, :].rearrange("p k t -> p (k t)"), b[:, :],
                           yh[:, c, :, :].rearrange("p k t -> p (k t)").bitcast(F32), ALU.subtract).then_inc(d, 1)
                        dve.wait_ge(d, i * 6 + (odd_use(f"T{c}", hp)[1] + 2))
                        dve.sem_inc(O["yT_done"], 1)

                def odd_low_of(j):
                    h_slot, s_ = odd_parts(j)
                    low(s_, h_slot, UNIT, lambda n: dve.wait_ge(odd_high, i * 16 + (2 * j + n + 1)), odd_low)

                odd_low_of(0)
                odd_low_of(1)
                rotate(0)
                odd_low_of(2)
                decay(0)
                odd_low_of(3)
                odd_low_of(4)
                finish(0)
                low_T(0)
                rotate(1)
                odd_low_of(5)
                odd_low_of(6)
                decay(1)
                odd_low_of(7)
                finish(1)
                low_T(1)
            summed = experts(1, lambda c: dve.wait_ge(O[f"out{c}"], RH))
            norm("fin", summed, 0, gain_in[0], 2)


_INS = ['x', 'ln_mix_e', 'w_in_e', 'ln_q_e', 'w_uq_e', 'ln_kv_e', 'w_ukv_e', 'b_f_e', 'w_out_e', 'ln_mix_o', 'w_in_o',
        'w_out_o', 'ln_ffn', 'w_rg', 'b_rg', 'w_re', 'b_re', 'w_gate', 'w_up', 'w_down', 'ln_f']


def kernel(**inputs):
    import concourse.bacc as _bacc
    from concourse.bass_utils import run_bass_kernel_spmd as _run

    nc = _bacc.Bacc("TRN2", target_bir_lowering=False, num_devices=1)
    arrays, args = {}, []
    c, o = tables()
    for name, a in [(n, inputs[n]) for n in _INS] + [("consts", c), ("consts_odd", o)]:
        a = np.ascontiguousarray(a)
        arrays[f"in_{name}"] = a
        args.append(nc.dram_tensor(f"in_{name}", a.shape, mybir.dt.from_np(a.dtype), kind="ExternalInput").ap())
    args.append(nc.dram_tensor("out_0", (1, SEQ, D), F32, kind="ExternalOutput").ap())
    build(nc, *args)
    return _run(nc, [arrays], core_ids=[0]).results[0]["out_0"]
```

```python
import concourse.bass as bass
from concourse import mybir
from contextlib import ExitStack
import numpy as np

F32 = mybir.dt.float32
F32R = mybir.dt.float32r
I32 = mybir.dt.int32
ACT = mybir.ActivationFunctionType
ALU = mybir.AluOpType
AX = mybir.AxisListType

P = 128
SEQ = 256
TC = SEQ // P
D = 1024
DC = D // P
EPS = 1e-6
Q_LORA, KV_LORA, ROPE, NOPE, VD = 256, 128, 32, 64, 64
HEADS = 8
QK = NOPE + ROPE
FOX = 64
FQ = Q_LORA + KV_LORA + ROPE
FW = HEADS * FOX
ZC = FQ + HEADS
RH, RQK, RV = 4, 256, 512
GROUPS, PER, EXPERTS, DE = 4, 8, 32, 512
NR = GROUPS + EXPERTS
SLOTS = 32
ROUNDS = SEQ // SLOTS
RING = 8
UNIT = 4096
EVEN_UNITS, ODD_UNITS = 7, 16
BODY_UNITS = 3 * PER
DEEP = 4
BIG = 1e30
SEG = ((0, 0, 128), (1, 128, 256))

CONSTS = {}
_at = 0
for _n, _w in (("ident", 128), ("tri", 128), ("mla", 384), ("fox", 384), ("cos", 32), ("sin", 32),
               ("iota", 32), ("arg4", 4), ("arg8", 8), ("more", ROUNDS - 1), ("pick", 8)):
    CONSTS[_n] = (_at, _at + _w)
    _at += _w
NCONST = _at
NODD = 512 + RH * 384


class Steps:

    def __init__(self, names):
        self.names, self.next = list(names), 0

    def done(self, name):
        assert self.names[self.next] == name, (name, self.names[self.next])
        self.next += 1
        return 1

    def at(self, name):
        return self.names.index(name) + 1


def tables():
    c = np.zeros((P, NCONST), np.float32)

    def put(name, a):
        lo, hi = CONSTS[name]
        c[:, lo:hi] = a

    p = np.arange(P)
    put("ident", np.eye(P))
    put("tri", p[:, None] <= p[None, :])
    q0, k0 = p[:, None], p[None, :]
    q1, k1 = P + p[:, None], np.arange(SEQ)[None, :]
    put("mla", np.where(np.concatenate([k0 // 64 <= q0 // 64, k1 // 64 <= q1 // 64], 1), 0.0, -BIG))
    put("fox", np.where(np.concatenate([k0 <= q0, k1 <= q1], 1), 0.0, -BIG))
    pos = np.arange(SEQ, dtype=np.float32)

    def phase(half):
        inv = np.float32(10000.0) ** (-np.arange(half, dtype=np.float32) / np.float32(half))
        return pos[:, None] * inv[None, :]

    a16 = phase(ROPE // 2).reshape(TC, P, 16).transpose(1, 0, 2).reshape(P, 32)
    put("cos", np.cos(a16))
    put("sin", np.sin(a16))
    put("iota", 1 + np.arange(SLOTS)[None, :])
    put("arg4", np.arange(GROUPS)[None, :] - GROUPS)
    put("arg8", np.arange(PER)[None, :] - PER)
    put("pick", p[:, None] % 32 == np.arange(HEADS)[None, :])
    put("more", SLOTS * np.arange(1, ROUNDS)[None, :])
    o = np.zeros((P, NODD), np.float32)
    aT = phase(RQK // 2).T
    o[:, 0:256], o[:, 256:512] = np.cos(aT), np.sin(aT)
    for h in range(RH):
        g = np.log(1.0 - 2.0 ** (-5.0 - h))
        t, s = np.arange(SEQ)[None, :], np.arange(SEQ)[:, None]
        dec = np.where(t >= s, np.exp(np.maximum(t - s, 0) * g), 0.0) * RQK ** -0.5
        o[:, 512 + 384 * h:512 + 384 * h + 256] = dec[0:128]
        o[:, 512 + 384 * h + 256:512 + 384 * (h + 1)] = dec[128:256, 128:256]
    return c, o


def build(nc, x_in, ln_mix_e, w_in_e, ln_q_e, w_uq_e, ln_kv_e, w_ukv_e, b_f_e, w_out_e,
          ln_mix_o, w_in_o, w_out_o, ln_ffn, w_rg, b_rg, w_re, b_re, w_gate, w_up, w_down,
          ln_f, consts, consts_odd, out):
    ctx = ExitStack()
    with ctx:
        def sb(name, shape, dt=F32):
            return ctx.enter_context(nc.sbuf_tensor(name, shape, dt))

        def sem(name):
            return ctx.enter_context(nc.semaphore(name))

        base = (nc.sbuf_base + 31) // 32 * 32
        ring = sb("ring", [P, RING, UNIT])
        x = sb("x", [P, TC, D])
        xn = sb("xn", [P, TC, DC, P])
        xnT = sb("xnT", [P, DC, SEQ])
        gain = sb("gain", [P, 2, D])
        arena = sb("arena", [P, 9984])
        const = sb("const", [P, NCONST])
        pick = sb("pick", [P, HEADS], F32R)
        small = sb("small", [P, 976])
        rounds = sb("rounds", [1, 2], I32)

        def C(name, rows=P):
            return const[0:rows, CONSTS[name][0]:CONSTS[name][1]]

        class Cut:
            def __init__(self, base):
                self.base, self.used = base, 0

            def __call__(self, n, pattern=None, **dims):
                a = self.base[:, self.used:self.used + n]
                self.used += n
                assert self.used <= self.base.shape[1], self.used
                return a.rearrange(pattern, **dims) if pattern else a

        def over(name, shape, floats):
            return nc.alloc_sbuf_tensor_at(name, shape, F32R, offset=base + 4 * floats)

        AT_FORGET = 2 * TC * 512 + 2 * HEADS * SEQ + 2 * 4 * SEQ
        AT_X = RING * UNIT
        AT_XN, AT_XNT, AT_ARENA = AT_X + TC * D, AT_X + 2 * TC * D, AT_X + 3 * TC * D + 2 * D
        part = [over(f"slot{s}_parts", [P, UNIT], s * UNIT) for s in range(RING)]
        exh = over("even_x_high", [P, DC, SEQ], 5 * UNIT)
        exl = over("even_x_low", [P, DC, SEQ], 5 * UNIT + DC * SEQ)
        oh = over("o_high", [P, DC, SEQ], AT_XNT)
        ol = over("o_low", [P, DC, SEQ], 4 * UNIT)
        xh = over("x_high", [P, DC, SEQ], AT_XNT)
        xl = over("x_low", [P, TC, DC, P], AT_XN)
        nc_parts = over("forget_parts", [P, SEQ], AT_ARENA + AT_FORGET)
        yh = over("y_high", [P, TC, 4, P], AT_ARENA)
        yl = over("y_low", [P, TC, 4, P], AT_ARENA + TC * RV)

        cut = Cut(small)
        wr = cut(2 * DC * NR, "p (l c n) -> p l c n", l=2, c=DC)
        br = cut(2 * NR, "p (l n) -> p l n", l=2)
        ones = cut(1)
        all_ones = ones.broadcast_to([P, P])
        bf = cut(HEADS)
        ss = cut(2)
        s2 = cut(2)
        ms = cut(2)
        warm = cut(12)
        std = cut(2)
        rstd = cut(2)
        s4 = cut(4)
        r4 = cut(4)
        zlog = cut(16, "p (c h) -> p c h", c=TC)
        zabs = cut(16, "p (c h) -> p c h", c=TC)
        zexp = cut(16, "p (c h) -> p c h", c=TC)
        logf = cut(16, "p (c h) -> p c h", c=TC)
        cum = cut(16, "p (c h) -> p c h", c=TC)
        mx = cut(2 * DEEP, "p (b c) -> p b c", b=DEEP)
        nmx = cut(2 * DEEP, "p (b c) -> p b c", b=DEEP)
        sm = cut(2 * DEEP, "p (b c) -> p b c", b=DEEP)
        rsm = cut(2 * DEEP, "p (b c) -> p b c", b=DEEP)
        lg = cut(2 * NR, "p (c n) -> p c n", c=TC)
        oh4 = cut(8, "p (c n) -> p c n", c=TC)
        t4 = cut(8, "p (c n) -> p c n", c=TC)
        oh8 = cut(32, "p (k c n) -> p k c n", k=2, c=TC)
        t8 = cut(16, "p (c n) -> p c n", c=TC)
        el, el2, ge1, ge2 = zabs, zexp, zlog, cum
        rt = cut(36)
        gmax, first, m1, m2, p2, sg4, sg8, pr1, pr2, den, p1, ga, gb = (rt[:, 2 * k:2 * k + 2] for k in range(13))
        mc, more = rt[:, 26:27], rt[0:1, 27:28]

        cut = Cut(arena)
        spare = Cut(ring[:, 4, 2 * HEADS * QK + 1024:])
        zc = spare(TC * ZC, "p (c n) -> p c n", c=TC)
        lnqkv = spare(Q_LORA + KV_LORA)
        ropek = spare(256)
        vm = cut(TC * 512, "p (c n) -> p c n", c=TC)
        vf = cut(TC * 512, "p (c n) -> p c n", c=TC)
        q96T = cut(HEADS * SEQ, "p (h t) -> p h t", h=HEADS)
        k96T = cut(HEADS * SEQ, "p (h t) -> p h t", h=HEADS)
        qfT = cut(4 * SEQ, "p (h t) -> p h t", h=4)
        kfT = cut(4 * SEQ, "p (h t) -> p h t", h=4)
        assert cut.used == AT_FORGET
        cut(SEQ)
        shared = cut(768)
        cqT = shared[:, 0:512].rearrange("p (k t) -> p k t", k=2)
        ckvT = shared[:, 512:768]
        probT = cut(2 * 384, "p (b n) -> p b n", b=2)
        q_tok = xn[:, :, :, :].rearrange("p c a b -> p c (a b)")[:, :, 0:HEADS * QK]
        prob = xn[:, :, :, :].rearrange("p c a b -> p (c a b)")[:, 0:DEEP * 384].rearrange(
            "p (b n) -> p b n", b=DEEP)

        cut = Cut(arena)
        cut(2 * TC * RV)
        qT = cut(512, "p (m t) -> p m t", m=2)
        kT = cut(512, "p (m t) -> p m t", m=2)
        ra = cut(512, "p (m t) -> p m t", m=2)
        rb = cut(512, "p (m t) -> p m t", m=2)
        vr = cut(TC * RV, "p (c n) -> p c n", c=TC)
        sg = cut(TC * RV, "p (c n) -> p c n", c=TC)
        yr = cut(TC * RV, "p (c n) -> p c n", c=TC)
        sT = cut(384)
        assert cut.used <= 7680
        cut(7680 - cut.used)
        odd = cut(NODD)

        cut = Cut(arena)
        asg = cut(TC * EXPERTS, "p (c g j) -> p c g j", c=TC, g=GROUPS)
        gates = cut(TC * EXPERTS, "p (c e) -> p c e", c=TC)
        place = cut(TC * EXPERTS, "p (c e) -> p c e", c=TC)
        tmp = cut(TC * EXPERTS, "p (c g j) -> p c g j", c=TC, g=GROUPS)
        sel = cut(TC * PER * SLOTS, "p (c e s) -> p c e s", c=TC, e=PER)
        gsel = cut(TC * PER * SLOTS, "p (c e s) -> p c e s", c=TC, e=PER)
        xg = cut(2 * DC * 4 * SLOTS, "p (b c s) -> p b c s", b=2, c=DC)
        act_g = cut(P)
        hid = cut(P)
        hidT = cut(P, "p (k s) -> p k s", k=4)
        ye = cut(D)
        gT = cut(SEQ)

        assert cut.used <= 7680

        acc = [ctx.enter_context(nc.psum_tensor(f"acc{i}", [P, 512], F32)) for i in range(4)]
        wk = [ctx.enter_context(nc.psum_tensor(f"wk{i}", [P, 512], F32)) for i in range(4)]

        x_in_sem = [sem(f"x_chunk{c}_loaded") for c in range(TC)]
        const_in = sem("consts_loaded")
        first_gain_in = sem("first_gain_loaded")
        gain_in = [sem(f"gain{b}_loaded") for b in range(2)]
        odd_in = sem("odd_consts_loaded")
        small_in = sem("small_loaded")
        router_in = sem("router_loaded")
        ready = sem("ones_and_router_ready")
        even_here = [sem(f"even_unit{s}_loaded") for s in range(EVEN_UNITS)]
        moe_here = [[sem(f"moe{l}_slot{s}_loaded") for s in range(RING)] for l in range(2)]
        odd_here = [sem(f"odd_slot{s}_loaded") for s in range(RING)]
        even_used = sem("even_units_used")
        moe_used = [sem(f"moe{l}_units_used") for l in range(2)]
        odd_used = sem("odd_units_used")
        even_high, even_low = sem("even_high_parts"), sem("even_low_parts")
        odd_high, odd_low = sem("odd_high_parts"), sem("odd_low_parts")
        pe_s = sem("pe_steps")
        act_s = sem("act_steps")
        dve_s = sem("dve_steps")
        pool_s = sem("pool_steps")
        chain_v = sem("dve_chain")
        chain_a = sem("act_chain")
        chain_p = sem("pool_chain")
        rounds_set = [sem(f"rounds{l}_set") for l in range(2)]
        stored = sem("out_stored")

        def moe_sems(l):
            names = ("sel_ready", "gath_ready", "xg_copied0", "xg_copied1", "gu_ready", "silu_done", "hid_done",
                     "hidT_ready", "hidT_copied", "y_ready", "y_copied", "g_ready", "g_copied", "combined0",
                     "combined", "place_moved", "gsel_ready")
            return {n: sem(f"m{l}_{n}") for n in names}

        M = [moe_sems(0), moe_sems(1)]
        odd_filled = [sem(f"odd_bank{b}_filled") for b in range(4)]
        odd_drained = [sem(f"odd_bank{b}_drained") for b in range(4)]
        O = {n: sem(f"o_{n}") for n in ("qT_done", "kT_done", "v_done", "sT_done", "sg_done", "y_done", "yT_done",
                                        "sq_done", "std_done",
                                        "ms_done", "rs_done", "ra_done", "yh_done", "out0", "out1")}

        SUMMED = ("ffn0", "mix1", "ffn1")

        def norm_steps(e):
            chunks = range(TC)
            act = sum([([f"{e}:sb{c}"] if e != "mix0" else []) + [f"{e}:sa{c}", f"{e}:std{c}"] for c in chunks], [])
            copy = lambda name: [f"{e}:{name}"] if e in SUMMED else []
            dve = sum([copy(f"xa{c}") + [f"{e}:b{c}"] + copy(f"x{c}") + [f"{e}:xn{c}"] for c in chunks], [])
            if e == "fin":
                return {"act": act, "dve": dve}
            if e == "mix1":
                drains = [[f"{e}:x{k}{b}" for b in range(4)] for k in "hl"]
            else:
                drains = [[f"{e}:xT{b}" for b in range(k, 4, 2)] for k in range(2)]
            return {"act": act + drains[0], "dve": dve + drains[1], "pe": [f"{e}:xT{i}" for i in range(4)]}

        N = {e: norm_steps(e) for e in ("mix0", "ffn0", "mix1", "ffn1", "fin")}
        att_pe = ["S0", "S1", "S2"]
        for a in range(16):
            att_pe += [f"T{a}"] + ([f"S{a + 3}"] if a < 13 else []) + ([f"O{a - 1}"] if a else [])
        att_pe += ["O15"]
        router_pe = lambda l: [f"lg{l}", f"rk{l}"]
        PE = Steps(N["mix0"]["pe"] + ["Z0", "Z1", "QF0", "QF1", "KF0", "KF1", "VF0", "VF1", "CU", "CT", "CQ", "CK",
                                      "QA0", "QB0", "QA1", "QB1", "KN0", "KN1", "KN2", "KN3", "VM0", "VM1",
                                      "QT0", "QT1", "QT2", "QT3"] + att_pe + ["OUT0:0", "OUT0:1"]
                   + N["ffn0"]["pe"] + router_pe(0) + N["mix1"]["pe"] + N["ffn1"]["pe"] + router_pe(1))
        att_act = []
        for a in range(16):
            att_act += [f"e{a}"] + ([f"p{a - 2}"] if a > 1 else [])
        att_act += ["p14", "p15"]
        router_act = lambda l: [f"ge{l}", f"ee{l}"]
        A = Steps(N["mix0"]["act"] + ["exh0", "exh1", "Z0", "Z1", "sq4", "QF0", "zabs", "zexp", "zln", "std4", "QF1", "VF0", "CT", "CQ", "kpe",
                                      "QA0", "QB0", "QA1", "QB1", "KN0", "KN2", "VM0", "QT0", "QT2"]
                  + att_act + N["ffn0"]["act"] + router_act(0) + N["mix1"]["act"] + N["ffn1"]["act"] + router_act(1)
                  + N["fin"]["act"])
        att_dve = []
        for a in range(16):
            att_dve += [f"s{a}", f"m{a}"] + ([f"r{a - 1}"] if a else []) + ([f"oh{a // 2 - 2}", f"o{a // 2 - 2}"] if a % 2 == 0 and a > 2 else [])
        att_dve += ["r15", "oh6", "o6", "oh7", "o7"]
        V = Steps(N["mix0"]["dve"] + ["exl0", "exl1", "zlog", "ms4", "KF0", "KF1", "logf", "VF1", "cqn", "kpe", "CU", "CTl", "CK",
                                      "rope0", "rope1", "KN1", "KN3", "VM1", "QT1", "QT3"] + att_dve
                  + N["ffn0"]["dve"] + ["gd0", "ed0", "asg0", "den0"] + N["mix1"]["dve"]
                  + N["ffn1"]["dve"] + ["gd1", "ed1", "asg1", "den1"] + N["fin"]["dve"])
        G = Steps([f"n{a}" for a in range(16)] + ["gates0", "gates1"])

        def wide(s):
            return ring[:, s, :].rearrange("p (c n) -> p c n", c=DC)

        def tall(s):
            return ring[:, s, :].rearrange("p (c n) -> p c n", c=4)

        z_w = ring[:, 0, 0:DC * ZC].rearrange("p (c n) -> p c n", c=DC)

        EVEN_SPLIT = (1, 2, 3, 5, 6)
        EVEN_SLOT = (0, 1, 2, 3, 4, 5, 0)

        def even_parts(u):
            return 6 + EVEN_SPLIT.index(u) % 2, EVEN_SLOT[u]

        def split_before(u):
            return 2 * EVEN_SPLIT.index(u) if u < 5 else 6 + 4 * (u - 5)

        def odd_parts(j):
            return 5 + j % 2, 1 + j % 4

        def shaped(t, n, c):
            return t[:, 0:n].rearrange("p (c n) -> p c n", c=c)

        uq_w = ring[:, 4, 0:2 * HEADS * QK].rearrange("p (c n) -> p c n", c=2)
        ukv_w = ring[:, 4, 2 * HEADS * QK:2 * HEADS * QK + 1024]

        def moe_slot(l, idx):
            return ((1, 7)[l] + idx) % RING

        ODD_ORDER = (("qk", 0), ("v", 0), ("g", 0), ("qk", 1), ("wo", 0), ("v", 1), ("g", 1), ("wo", 1))
        ODD_USES = [(n, h) for h, n in (
            (0, "q"), (0, "k"), (0, "v0"), (0, "v1"), (0, "S0"), (0, "S1"), (0, "g0"), (0, "O0"), (0, "O1"), (0, "g1"),
            (1, "q"), (1, "k"), (0, "T0"), (0, "T1"),
            (1, "v0"), (1, "v1"), (1, "S0"), (1, "S1"), (1, "g0"), (1, "O0"), (1, "O1"), (1, "g1"), (1, "T0"), (1, "T1"))]

        def odd_use(name, hp):
            u = ODD_USES.index((name, hp))
            return u % 4, u // 4

        def wide_of(s, n):
            return s[:, :, None].broadcast_to([P, TC, n])

        def four(v):
            return v[:, :, None, :].broadcast_to([P, TC, GROUPS, PER])

        def group_of(v):
            return v[:, :, :, None].broadcast_to([P, TC, GROUPS, PER])

        def turned(a):
            return (wk[2], acc[0] if a < 12 else wk[0])[a % 2]

        def weighed(pair):
            return (wk[3], acc[1] if pair < 7 else wk[1])[pair % 2]

        block = ctx.enter_context(nc.Block())

        @block.sync
        def _(sp):
            x_v = x_in.rearrange("b (c p) d -> p (b c) d", p=P)
            for c in range(TC):
                sp.dma_start(x[:, c, :], x_v[:, c, :]).then_inc(x_in_sem[c], 16)
            sp.dma_start(gain[:, 0, :], ln_mix_e[0:1, :].broadcast_to([P, D])).then_inc(first_gain_in, 16)
            sp.dma_start(const[:, :], consts).then_inc(const_in, 16)
            w = w_in_e[0].rearrange("(p c) n -> p c n", c=DC)
            sp.dma_start(z_w[:, :, 0:FQ], w[:, :, 0:FQ]).then_inc(even_here[0], 16)
            sp.dma_start(z_w[:, :, FQ:ZC], w[:, :, FQ + 3 * FW:]).then_inc(even_here[0], 16)
            for u in range(3):
                sp.dma_start(wide(1 + u), w[:, :, FQ + u * FW:FQ + (u + 1) * FW]).then_inc(even_here[1 + u], 16)
            sp.dma_start(uq_w, w_uq_e[0].rearrange("(c p) n -> p c n", p=P)).then_inc(even_here[4], 16)
            sp.dma_start(ukv_w, w_ukv_e[0]).then_inc(even_here[4], 16)
            wo = w_out_e[0].rearrange("(u c p) n -> u p c n", u=2, c=4)
            sp.wait_ge(even_used, 1)
            sp.wait_ge(ready, 5)
            sp.dma_start(tall(EVEN_SLOT[6]), wo[1]).then_inc(even_here[6], 16)

            gate_v = w_gate.rearrange("l e (p c) n -> (l e) p (c n)", c=DC)
            up_v = w_up.rearrange("l e (p c) n -> (l e) p (c n)", c=DC)
            down_v = w_down.rearrange("l e (c p) n -> (l e) p c n", c=4)

            def load_expert_part(l, group, idx):
                e = group * PER + (l * EXPERTS + idx // 3)
                s = moe_slot(l, idx)
                if idx % 3 == 2:
                    sp.dma_start(tall(s), down_v[bass.ds(e, 1)].rearrange("e p c n -> p (e c) n")
                                 ).then_inc(moe_here[l][s], 16)
                else:
                    v = (gate_v, up_v)[idx % 3]
                    sp.dma_start(ring[:, s, :], v[bass.ds(e, 1)].rearrange("e p n -> p (e n)")
                                 ).then_inc(moe_here[l][s], 16)

            def rest_of_experts(l):
                sp.sem_inc(moe_used[l], RING)
                with sp.Fori(0, GROUPS - 1) as i:
                    for idx in range(RING, BODY_UNITS):
                        sp.wait_ge(moe_used[l], i * BODY_UNITS + (idx + 1))
                        load_expert_part(l, i, idx)
                    for idx in range(RING):
                        sp.wait_ge(moe_used[l], i * BODY_UNITS + (BODY_UNITS + idx + 1))
                        load_expert_part(l, i + 1, idx)
                for idx in range(RING, BODY_UNITS):
                    sp.wait_ge(moe_used[l], (GROUPS - 1) * BODY_UNITS + idx + 1)
                    load_expert_part(l, GROUPS - 1, idx)
                sp.wait_ge(rounds_set[l], 1)
                n = sp.value_load(rounds[0:1, l:l + 1], min_val=1, max_val=ROUNDS)
                with sp.If(n > 1):
                    with sp.Fori(1, n) as r:
                        with sp.Fori(0, GROUPS) as i:
                            for idx in range(BODY_UNITS):
                                sp.wait_ge(moe_used[l], r * (GROUPS * BODY_UNITS) + i * BODY_UNITS + (idx + 1))
                                load_expert_part(l, i, idx)
                return n

            for idx in range(RING):
                sp.wait_ge(even_used, idx + 2 if idx < 3 else EVEN_UNITS)
                load_expert_part(0, 0, idx)
                if idx == 2:
                    sp.dma_start(tall(EVEN_SLOT[5]), wo[0]).then_inc(even_here[5], 16)
            n0 = rest_of_experts(0)

            wi = w_in_o[0].rearrange("(p c) n -> p c n", c=DC)
            wo2 = w_out_o[0].rearrange("(h c p) n -> h p c n", h=RH, c=4)

            def load_odd(i, j):
                kind, hp = ODD_ORDER[j]
                s = odd_parts(j)[1]
                h = i * 2 + hp
                if kind == "qk":
                    for m in range(2):
                        sp.dma_start(wide(s)[:, :, m * RQK:(m + 1) * RQK],
                                     wi[:, :, bass.ds(h * RQK + m * RH * RQK, RQK)]).then_inc(odd_here[s], 16)
                elif kind == "wo":
                    sp.dma_start(tall(s), wo2[bass.ds(h, 1)].rearrange("e p c n -> p (e c) n")).then_inc(odd_here[s], 16)
                else:
                    first = 2 * RH * RQK + (RH * RV if kind == "g" else 0)
                    sp.dma_start(wide(s), wi[:, :, bass.ds(h * RV + first, RV)]).then_inc(odd_here[s], 16)

            for j in range(4):
                sp.wait_ge(moe_used[0], n0 * (GROUPS * BODY_UNITS) + (j + 1))
                load_odd(0, j)
            for j in range(4, RING):
                sp.wait_ge(odd_used, 2 + j - 3)
                load_odd(0, j)
            for j in range(RING):
                sp.wait_ge(odd_used, 2 + RING + j - 3)
                load_odd(1, j)
                if j == 0:
                    sp.wait_ge(moe_used[0], n0 * (GROUPS * BODY_UNITS) + RING)
                    for idx in range(2):
                        load_expert_part(1, 0, idx)
            for idx in range(2, RING):
                sp.wait_ge(odd_used, 2 + (11 + idx if idx < 6 else ODD_UNITS))
                load_expert_part(1, 0, idx)
            rest_of_experts(1)

            out_v = out.rearrange("b (c p) d -> p (b c) d", p=P)
            for c in range(TC):
                sp.wait_ge(dve_s, V.at(f"fin:xn{c}"))
                sp.dma_start(out_v[:, c, :], x[:, c, :]).then_inc(stored, 16)
            sp.wait_ge(stored, 32)

        @block.gpsimd
        def _(pool):
            def bcast(ap, n):
                return ap.broadcast_to([P, n])

            pool.dma_start(lnqkv[:, 0:Q_LORA], bcast(ln_q_e[0:1, :], Q_LORA)).then_inc(small_in, 16)
            pool.dma_start(lnqkv[:, Q_LORA:], bcast(ln_kv_e[0:1, :], KV_LORA)).then_inc(small_in, 16)
            pool.dma_start(bf, bcast(b_f_e[0:1, :], HEADS)).then_inc(small_in, 16)
            pool.dma_start(gain[:, 1, :], bcast(ln_ffn[0:1, :], D)).then_inc(gain_in[1], 16)
            stage_g = ring[:, 0, DC * ZC:DC * (ZC + 2 * GROUPS)].rearrange("p (l n) -> p l n", l=2)
            stage_e = ring[:, 0, DC * (ZC + 2 * GROUPS):DC * (ZC + 2 * NR)].rearrange("p (l n) -> p l n", l=2)
            pool.dma_start(br[:, 0, 0:GROUPS], bcast(b_rg[0:1, :], GROUPS)).then_inc(small_in, 16)
            pool.dma_start(br[:, 1, 0:GROUPS], bcast(b_rg[1:2, :], GROUPS)).then_inc(small_in, 16)
            pool.dma_start(br[:, 0, GROUPS:], bcast(b_re[0:1, :], EXPERTS)).then_inc(small_in, 16)
            pool.dma_start(br[:, 1, GROUPS:], bcast(b_re[1:2, :], EXPERTS)).then_inc(small_in, 16)
            nc.gpsimd.memset(warm, 1.0)
            nc.gpsimd.memset(ones, 1.0).then_inc(ready, 1)
            for l in range(2):
                pool.dma_start(stage_g[:, l, :], w_rg[l].rearrange("(p c) n -> p (c n)", c=DC)).then_inc(router_in, 16)
                pool.dma_start(stage_e[:, l, :], w_re[l].rearrange("(p c) n -> p (c n)", c=DC)).then_inc(router_in, 16)
            pool.wait_ge(router_in, 64)
            for l in range(2):
                nc.gpsimd.tensor_copy(wr[:, l, :, 0:GROUPS], stage_g[:, l, :].rearrange("p (c n) -> p c n", c=DC)
                                      ).then_inc(ready, 1)
                nc.gpsimd.tensor_copy(wr[:, l, :, GROUPS:], stage_e[:, l, :].rearrange("p (c n) -> p c n", c=DC)
                                      ).then_inc(ready, 1)
            pool.wait_ge(dve_s, V.at("mix0:xn1"))
            pool.dma_start(gain[:, 0, :], bcast(ln_mix_o[0:1, :], D)).then_inc(gain_in[0], 16)
            for a in range(16):
                pool.wait_ge(act_s, A.at(f"e{a}"))
                pool.wait_ge(dve_s, V.at(f"r{a}"))
                for c, lo, n in SEG:
                    last = nc.gpsimd.tensor_scalar(prob[:, a % DEEP, lo:lo + n], prob[:, a % DEEP, lo:lo + n],
                                                   rsm[:, a % DEEP, c:c + 1], None, ALU.mult)
                last.then_inc(pool_s, G.done(f"n{a}"))
            links = [0]

            def link(ins):
                links[0] += 1
                ins.then_inc(chain_p, 1)
                pool.wait_ge(chain_p, links[0])

            def gating(l):
                tt = nc.gpsimd.tensor_tensor
                pool.wait_ge(dve_s, V.at(f"den{l}"))
                tt(ga, p1, pr1, ALU.mult)
                link(tt(gb, p1, pr2, ALU.mult))
                tt(ga, ga, den, ALU.mult)
                link(tt(gb, gb, den, ALU.mult))
                tt(ge1, oh8[:, 0], wide_of(ga, PER), ALU.mult)
                link(tt(ge2, oh8[:, 1], wide_of(gb, PER), ALU.mult))
                link(tt(ge1, ge1, ge2, ALU.add))
                tt(gates.rearrange("p c (g j) -> p c g j", g=GROUPS), four(ge1), group_of(oh4), ALU.mult
                   ).then_inc(pool_s, G.done(f"gates{l}"))

            pool.wait_ge(dve_s, V.at("ffn0:xn1"))
            pool.dma_start(gain[:, 1, :], bcast(ln_ffn[1:2, :], D)).then_inc(gain_in[1], 16)
            pool.dma_start(odd, consts_odd).then_inc(odd_in, 16)
            gating(0)
            pool.wait_ge(dve_s, V.at("mix1:xn1"))
            pool.dma_start(gain[:, 0, :], bcast(ln_f[None, :], D)).then_inc(gain_in[0], 16)
            gating(1)

        @block.tensor
        def _(pe):
            ident = C("ident")

            def transposed_norm(e):
                for c in range(TC):
                    pe.wait_ge(dve_s, V.at(f"{e}:xn{c}"))
                    for half in range(2):
                        for i in range(4):
                            last = nc.tensor.transpose(wk[2 * c + half][:, i * P:(i + 1) * P],
                                                       xn[:, c, 4 * half + i, :], ident)
                        last.then_inc(pe_s, PE.done(f"{e}:xT{2 * c + half}"))

            def project(dst, lhs, rhs, n=DC, first=True, last_one=True):
                for k in range(n):
                    last = nc.tensor.matmul(dst, lhs(k), rhs(k), start=(k == 0 and first), stop=(k == n - 1 and last_one))
                return last

            def tok(c):
                return slice(c * P, (c + 1) * P)

            def split_project(dst, stat, mov, split=None, pieces=2, n=DC, first=True, last_one=True):
                for k in range(n):
                    if split and k % (n // pieces) == 0:
                        split(k // (n // pieces))
                    sh, sl = stat(k)
                    mh, ml = mov(k)
                    nc.tensor.matmul(dst, sh, mh, start=(k == 0 and first), stop=False, skip_group_check=True)
                    nc.tensor.matmul(dst, sh, ml, start=False, stop=False, skip_group_check=True)
                    last = nc.tensor.matmul(dst, sl, mh, start=False, stop=(k == n - 1 and last_one),
                                            skip_group_check=True)
                return last

            def x_tok(c):
                return lambda k: (xh[:, k, tok(c)], xl[:, c, k, :])

            def x_all(k):
                return xh[:, k, :].rearrange("p (c t) -> p c t", c=TC), xl[:, :, k, :]

            def normed(e, c):
                pe.wait_ge(act_s, A.at(f"{e}:xT{2 * c}"))
                pe.wait_ge(dve_s, V.at(f"{e}:xT{2 * c + 1}"))

            def ex_tok(c):
                return lambda k: (exh[:, k, tok(c)], exl[:, k, tok(c)])

            def ex_all(k):
                return exh[:, k, :], exl[:, k, :]

            def even_half(u):
                def half(i):
                    pe.wait_ge(even_low, split_before(u) + i + 1)
                return half

            pe.wait_ge(const_in, 16)
            transposed_norm("mix0")
            pe.wait_ge(even_here[0], 32)
            for c in range(TC):
                normed("mix0", c)
                project(wk[c][:, 0:ZC], lambda k: xnT[:, k, tok(c)], lambda k: z_w[:, k, :]
                        ).then_inc(pe_s, PE.done(f"Z{c}"))
            pe.wait_ge(pe_s, PE.at("Z1"))
            pe.sem_inc(even_used, 1)
            pe.wait_ge(dve_s, V.at("exl1"))
            for u, name in ((1, "QF"), (2, "KF")):
                hi, lo = (shaped(part[s_], UNIT, DC) for s_ in even_parts(u))
                for b in range(2):
                    bank = wk[(2 if name == "QF" else 0) + b]
                    if name == "KF":
                        pe.wait_ge(act_s, A.at(f"Z{b}"))
                    for i in range(2):
                        m = 2 * b + i
                        last = split_project(bank[:, i * SEQ:(i + 1) * SEQ],
                                             lambda k: (hi[:, k, m * P:(m + 1) * P], lo[:, k, m * P:(m + 1) * P]),
                                             ex_all, even_half(u))
                    last.then_inc(pe_s, PE.done(f"{name}{b}"))
                pe.wait_ge(pe_s, PE.at(f"{name}1"))
                pe.sem_inc(even_used, 1)
            hi, lo = (shaped(part[s_], UNIT, DC) for s_ in even_parts(3))
            for c in range(TC):
                pe.wait_ge(act_s, A.at(f"QF{c}"))
                split_project(wk[2 + c][:, :], ex_tok(c), lambda k: (hi[:, k, :], lo[:, k, :]), even_half(3)
                              ).then_inc(pe_s, PE.done(f"VF{c}"))
            pe.wait_ge(pe_s, PE.at("VF1"))
            pe.sem_inc(even_used, 1)
            pe.wait_ge(dve_s, V.at("logf"))
            pe.wait_ge(dve_s, V.at("KF0"))
            pe.wait_ge(ready, 1)
            nc.tensor.matmul(wk[0][:, 0:8], C("tri"), logf[:, 0, :], start=True, stop=True)
            nc.tensor.matmul(wk[0][:, 8:16], C("tri"), logf[:, 1, :], start=True, stop=False)
            nc.tensor.matmul(wk[0][:, 8:16], all_ones, logf[:, 0, :], start=False, stop=True).then_inc(pe_s, PE.done("CU"))
            pe.wait_ge(dve_s, V.at("CU"))
            for c in range(TC):
                last = nc.tensor.matmul(wk[1][0:8, tok(c)], cum[:, c, :], ident, start=True, stop=True)
            last.then_inc(pe_s, PE.done("CT"))
            for k in range(2):
                for c in range(TC):
                    last = nc.tensor.transpose(wk[0][:, k * SEQ + c * P:k * SEQ + (c + 1) * P],
                                               zc[:, c, k * P:(k + 1) * P], ident)
            last.then_inc(pe_s, PE.done("CQ"))
            pe.wait_ge(act_s, A.at("VF0"))
            for c in range(TC):
                nc.tensor.transpose(wk[2][:, tok(c)], zc[:, c, Q_LORA:Q_LORA + KV_LORA], ident)
            for c in range(TC):
                last = nc.tensor.matmul(wk[2][64:96, SEQ + c * P:SEQ + (c + 1) * P], zc[:, c, FQ - ROPE:FQ], ident,
                                        start=True, stop=True)
            last.then_inc(pe_s, PE.done("CK"))
            pe.wait_ge(even_here[4], 32)
            pe.wait_ge(act_s, A.at("CQ"))
            pe.wait_ge(dve_s, V.at("VF1"))
            banks = {"QA0": 3, "QB0": 0, "QA1": 1, "QB1": 3}
            for c in range(TC):
                for i, name in enumerate(("QA", "QB")):
                    if (c, i) == (1, 1):
                        pe.wait_ge(act_s, A.at("QA0"))
                    if (c, i) == (1, 0):
                        pe.wait_ge(dve_s, V.at("CTl"))
                    b = wk[banks[f"{name}{c}"]]
                    project(b[:, 0:384], lambda k: cqT[:, k, tok(c)], lambda k: uq_w[:, k, i * 384:(i + 1) * 384], n=2
                            ).then_inc(pe_s, PE.done(f"{name}{c}"))
            pe.wait_ge(dve_s, V.at("CK"))
            pe.wait_ge(act_s, A.at("kpe"))
            kn_bank = (2, 0, 1, 3)
            kn_free = (None, "QB0", "QA1", "QB1")
            for m in range(4):
                if kn_free[m]:
                    pe.wait_ge(act_s, A.at(kn_free[m]))
                for i in range(2):
                    h = 2 * m + i
                    last = nc.tensor.matmul(wk[kn_bank[m]][0:64, i * SEQ:(i + 1) * SEQ],
                                            ukv_w[:, h * 128:h * 128 + NOPE], ckvT, start=True, stop=True)
                last.then_inc(pe_s, PE.done(f"KN{m}"))
            uv = ukv_w.rearrange("p (h d) -> p h d", h=HEADS)[:, :, NOPE:]
            for c in range(TC):
                pe.wait_ge(act_s, A.at("KN0")) if c == 0 else pe.wait_ge(dve_s, V.at("KN1"))
                nc.tensor.matmul(wk[2 if c == 0 else 0][:, :], ckvT[:, tok(c)], uv, start=True, stop=True
                                 ).then_inc(pe_s, PE.done(f"VM{c}"))
            pe.wait_ge(pe_s, PE.at("VM1"))
            pe.wait_ge(dve_s, V.at("rope1"))
            pe.sem_inc(even_used, 1)
            qt_bank = (1, 3, 2, 0)
            for m in range(4):
                if m == 0:
                    pe.wait_ge(act_s, A.at("KN2"))
                elif m == 1:
                    pe.wait_ge(dve_s, V.at("KN3"))
                elif m == 2:
                    pe.wait_ge(act_s, A.at("VM0"))
                else:
                    pe.wait_ge(dve_s, V.at("VM1"))
                for i in range(2):
                    h = 2 * m + i
                    for c in range(TC):
                        last = nc.tensor.transpose(wk[qt_bank[m]][0:QK, i * SEQ + c * P:i * SEQ + (c + 1) * P],
                                                   q_tok[:, c, h * QK:(h + 1) * QK], ident)
                last.then_inc(pe_s, PE.done(f"QT{m}"))

            pe.wait_ge(act_s, A.at("QT2"))
            pe.wait_ge(dve_s, V.at("QT3"))
            s_bank = (wk[0], wk[1], acc[2], acc[3])

            def scores(a):
                b = s_bank[a % DEEP]
                if a >= DEEP:
                    pe.wait_ge(dve_s, V.at(f"s{a - DEEP}"))
                for c, lo, n in SEG:
                    if a < 8:
                        last = nc.tensor.matmul(b[:, lo:lo + n], q96T[0:QK, a, tok(c)], k96T[0:QK, a, 0:n],
                                                start=True, stop=True)
                    else:
                        h = a - 8
                        r = 64 * (h % 2)
                        nc.tensor.matmul(b[:, lo:lo + n], qfT[r:r + 64, h // 2, tok(c)], kfT[r:r + 64, h // 2, 0:n],
                                         start=True, stop=False)
                        last = nc.tensor.matmul(b[:, lo:lo + n], pick[r:r + 40, h:h + 1].broadcast_to([40, P]),
                                                nc_parts[r:r + 40, 0:n], start=False, stop=True)
                last.then_inc(pe_s, PE.done(f"S{a}"))

            def weigh(a):
                ob = weighed(a // 2)
                pe.wait_ge(act_s, A.at(f"p{a}"))
                if a == 14:
                    pe.wait_ge(dve_s, V.at("s13"))
                elif a % 2 == 0 and a >= 4:
                    pe.wait_ge(dve_s, V.at(f"o{a // 2 - 2}"))
                h = a % 8
                v = vm if a < 8 else vf
                r = 64 * (a % 2)
                nc.tensor.matmul(ob[r:r + 64, 0:SEQ], v[:, 0, h * 64:(h + 1) * 64], probT[:, a % 2, 0:256],
                                 start=True, stop=False)
                nc.tensor.matmul(ob[r:r + 64, P:SEQ], v[:, 1, h * 64:(h + 1) * 64], probT[:, a % 2, 256:384],
                                 start=False, stop=True).then_inc(pe_s, PE.done(f"O{a}"))

            def seed(c, hf):
                nc.tensor.matmul(acc[2 * c + hf][:, :], ident, x[:, c, hf * 512:(hf + 1) * 512],
                                 start=True, stop=False, skip_group_check=True)

            def seed_wide():
                for c in range(TC):
                    for hf in range(2):
                        seed(c, hf)

            def even_out(u, c, hf, first, n):
                hi, lo = (shaped(part[s_], UNIT, 4) for s_ in even_parts(5 + u))
                cols = slice(hf * 512, (hf + 1) * 512)
                return split_project(acc[2 * c + hf][:, :],
                                     lambda k: tuple(o_[:, 4 * u + first + k, tok(c)] for o_ in (oh, ol)),
                                     lambda k: (hi[:, first + k, cols], lo[:, first + k, cols]),
                                     n=n, first=False, last_one=(u == 1 and first + n == 4))

            for a in range(3):
                scores(a)
            for a in range(16):
                tb = turned(a)
                pe.wait_ge(pool_s, G.at(f"n{a}"))
                if a >= 2:
                    pe.wait_ge(act_s, A.at(f"p{a - 2}"))
                if a == 13:
                    pe.wait_ge(dve_s, V.at("s12"))
                for k in range(3):
                    last = nc.tensor.transpose(tb[:, k * P:(k + 1) * P], prob[:, a % DEEP, k * P:(k + 1) * P], ident)
                last.then_inc(pe_s, PE.done(f"T{a}"))
                if a < 13:
                    scores(a + 3)
                if a:
                    weigh(a - 1)
                if a == 13:
                    even_half(5)(3)
                    pe.wait_ge(dve_s, V.at("o3"))
                    seed(0, 0)
                    even_out(0, 0, 0, 0, 4)
                if a == 14:
                    pe.wait_ge(dve_s, V.at("s14"))
                    seed(1, 0)
                    even_out(0, 1, 0, 0, 4)
                if a == 15:
                    pe.wait_ge(dve_s, V.at("o5"))
                    seed(0, 1)
                    even_out(0, 0, 1, 0, 4)
            weigh(15)
            pe.wait_ge(dve_s, V.at("s15"))
            seed(1, 1)
            even_out(0, 1, 1, 0, 4).then_inc(even_used, 1)
            even_half(6)(3)
            for c in range(TC):
                for hf in range(2):
                    even_out(1, c, hf, 0, 2)
            pe.wait_ge(dve_s, V.at("o7"))
            for c in range(TC):
                even_out(1, c, 0, 2, 2)
                even_out(1, c, 1, 2, 2).then_inc(pe_s, PE.done(f"OUT0:{c}"))
            pe.wait_ge(pe_s, PE.at("OUT0:1"))
            pe.sem_inc(even_used, 1)

            def experts(l):
                m = M[l]
                e_ = f"ffn{l}"
                transposed_norm(e_)
                pe.wait_ge(ready, 5)
                for c in range(TC):
                    normed(e_, c)
                    last = project(wk[0][:, c * 64:c * 64 + NR], lambda k: xnT[:, k, tok(c)], lambda k: wr[:, l, k, :])
                last.then_inc(pe_s, PE.done(f"lg{l}"))
                seed_wide()
                pe.wait_ge(dve_s, V.at(f"asg{l}"))
                a_ = [asg[:, c, :, :].rearrange("p g j -> p (g j)") for c in range(TC)]
                nc.tensor.matmul(wk[1][:, 0:32], C("tri"), a_[0], start=True, stop=True)
                nc.tensor.matmul(wk[1][:, 32:64], C("tri"), a_[1], start=True, stop=False)
                nc.tensor.matmul(wk[1][:, 32:64], all_ones, a_[0], start=False, stop=True)
                nc.tensor.matmul(wk[1][:, 64:96], all_ones, a_[0], start=True, stop=False)
                nc.tensor.matmul(wk[1][:, 64:96], all_ones, a_[1], start=False, stop=True).then_inc(pe_s, PE.done(f"rk{l}"))
                for n in ("hidT_ready", "y_ready", "combined"):
                    pe.sem_inc(m[n], 1)
                pe.wait_ge(rounds_set[l], 1)
                nr = pe.value_load(rounds[0:1, l:l + 1], min_val=1, max_val=ROUNDS)
                with pe.Fori(0, nr) as r:
                    with pe.Fori(0, GROUPS) as i:
                        it = r * GROUPS + i

                        def here(idx):
                            pe.wait_ge(moe_here[l][moe_slot(l, idx)], it * 48 + 16 * (idx // RING + 1))

                        def combine(quad):
                            pe.wait_ge(m["y_copied"], (it * PER + 4 * quad) * 2 + 9)
                            pe.wait_ge(m["g_copied"], it * 2 + (quad + 2))
                            for c in range(TC):
                                for hf in range(2):
                                    last = nc.tensor.matmul(acc[2 * c + hf][:, :], gT[:, tok(c)],
                                                            ye[:, hf * 512:(hf + 1) * 512],
                                                            start=False, stop=False, skip_group_check=True)
                                last.then_inc(m["combined0" if c == 0 else "combined"], 1)

                        pe.wait_ge(m["sel_ready"], it + 1)
                        for e in range(PER):
                            n_ = it * PER + e
                            quad = e // 4
                            if e % 4 == 0:
                                pe.wait_ge(m["g_copied"], it * 2 + (quad + 1))
                                for half in range(2):
                                    b = wk[2 - half]
                                    for k in range(4):
                                        for c in range(TC):
                                            last = nc.tensor.matmul(
                                                b[:, k * P:(k + 1) * P], xn[:, c, 4 * half + k, :],
                                                sel[:, c, 4 * quad:4 * quad + 4, :].rearrange("p e s -> p (e s)"),
                                                start=(c == 0), stop=(c == TC - 1))
                                    last.then_inc(m["gath_ready"], 1)
                            xe = xg[:, quad, :, (e % 4) * SLOTS:(e % 4 + 1) * SLOTS]

                            def up_or_gate(part):
                                here(3 * e + part)
                                w_ = wide(moe_slot(l, 3 * e + part))
                                for k in range(DC):
                                    if part == 0 and e % 4 == 0 and k % 4 == 0:
                                        pe.wait_ge(m[f"xg_copied{k // 4}"], it * 2 + (quad + 1))
                                    for j in range(4):
                                        last = nc.tensor.matmul(wk[0][32 * j:32 * j + 32, part * P:(part + 1) * P],
                                                                xe[:, k, :], w_[:, k, j * P:(j + 1) * P],
                                                                start=(k == 0), stop=(k == DC - 1))
                                return last

                            up_or_gate(0).then_inc(moe_used[l], 1)
                            if e % 4 == 0:
                                pe.wait_ge(m["gsel_ready"], it + 1)
                                for c in range(TC):
                                    last = nc.tensor.matmul(
                                        wk[1][:, tok(c)], gsel[:, c, e:e + 4, :].rearrange("p e s -> p (e s)"),
                                        ident, start=True, stop=True)
                                last.then_inc(m["g_ready"], 1)
                            up_or_gate(1).then_inc(m["gu_ready"], 1)
                            if e == 4:
                                combine(0)
                            pe.wait_ge(m["hid_done"], n_ + 2)
                            pe.sem_inc(moe_used[l], 1)
                            nc.tensor.transpose(wk[2][:, 0:P], hid, ident).then_inc(m["hidT_ready"], 1)
                            here(3 * e + 2)
                            pe.wait_ge(m["hidT_copied"], n_ + 1)
                            pe.wait_ge(m["y_copied"], n_ * 2 + 1)
                            wd = tall(moe_slot(l, 3 * e + 2))
                            for k in range(4):
                                for j in range(4):
                                    last = nc.tensor.matmul(wk[3][32 * j:32 * j + 32, 0:256], hidT[:, k, :],
                                                            wd[:, k, j * 256:(j + 1) * 256],
                                                            start=(k == 0), stop=(k == 3))
                            last.then_inc(m["y_ready"], 1)
                            pe.wait_ge(m["y_ready"], n_ + 2)
                            pe.sem_inc(moe_used[l], 1)
                        combine(1)

            experts(0)

            transposed_norm("mix1")
            pe.wait_ge(dve_s, V.at("mix1:x1"))
            pe.wait_ge(act_s, A.at("mix1:sa1"))
            seed_wide()
            pe.wait_ge(dve_s, V.at("mix1:xl3"))
            pe.sem_inc(odd_used, 2)
            with pe.Fori(0, RH // 2) as i:
                def fill(name, hp):
                    b, k = odd_use(name, hp)
                    pe.wait_ge(odd_drained[b], i * 6 + (k + 1))
                    return wk[b], odd_filled[b]

                def parts(kind, hp):
                    j = ODD_ORDER.index((kind, hp))
                    hi, lo = (shaped(part[s_], UNIT, 4 if kind == "wo" else DC) for s_ in odd_parts(j))

                    def quarter(n):
                        pe.wait_ge(odd_low, i * 32 + (4 * j + n + 1))
                    return hi, lo, quarter

                def used(name, hp):
                    b, k = odd_use(name, hp)
                    pe.wait_ge(odd_filled[b], i * 6 + (k + 1))
                    pe.sem_inc(odd_used, 1)

                def qk(hp):
                    hi, lo, quarter = parts("qk", hp)
                    for j, name in enumerate("qk"):
                        b, f = fill(name, hp)
                        for m_ in range(2):
                            cols = slice(j * RQK + m_ * P, j * RQK + (m_ + 1) * P)
                            last = split_project(b[:, m_ * SEQ:(m_ + 1) * SEQ],
                                                 lambda k: (hi[:, k, cols], lo[:, k, cols]), x_all, quarter, 4)
                        last.then_inc(f, 1)
                    used("k", hp)

                def token_major(kind, hp, between=None):
                    hi, lo, quarter = parts(kind, hp)
                    for c in range(TC):
                        if c and between:
                            between(hp)
                        b, f = fill(f"{kind}{c}", hp)
                        split_project(b[:, :], x_tok(c), lambda k: (hi[:, k, :], lo[:, k, :]), quarter, 4
                                      ).then_inc(f, 1)
                    used(f"{kind}1", hp)

                def ret_scores(hp):
                    pe.wait_ge(O["qT_done"], i * 2 + (hp + 1))
                    pe.wait_ge(O["kT_done"], i * 2 + (hp + 1))
                    for s in range(2):
                        b, f = fill(f"S{s}", hp)
                        for m_ in range(2):
                            last = nc.tensor.matmul(b[:, 0:SEQ - s * P], kT[:, m_, tok(s)], qT[:, m_, s * P:SEQ],
                                                    start=(m_ == 0), stop=(m_ == 1))
                        last.then_inc(f, 1)

                def ret_out(hp):
                    pe.wait_ge(O["sT_done"], i * 4 + (2 * hp + 2))
                    pe.wait_ge(O["v_done"], i * 4 + (2 * hp + 2))
                    b, f = fill("O0", hp)
                    nc.tensor.matmul(b[:, :], sT[:, 0:128], vr[:, 0, :], start=True, stop=True).then_inc(f, 1)
                    b, f = fill("O1", hp)
                    nc.tensor.matmul(b[:, :], sT[:, 128:256], vr[:, 0, :], start=True, stop=False)
                    nc.tensor.matmul(b[:, :], sT[:, 256:384], vr[:, 1, :], start=False, stop=True).then_inc(f, 1)

                def turn(hp):
                    for c in range(TC):
                        pe.wait_ge(O["y_done"], i * 4 + (2 * hp + c + 1))
                        b, f = fill(f"T{c}", hp)
                        for k in range(4):
                            last = nc.tensor.transpose(b[:, k * P:(k + 1) * P], yr[:, c, k * P:(k + 1) * P], ident)
                        last.then_inc(f, 1)

                def out_proj(hp):
                    hi, lo, quarter = parts("wo", hp)
                    for c in range(TC):
                        pe.wait_ge(O["yT_done"], i * 4 + (2 * hp + c + 1))
                        for hf in range(2):
                            cols = slice(hf * 512, (hf + 1) * 512)
                            last = split_project(acc[2 * c + hf][:, :], lambda k: (yh[:, c, k, :], yl[:, c, k, :]),
                                                 lambda k: (hi[:, k, cols], lo[:, k, cols]), quarter, 4,
                                                 n=4, first=False, last_one=False)
                        last.then_inc(O[f"out{c}"], 1)
                    pe.wait_ge(O["out1"], i * 2 + (hp + 1))
                    pe.sem_inc(odd_used, 1)

                qk(0)
                token_major("v", 0)
                ret_scores(0)
                token_major("g", 0, ret_out)
                qk(1)
                turn(0)
                out_proj(0)
                token_major("v", 1)
                ret_scores(1)
                token_major("g", 1, ret_out)
                turn(1)
                out_proj(1)
            experts(1)

        @block.scalar
        def _(act):
            links = [0]

            def link(ins):
                links[0] += 1
                ins.then_inc(chain_a, 1)
                act.wait_ge(chain_a, links[0])

            warmed = [0]

            def preload(function):
                k = warmed[0]
                warmed[0] += 1
                nc.scalar.activation(warm[:, 1 + k:2 + k], warm[:, 0:1], function)

            def norm_stats(e, arrived):
                for c in range(TC):
                    arrived(c)

                    def squares(half, sums):
                        src = x[:, c, half * 512:(half + 1) * 512] if e == "mix0" else acc[2 * c + half][:, :]
                        return nc.scalar.activation(xn[:, c, 4 * half:4 * half + 4, :].rearrange("p a b -> p (a b)"),
                                                    src, ACT.Square, accum_out=sums[:, c:c + 1])

                    if e != "mix0":
                        squares(1, s2).then_inc(act_s, A.done(f"{e}:sb{c}"))
                    if e in SUMMED:
                        act.wait_ge(dve_s, V.at(f"{e}:xa{c}"))
                    squares(0, ss).then_inc(act_s, A.done(f"{e}:sa{c}"))
                    act.wait_ge(act_s, A.at(f"{e}:sa{c}"))
                    act.wait_ge(dve_s, V.at(f"{e}:b{c}"))
                    nc.scalar.activation(std[:, c:c + 1], ss[:, c:c + 1], ACT.Sqrt, scale=1.0 / D,
                                         bias=ms[:, c:c + 1]).then_inc(act_s, A.done(f"{e}:std{c}"))

            def drain_xT(e):
                for c in range(TC):
                    act.wait_ge(pe_s, PE.at(f"{e}:xT{2 * c}"))
                    nc.scalar.activation(xnT[:, 0:4, c * P:(c + 1) * P],
                                         wk[2 * c][:, :].rearrange("p (k t) -> p k t", k=4),
                                         ACT.Copy).then_inc(act_s, A.done(f"{e}:xT{2 * c}"))

            def high(u_slot, h_slot, n, first, done, pieces=2, which=None):
                for i in range(pieces) if which is None else (which,):
                    if i == 0:
                        first()
                    cols = slice(i * n // pieces, (i + 1) * n // pieces)
                    nc.scalar.activation(part[h_slot][:, cols], ring[:, u_slot, cols], ACT.Copy).then_inc(done, 1)

            def even_high_of(u, pieces=2, which=None):
                h_slot, u_slot = even_parts(u)
                high(u_slot, h_slot, UNIT, lambda: act.wait_ge(even_here[u], 16), even_high, pieces, which)

            def high_xT(e):
                for b in range(4):
                    act.wait_ge(pe_s, PE.at(f"{e}:xT{b}"))
                    c, half = b // 2, b % 2
                    nc.scalar.activation(xh[:, 4 * half:4 * half + 4, c * P:(c + 1) * P],
                                         wk[b][:, :].rearrange("p (k t) -> p k t", k=4),
                                         ACT.Copy).then_inc(act_s, A.done(f"{e}:xh{b}"))

            act.wait_ge(ready, 1)
            preload(ACT.Sqrt)
            norm_stats("mix0", lambda c: act.wait_ge(x_in_sem[c], 16))
            drain_xT("mix0")
            act.wait_ge(const_in, 16)
            nc.scalar.activation(pick[:, :], C("pick"), ACT.Copy)
            link(nc.scalar.activation(nc_parts[:, :], const[:, 0:SEQ], ACT.Copy, scale=0.0))
            act.wait_ge(act_s, A.at("mix0:xT2"))
            act.wait_ge(dve_s, V.at("mix0:xT3"))
            for i in range(2):
                nc.scalar.activation(exh[:, 4 * i:4 * i + 4, :], xnT[:, 4 * i:4 * i + 4, :], ACT.Copy
                                     ).then_inc(act_s, A.done(f"exh{i}"))
            even_high_of(1)
            for c in range(TC):
                act.wait_ge(pe_s, PE.at(f"Z{c}"))
                nc.scalar.activation(zc[:, c, :], wk[c][:, 0:ZC], ACT.Copy).then_inc(act_s, A.done(f"Z{c}"))
            act.wait_ge(act_s, A.at("Z1"))
            for c in range(TC):
                nc.scalar.activation(cqT[:, c, :], zc[:, c, 0:Q_LORA], ACT.Square, accum_out=s4[:, 2 * c:2 * c + 1])
                last = nc.scalar.activation(probT[:, c, 0:KV_LORA], zc[:, c, Q_LORA:Q_LORA + KV_LORA], ACT.Square,
                                            accum_out=s4[:, 2 * c + 1:2 * c + 2])
            last.then_inc(act_s, A.done("sq4"))
            even_high_of(2)
            half8 = FOX ** -0.5

            def drain_qf(b):
                act.wait_ge(pe_s, PE.at(f"QF{b}"))
                nc.scalar.activation(qfT[:, 2 * b:2 * b + 2, :], wk[2 + b][:, :].rearrange("p (c t) -> p c t", c=2),
                                     ACT.Copy, scale=half8).then_inc(act_s, A.done(f"QF{b}"))

            drain_qf(0)
            act.wait_ge(dve_s, V.at("zlog"))
            nc.scalar.activation(zabs, zlog, ACT.Abs).then_inc(act_s, A.done("zabs"))
            act.wait_ge(act_s, A.at("zabs"))
            nc.scalar.activation(zexp, zabs, ACT.Exp, scale=-1.0).then_inc(act_s, A.done("zexp"))
            act.wait_ge(act_s, A.at("zexp"))
            nc.scalar.activation(zabs, zexp, ACT.Ln, bias=ones[:, 0:1]).then_inc(act_s, A.done("zln"))
            act.wait_ge(dve_s, V.at("ms4"))
            nc.scalar.activation(r4, s4, ACT.Sqrt).then_inc(act_s, A.done("std4"))
            preload(ACT.Exp)
            drain_qf(1)
            act.wait_ge(pe_s, PE.at("QF1"))
            even_high_of(3)
            act.wait_ge(pe_s, PE.at("VF0"))
            nc.scalar.activation(vf[:, 0, :], wk[2][:, :], ACT.Copy).then_inc(act_s, A.done("VF0"))
            act.wait_ge(pe_s, PE.at("CT"))
            for r in (0, 64):
                last = nc.scalar.activation(nc_parts[r:r + 8, :], wk[1][0:8, 0:SEQ], ACT.Copy, scale=-1.0)
            last.then_inc(act_s, A.done("CT"))
            act.wait_ge(pe_s, PE.at("CQ"))
            nc.scalar.activation(cqT, wk[0][:, :].rearrange("p (c t) -> p c t", c=2), ACT.Copy
                                 ).then_inc(act_s, A.done("CQ"))
            act.wait_ge(pe_s, PE.at("CK"))
            act.wait_ge(dve_s, V.at("CK"))
            nc.scalar.activation(k96T[64:96, :, :], wk[2][64:96, None, SEQ:2 * SEQ].broadcast_to([32, HEADS, SEQ]),
                                 ACT.Copy).then_inc(act_s, A.done("kpe"))
            banks = {"QA0": 3, "QB0": 0, "QA1": 1, "QB1": 3}
            for c in range(TC):
                for i, name in enumerate(("QA", "QB")):
                    act.wait_ge(pe_s, PE.at(f"{name}{c}"))
                    nc.scalar.activation(q_tok[:, c, i * 384:(i + 1) * 384], wk[banks[f"{name}{c}"]][:, 0:384], ACT.Copy,
                                         scale=QK ** -0.5).then_inc(act_s, A.done(f"{name}{c}"))
            for m_, b in ((0, 2), (2, 1)):
                act.wait_ge(pe_s, PE.at(f"KN{m_}"))
                nc.scalar.activation(k96T[0:64, 2 * m_:2 * m_ + 2, :], wk[b][0:64, :].rearrange("p (c t) -> p c t", c=2),
                                     ACT.Copy).then_inc(act_s, A.done(f"KN{m_}"))
            act.wait_ge(pe_s, PE.at("VM0"))
            nc.scalar.activation(vm[:, 0, :], wk[2][:, :], ACT.Copy).then_inc(act_s, A.done("VM0"))
            for m_, b in ((0, 1), (2, 2)):
                act.wait_ge(pe_s, PE.at(f"QT{m_}"))
                nc.scalar.activation(q96T[0:QK, 2 * m_:2 * m_ + 2, :], wk[b][0:QK, :].rearrange("p (c t) -> p c t", c=2),
                                     ACT.Copy).then_inc(act_s, A.done(f"QT{m_}"))

            def drain_probT(a):
                act.wait_ge(pe_s, PE.at(f"T{a}"))
                if a >= 2:
                    act.wait_ge(pe_s, PE.at(f"O{a - 2}"))
                nc.scalar.activation(probT[:, a % 2, :], turned(a)[:, 0:384], ACT.Copy
                                     ).then_inc(act_s, A.done(f"p{a}"))

            for a in range(16):
                act.wait_ge(dve_s, V.at(f"m{a}"))
                for c, lo, n in SEG:
                    last = nc.scalar.activation(prob[:, a % DEEP, lo:lo + n], prob[:, a % DEEP, lo:lo + n], ACT.Exp,
                                                bias=nmx[:, a % DEEP, c:c + 1], accum_out=sm[:, a % DEEP, c:c + 1])
                last.then_inc(act_s, A.done(f"e{a}"))
                if a > 1:
                    drain_probT(a - 2)
                if 2 <= a < 10:
                    act.wait_ge(pe_s, PE.at("VF1"))
                    even_high_of(5 + (a - 2) // 4, 4, (a - 2) % 4)
            drain_probT(14)
            drain_probT(15)

            preload(ACT.Sqrt)
            def experts(l, arrived):
                m = M[l]
                norm_stats(f"ffn{l}", arrived)
                preload(ACT.Exp)
                drain_xT(f"ffn{l}")
                act.wait_ge(dve_s, V.at(f"gd{l}"))
                for c in range(TC):
                    last = nc.scalar.activation(t4[:, c, :], t4[:, c, :], ACT.Exp, accum_out=sg4[:, c:c + 1])
                last.then_inc(act_s, A.done(f"ge{l}"))
                act.wait_ge(dve_s, V.at(f"ed{l}"))
                for c in range(TC):
                    nc.scalar.activation(t8[:, c, :], t8[:, c, :], ACT.Exp, accum_out=sg8[:, c:c + 1])
                nc.scalar.activation(p2, p2, ACT.Exp).then_inc(act_s, A.done(f"ee{l}"))
                preload(ACT.Silu)
                act.wait_ge(rounds_set[l], 1)
                nr = act.value_load(rounds[0:1, l:l + 1], min_val=1, max_val=ROUNDS)
                with act.Fori(0, nr) as r:
                    with act.Fori(0, GROUPS) as i:
                        it = r * GROUPS + i
                        for e in range(PER):
                            n_ = it * PER + e
                            if e % 4 == 0:
                                act.wait_ge(m["gath_ready"], it * 4 + (e // 2 + 1))
                                nc.scalar.activation(xg[:, e // 4, 0:4, :],
                                                     wk[2][:, :].rearrange("p (c s) -> p c s", c=4), ACT.Copy
                                                     ).then_inc(m["xg_copied0"], 1)
                            act.wait_ge(m["gu_ready"], n_ + 1)
                            act.wait_ge(m["hid_done"], n_ + 1)
                            nc.scalar.activation(act_g, wk[0][:, 0:P], ACT.Silu
                                                 ).then_inc(m["silu_done"], 1)
                            act.wait_ge(m["hidT_ready"], n_ + 2)
                            act.wait_ge(m["y_ready"], n_ + 1)
                            nc.scalar.activation(hidT.rearrange("p k s -> p (k s)"), wk[2][:, 0:P], ACT.Copy
                                                 ).then_inc(m["hidT_copied"], 1)
                            act.wait_ge(m["y_ready"], n_ + 2)
                            if e % 4 == 0:
                                act.wait_ge(m["combined"], it * 2 + (e // 4 + 1))
                            q = slice(32 * (e % 4), 32 * (e % 4) + 32)
                            for j in range(2):
                                last = nc.scalar.activation(ye[q, j * 256:(j + 1) * 256],
                                                            wk[3][32 * j:32 * j + 32, 0:256], ACT.Copy)
                            last.then_inc(m["y_copied"], 1)
                preload(ACT.Sqrt)
                return lambda c: act.wait_ge(m["combined0" if c == 0 else "combined"], nr * (GROUPS * 2) + c)

            summed = experts(0, lambda c: act.wait_ge(pe_s, PE.at(f"OUT0:{c}")))

            norm_stats("mix1", summed)
            preload(ACT.Silu)
            high_xT("mix1")
            for b in range(4):
                act.sem_inc(odd_drained[b], 1)
            with act.Fori(0, RH // 2) as i:
                def got(name, hp):
                    b, k = odd_use(name, hp)
                    act.wait_ge(odd_filled[b], i * 6 + (k + 1))
                    return wk[b], odd_drained[b]

                def values(hp):
                    for c in range(TC):
                        b, d = got(f"v{c}", hp)
                        ins = nc.scalar.activation(vr[:, c, :], b[:, :], ACT.Copy)
                        ins.then_inc(d, 1)
                    act.wait_ge(d, i * 6 + (odd_use("v1", hp)[1] + 2))
                    act.sem_inc(O["v_done"], 2)

                def gate(hp):
                    for c in range(TC):
                        b, d = got(f"g{c}", hp)
                        nc.scalar.activation(sg[:, c, :], b[:, :], ACT.Silu).then_inc(d, 1)
                        act.wait_ge(d, i * 6 + (odd_use(f"g{c}", hp)[1] + 2))
                        act.sem_inc(O["sg_done"], 1)

                def stats(hp):
                    for c in range(TC):
                        b, _ = got(f"O{c}", hp)
                        nc.scalar.activation(yr[:, c, :], b[:, :], ACT.Square, accum_out=ss[:, c:c + 1]
                                             ).then_inc(O["sq_done"], 1)
                    act.wait_ge(O["ms_done"], i * 2 + (hp + 1))
                    nc.scalar.activation(std, ms, ACT.Sqrt).then_inc(O["std_done"], 1)

                def high_T(hp):
                    for c in range(TC):
                        b, _ = got(f"T{c}", hp)
                        nc.scalar.activation(yh[:, c, :, :].rearrange("p k t -> p (k t)"), b[:, :], ACT.Copy
                                             ).then_inc(O["yh_done"], 1)

                def odd_high_of(j):
                    kind = ODD_ORDER[j][0]
                    h_slot, s_ = odd_parts(j)

                    def first():
                        per = 48 if j % 4 in (0, 3) else 32
                        act.wait_ge(odd_here[s_], i * per + (per if j >= 4 else (32 if kind == "qk" else 16)))
                        act.wait_ge(odd_used, i * RING + (j + 1))
                    high(s_, h_slot, UNIT, first, odd_high, 4)

                odd_high_of(0)
                odd_high_of(1)
                odd_high_of(2)
                values(0)
                odd_high_of(3)
                stats(0)
                gate(0)
                odd_high_of(4)
                high_T(0)
                odd_high_of(5)
                odd_high_of(6)
                values(1)
                odd_high_of(7)
                stats(1)
                gate(1)
                high_T(1)
            preload(ACT.Sqrt)
            summed = experts(1, lambda c: act.wait_ge(O[f"out{c}"], RH))
            norm_stats("fin", summed)

        @block.vector
        def _(dve):
            links = [0]

            def link(ins):
                links[0] += 1
                ins.then_inc(chain_v, 1)
                dve.wait_ge(chain_v, links[0])

            tt, ts, stt = nc.vector.tensor_tensor, nc.vector.tensor_scalar, nc.vector.scalar_tensor_tensor

            def norm(e, arrived, slot, gain_loaded, loads=1):
                for c in range(TC):
                    arrived(c)
                    if e in SUMMED:
                        nc.vector.tensor_copy(x[:, c, 0:512], acc[2 * c][:, :]).then_inc(dve_s, V.done(f"{e}:xa{c}"))
                    if e == "mix0":
                        link(stt(xn[:, c, 4:8, :].rearrange("p a b -> p (a b)"), x[:, c, 512:], 1.0, x[:, c, 512:],
                                 ALU.mult, ALU.mult, accum_out=s2[:, c:c + 1]))
                    else:
                        dve.wait_ge(act_s, A.at(f"{e}:sb{c}"))
                    ts(ms[:, c:c + 1], s2[:, c:c + 1], 1.0 / D, EPS, ALU.mult, ALU.add
                       ).then_inc(dve_s, V.done(f"{e}:b{c}"))
                    if e in SUMMED:
                        nc.vector.tensor_copy(x[:, c, 512:], acc[2 * c + 1][:, :]).then_inc(dve_s, V.done(f"{e}:x{c}"))
                        dve.wait_ge(dve_s, V.at(f"{e}:x{c}"))
                    dve.wait_ge(act_s, A.at(f"{e}:std{c}"))
                    link(nc.vector.reciprocal(rstd[:, c:c + 1], std[:, c:c + 1]))
                    if c == 0:
                        dve.wait_ge(gain_loaded, 16 * loads)
                    if e == "fin":
                        for hf in range(2):
                            cols = slice(hf * 512, (hf + 1) * 512)
                            last = stt(x[:, c, cols], acc[2 * c + hf][:, :], rstd[:, c:c + 1], gain[:, slot, cols],
                                       ALU.mult, ALU.mult)
                        last.then_inc(dve_s, V.done(f"{e}:xn{c}"))
                    else:
                        stt(xn[:, c, :, :], x[:, c, :].rearrange("p (a b) -> p b a", b=DC), rstd[:, c:c + 1],
                            gain[:, slot, :].rearrange("p (a b) -> p b a", b=DC), ALU.mult, ALU.mult
                            ).then_inc(dve_s, V.done(f"{e}:xn{c}"))

            def drain_xT(e):
                for c in range(TC):
                    dve.wait_ge(pe_s, PE.at(f"{e}:xT{2 * c + 1}"))
                    nc.vector.tensor_copy(xnT[:, 4:8, c * P:(c + 1) * P],
                                          wk[2 * c + 1][:, :].rearrange("p (k t) -> p k t", k=4)
                                          ).then_inc(dve_s, V.done(f"{e}:xT{2 * c + 1}"))

            def drain(dst, name, src):
                dve.wait_ge(pe_s, PE.at(name))
                nc.vector.tensor_copy(dst, src).then_inc(dve_s, V.done(name))

            def low(u_slot, h_slot, n, highs, done, pieces=2, which=None):
                for i in range(pieces) if which is None else (which,):
                    cols = slice(i * n // pieces, (i + 1) * n // pieces)
                    highs(i)
                    tt(part[u_slot][:, cols], ring[:, u_slot, cols], part[h_slot][:, cols].bitcast(F32), ALU.subtract
                       ).then_inc(done, 1)

            def even_low_of(u, pieces=2, which=None):
                h_slot, u_slot = even_parts(u)
                low(u_slot, h_slot, UNIT, lambda i: dve.wait_ge(even_high, split_before(u) + i + 1), even_low, pieces,
                    which)

            def low_xT(e):
                for b in range(4):
                    dve.wait_ge(act_s, A.at(f"{e}:xh{b}"))
                    c, half = b // 2, b % 2
                    if half == 0:
                        dve.wait_ge(pe_s, PE.at(f"{e}:xT{2 * c + 1}"))
                    tt(xl[:, c, 4 * half:4 * half + 4, :], wk[b][:, :].rearrange("p (k t) -> p k t", k=4),
                       xh[:, 4 * half:4 * half + 4, c * P:(c + 1) * P].bitcast(F32), ALU.subtract
                       ).then_inc(dve_s, V.done(f"{e}:xl{b}"))

            norm("mix0", lambda c: dve.wait_ge(x_in_sem[c], 16), 0, first_gain_in)
            drain_xT("mix0")
            for i in range(2):
                dve.wait_ge(act_s, A.at(f"exh{i}"))
                tt(exl[:, 4 * i:4 * i + 4, :], xnT[:, 4 * i:4 * i + 4, :], exh[:, 4 * i:4 * i + 4, :].bitcast(F32),
                   ALU.subtract).then_inc(dve_s, V.done(f"exl{i}"))
            even_low_of(1)
            dve.wait_ge(const_in, 16)
            dve.wait_ge(act_s, A.at("Z1"))
            dve.wait_ge(small_in, 16 * 7)
            tt(zlog, zc[:, :, FQ:ZC], bf[:, None, :].broadcast_to([P, TC, HEADS]), ALU.add).then_inc(dve_s, V.done("zlog"))
            dve.wait_ge(act_s, A.at("sq4"))
            lat = s4.rearrange("p (c k) -> p c k", c=TC)
            link(ts(lat[:, :, 0], lat[:, :, 0], 1.0 / Q_LORA, EPS, ALU.mult, ALU.add))
            ts(lat[:, :, 1], lat[:, :, 1], 1.0 / KV_LORA, EPS, ALU.mult, ALU.add).then_inc(dve_s, V.done("ms4"))
            two = lambda b: b[:, :].rearrange("p (c t) -> p c t", c=2)
            even_low_of(2)
            even_low_of(3)
            drain(kfT[:, 0:2, :], "KF0", two(wk[0]))
            drain(kfT[:, 2:4, :], "KF1", two(wk[1]))
            dve.wait_ge(act_s, A.at("zln"))
            stt(logf, zlog, 0.0, zabs, ALU.min, ALU.subtract).then_inc(dve_s, V.done("logf"))
            drain(vf[:, 1, :], "VF1", wk[3][:, :])
            dve.wait_ge(act_s, A.at("std4"))
            link(nc.vector.reciprocal(r4, r4))
            for c in range(TC):
                stt(zc[:, c, 0:Q_LORA], zc[:, c, 0:Q_LORA], r4[:, 2 * c:2 * c + 1], lnqkv[:, 0:Q_LORA], ALU.mult, ALU.mult)
                last = stt(zc[:, c, Q_LORA:Q_LORA + KV_LORA], zc[:, c, Q_LORA:Q_LORA + KV_LORA],
                           r4[:, 2 * c + 1:2 * c + 2], lnqkv[:, Q_LORA:], ALU.mult, ALU.mult)
            last.then_inc(dve_s, V.done("cqn"))

            def rope(parts, heads, cos, sin, name):
                a = ropek[:, 0:0 + heads * 32]
                bb = tmp_rope[:, 0:heads * 32]
                a4 = a.rearrange("p (h k f) -> p h k f", h=heads, k=2)
                b4 = bb.rearrange("p (h k f) -> p h k f", h=heads, k=2)
                tt(a4, parts, cos, ALU.mult)
                link(tt(b4, parts, sin, ALU.mult))
                tt(parts[:, :, 0, :], a4[:, :, 0, :], b4[:, :, 1, :], ALU.subtract)
                return tt(parts[:, :, 1, :], b4[:, :, 0, :], a4[:, :, 1, :], ALU.add)

            tmp_rope = probT.rearrange("p b n -> p (b n)")

            def phase(name, c=None, heads=HEADS):
                v = C(name).rearrange("p (c f) -> p c f", c=TC)
                if c is None:
                    return v[:, :, None, :].broadcast_to([P, TC, 2, 16])
                return v[:, c:c + 1, None, :].broadcast_to([P, heads, 2, 16])

            rope(zc[:, :, FQ - ROPE:FQ].rearrange("p c (k f) -> p c k f", k=2), TC, phase("cos"), phase("sin"), "kpe"
                 ).then_inc(dve_s, V.done("kpe"))
            dve.wait_ge(dve_s, V.at("kpe"))
            dve.wait_ge(pe_s, PE.at("CU"))
            nc.vector.tensor_copy(cum.rearrange("p c h -> p (c h)"), wk[0][:, 0:16]).then_inc(dve_s, V.done("CU"))
            dve.wait_ge(act_s, A.at("CT"))
            for r in (0, 64):
                last = stt(nc_parts[r + 32:r + 40, :], wk[1][0:8, 0:SEQ], -1.0, nc_parts[0:8, :].bitcast(F32),
                           ALU.mult, ALU.subtract)
            last.then_inc(dve_s, V.done("CTl"))
            drain(ckvT, "CK", wk[2][:, 0:SEQ])
            for c in range(TC):
                dve.wait_ge(act_s, A.at(f"QB{c}"))
                parts = q_tok[:, c, :].rearrange("p (h n) -> p h n", h=HEADS)[:, :, NOPE:].rearrange(
                    "p h (k f) -> p h k f", k=2)
                rope(parts, HEADS, phase("cos", c), phase("sin", c), f"rope{c}").then_inc(dve_s, V.done(f"rope{c}"))
                dve.wait_ge(dve_s, V.at(f"rope{c}"))
            drain(k96T[0:64, 2:4, :], "KN1", two(wk[0])[0:64])
            drain(k96T[0:64, 6:8, :], "KN3", two(wk[3])[0:64])
            drain(vm[:, 1, :], "VM1", wk[0][:, :])
            drain(q96T[0:QK, 2:4, :], "QT1", two(wk[3])[0:QK])
            drain(q96T[0:QK, 6:8, :], "QT3", two(wk[0])[0:QK])

            def drain_o(pair):
                dve.wait_ge(pe_s, PE.at(f"O{2 * pair + 1}"))
                bank = weighed(pair)[:, 0:SEQ]
                nc.vector.tensor_copy(oh[:, pair, :], bank).then_inc(dve_s, V.done(f"oh{pair}"))
                dve.wait_ge(dve_s, V.at(f"oh{pair}"))
                tt(ol[:, pair, :], bank, oh[:, pair, :].bitcast(F32), ALU.subtract).then_inc(dve_s, V.done(f"o{pair}"))

            def invert(a):
                dve.wait_ge(act_s, A.at(f"e{a}"))
                nc.vector.reciprocal(rsm[:, a % DEEP, :], sm[:, a % DEEP, :]).then_inc(dve_s, V.done(f"r{a}"))

            for a in range(16):
                dve.wait_ge(pe_s, PE.at(f"S{a}"))
                sc = (wk[0], wk[1], acc[2], acc[3])[a % DEEP]
                pr = prob[:, a % DEEP, :]
                if a >= DEEP:
                    dve.wait_ge(pe_s, PE.at(f"T{a - DEEP}"))
                if a < 8:
                    ins = tt(pr, sc[:, 0:384], C("mla"), ALU.add)
                else:
                    for c, lo, n in SEG:
                        ins = stt(pr[:, lo:lo + n], sc[:, lo:lo + n], cum[:, c, a - 8:a - 7],
                                  C("fox")[:, lo:lo + n], ALU.add, ALU.add)
                ins.then_inc(dve_s, V.done(f"s{a}"))
                dve.wait_ge(dve_s, V.at(f"s{a}"))
                for c, lo, n in SEG:
                    ins = nc.vector.reduce_max(mx[:, a % DEEP, c:c + 1], pr[:, lo:lo + n], AX.X)
                link(ins)
                ts(nmx[:, a % DEEP, :], mx[:, a % DEEP, :], -1.0, None, ALU.mult).then_inc(dve_s, V.done(f"m{a}"))
                if a:
                    invert(a - 1)
                if a % 2 == 0 and a > 2:
                    drain_o(a // 2 - 2)
                if 3 <= a < 11:
                    even_low_of(5 + (a - 3) // 4, 4, (a - 3) % 4)
            invert(15)
            drain_o(6)
            drain_o(7)

            def experts(l, arrived):
                m = M[l]
                norm(f"ffn{l}", arrived, 1, gain_in[1], l + 1)
                drain_xT(f"ffn{l}")
                dve.wait_ge(pe_s, PE.at(f"lg{l}"))
                logits = wk[0][:, 0:128].rearrange("p (c n) -> p c n", c=TC)[:, :, 0:NR]
                link(tt(lg, logits, br[:, l:l + 1, :].broadcast_to([P, TC, NR]), ALU.add))
                gl = lg[:, :, 0:GROUPS]

                def first_max(dst, vals, best, arg, n, t):
                    link(tt(t, vals, wide_of(best, n), ALU.is_equal))
                    ar = C(arg)[:, None, :].broadcast_to([P, TC, n])
                    link(tt(t, t, ar, ALU.mult))
                    link(nc.vector.tensor_reduce(first, t, AX.X, ALU.min))
                    link(tt(dst, ar, wide_of(first, n), ALU.is_equal))

                link(nc.vector.reduce_max(gmax, gl, AX.X))
                first_max(oh4, gl, gmax, "arg4", GROUPS, t4)
                tt(t4, gl, wide_of(gmax, GROUPS), ALU.subtract).then_inc(dve_s, V.done(f"gd{l}"))
                ea = lg[:, :, GROUPS:].rearrange("p c (g j) -> p c g j", g=GROUPS)
                link(tt(tmp, ea, oh4[:, :, :, None].broadcast_to([P, TC, GROUPS, PER]), ALU.mult))
                link(nc.vector.reduce_sum(el, tmp.rearrange("p c g j -> p c j g"), AX.X))
                link(nc.vector.reduce_max(m1, el, AX.X))
                first_max(oh8[:, 0], el, m1, "arg8", PER, t8)
                link(stt(el2, oh8[:, 0], -BIG, el, ALU.mult, ALU.add))
                link(nc.vector.reduce_max(m2, el2, AX.X))
                first_max(oh8[:, 1], el2, m2, "arg8", PER, t8)
                tt(t8, el, wide_of(m1, PER), ALU.subtract)
                tt(p2, m2, m1, ALU.subtract).then_inc(dve_s, V.done(f"ed{l}"))
                link(tt(el2, oh8[:, 0], oh8[:, 1], ALU.add))
                tt(asg, four(el2), group_of(oh4), ALU.mult).then_inc(dve_s, V.done(f"asg{l}"))
                dve.wait_ge(act_s, A.at(f"ee{l}"))
                nc.vector.reciprocal(p1, sg4)
                link(nc.vector.reciprocal(pr1, sg8))
                link(tt(pr2, p2, pr1, ALU.mult))
                link(tt(den, pr1, pr2, ALU.add))
                nc.vector.reciprocal(den, den).then_inc(dve_s, V.done(f"den{l}"))
                dve.wait_ge(pe_s, PE.at(f"rk{l}"))
                rank = wk[1][:, 0:64].rearrange("p (c e) -> p c e", c=TC)
                link(nc.vector.reduce_max(mc, wk[1][:, 64:96], AX.X))
                link(ts(rt[0:1, 28:28 + ROUNDS - 1], C("more", 1), mc[0:1, :], None, ALU.is_lt))
                link(nc.vector.reduce_sum(more, rt[0:1, 28:28 + ROUNDS - 1], AX.X))
                ts(rounds[0:1, l:l + 1], more, 1.0, None, ALU.add).then_inc(rounds_set[l], 1)
                link(tt(place, rank, asg.rearrange("p c g j -> p c (g j)"), ALU.mult))
                dve.wait_ge(rounds_set[l], 1)
                for n in ("hid_done", "g_copied", "y_copied"):
                    dve.sem_inc(m[n], 1)
                nr = dve.value_load(rounds[0:1, l:l + 1], min_val=1, max_val=ROUNDS)
                with dve.Fori(0, nr) as r:
                    with dve.Fori(0, GROUPS) as i:
                        it = r * GROUPS + i
                        slots = C("iota")[:, None, :].broadcast_to([P, PER, SLOTS])
                        for c in range(TC):
                            pl = place[:, c, bass.ds(i * PER, PER)][:, :, None].broadcast_to([P, PER, SLOTS])
                            ins = tt(sel[:, c], pl, slots, ALU.is_equal)
                        ins.then_inc(m["sel_ready"], 1)
                        dve.wait_ge(m["sel_ready"], it + 1)
                        dve.wait_ge(pool_s, G.at(f"gates{l}"))
                        for c in range(TC):
                            gt = gates[:, c, bass.ds(i * PER, PER)][:, :, None].broadcast_to([P, PER, SLOTS])
                            ins = tt(gsel[:, c], sel[:, c], gt, ALU.mult)
                        ins.then_inc(m["gsel_ready"], 1)
                        for e in range(PER):
                            n_ = it * PER + e
                            if e % 4 == 0:
                                dve.wait_ge(m["gath_ready"], it * 4 + (e // 2 + 2))
                                nc.vector.tensor_copy(xg[:, e // 4, 4:8, :],
                                                      wk[1][:, :].rearrange("p (c s) -> p c s", c=4)
                                                      ).then_inc(m["xg_copied1"], 1)
                            dve.wait_ge(m["silu_done"], n_ + 1)
                            dve.wait_ge(m["hidT_ready"], n_ + 1)
                            tt(hid, wk[0][:, P:2 * P], act_g, ALU.mult).then_inc(m["hid_done"], 1)
                            if e % 4 == 0:
                                dve.wait_ge(m["g_ready"], it * 2 + (e // 4 + 1))
                                dve.wait_ge(m["combined"], it * 2 + (e // 4 + 1))
                                nc.vector.tensor_copy(gT, wk[1][:, 0:SEQ]).then_inc(m["g_copied"], 1)
                            dve.wait_ge(m["y_ready"], n_ + 2)
                            q = slice(32 * (e % 4), 32 * (e % 4) + 32)
                            for j in range(2, 4):
                                last = nc.vector.tensor_copy(ye[q, j * 256:(j + 1) * 256],
                                                             wk[3][32 * j:32 * j + 32, 0:256])
                            last.then_inc(m["y_copied"], 1)
                    ts(place, place, float(SLOTS), None, ALU.subtract).then_inc(m["place_moved"], 1)
                    dve.wait_ge(m["place_moved"], r + 1)
                return lambda c: dve.wait_ge(m["combined0" if c == 0 else "combined"], nr * (GROUPS * 2) + c)

            summed = experts(0, lambda c: dve.wait_ge(pe_s, PE.at(f"OUT0:{c}")))

            norm("mix1", summed, 0, gain_in[0])
            low_xT("mix1")
            dve.wait_ge(odd_in, 16)
            cosT = odd[:, 0:256][:, None, :].broadcast_to([P, 2, SEQ])
            sinT = odd[:, 256:512][:, None, :].broadcast_to([P, 2, SEQ])
            with dve.Fori(0, RH // 2) as i:
                def got(name, hp):
                    b, k = odd_use(name, hp)
                    dve.wait_ge(odd_filled[b], i * 6 + (k + 1))
                    return wk[b], odd_drained[b]

                def rotate(hp):
                    for j, (name, dst) in enumerate((("q", qT), ("k", kT))):
                        b, d = got(name, hp)
                        src = b[:, :].rearrange("p (m t) -> p m t", m=2)
                        tt(ra, src, cosT, ALU.mult).then_inc(O["ra_done"], 1)
                        tt(rb, src, sinT, ALU.mult).then_inc(d, 1)
                        k = odd_use(name, hp)[1]
                        dve.wait_ge(O["ra_done"], i * 4 + (2 * hp + j + 1))
                        dve.wait_ge(d, i * 6 + (k + 2))
                        tt(dst[:, 0, :], ra[:, 0, :], rb[:, 1, :], ALU.subtract)
                        tt(dst[:, 1, :], rb[:, 0, :], ra[:, 1, :], ALU.add).then_inc(O[f"{name}T_done"], 1)
                        dve.wait_ge(O[f"{name}T_done"], i * 2 + (hp + 1))

                def decay(hp):
                    dec = odd[:, bass.ds(i * 768 + (512 + 384 * hp), 384)]
                    for s in range(2):
                        b, d = got(f"S{s}", hp)
                        w_ = SEQ - s * P
                        tt(sT[:, s * SEQ:s * SEQ + w_], b[:, 0:w_], dec[:, s * SEQ:s * SEQ + w_], ALU.mult).then_inc(d, 1)
                        dve.wait_ge(d, i * 6 + (odd_use(f"S{s}", hp)[1] + 2))
                        dve.sem_inc(O["sT_done"], 1)

                def finish(hp):
                    dve.wait_ge(O["sq_done"], i * 4 + (2 * hp + 2))
                    ts(ms, ss, 1.0 / RV, EPS, ALU.mult, ALU.add).then_inc(O["ms_done"], 1)
                    dve.wait_ge(O["std_done"], i * 2 + (hp + 1))
                    nc.vector.reciprocal(rstd, std).then_inc(O["rs_done"], 1)
                    dve.wait_ge(O["rs_done"], i * 2 + (hp + 1))
                    for c in range(TC):
                        dve.wait_ge(O["sg_done"], i * 4 + (2 * hp + c + 1))
                        b, d = got(f"O{c}", hp)
                        stt(yr[:, c, :], b[:, :], rstd[:, c:c + 1], sg[:, c, :], ALU.mult, ALU.mult).then_inc(d, 1)
                        dve.wait_ge(d, i * 6 + (odd_use(f"O{c}", hp)[1] + 2))
                        dve.sem_inc(O["y_done"], 1)

                def low_T(hp):
                    for c in range(TC):
                        b, d = got(f"T{c}", hp)
                        dve.wait_ge(O["yh_done"], i * 4 + (2 * hp + c + 1))
                        tt(yl[:, c, :, :].rearrange("p k t -> p (k t)"), b[:, :],
                           yh[:, c, :, :].rearrange("p k t -> p (k t)").bitcast(F32), ALU.subtract).then_inc(d, 1)
                        dve.wait_ge(d, i * 6 + (odd_use(f"T{c}", hp)[1] + 2))
                        dve.sem_inc(O["yT_done"], 1)

                def odd_low_of(j):
                    h_slot, s_ = odd_parts(j)
                    low(s_, h_slot, UNIT, lambda n: dve.wait_ge(odd_high, i * 32 + (4 * j + n + 1)), odd_low, 4)

                odd_low_of(0)
                odd_low_of(1)
                rotate(0)
                odd_low_of(2)
                decay(0)
                odd_low_of(3)
                finish(0)
                odd_low_of(4)
                low_T(0)
                rotate(1)
                odd_low_of(5)
                odd_low_of(6)
                decay(1)
                odd_low_of(7)
                finish(1)
                low_T(1)
            summed = experts(1, lambda c: dve.wait_ge(O[f"out{c}"], RH))
            norm("fin", summed, 0, gain_in[0], 2)


_INS = ['x', 'ln_mix_e', 'w_in_e', 'ln_q_e', 'w_uq_e', 'ln_kv_e', 'w_ukv_e', 'b_f_e', 'w_out_e', 'ln_mix_o', 'w_in_o',
        'w_out_o', 'ln_ffn', 'w_rg', 'b_rg', 'w_re', 'b_re', 'w_gate', 'w_up', 'w_down', 'ln_f']


def kernel(**inputs):
    import concourse.bacc as _bacc
    from concourse.bass_utils import run_bass_kernel_spmd as _run

    nc = _bacc.Bacc("TRN2", target_bir_lowering=False, num_devices=1)
    arrays, args = {}, []
    c, o = tables()
    for name, a in [(n, inputs[n]) for n in _INS] + [("consts", c), ("consts_odd", o)]:
        a = np.ascontiguousarray(a)
        arrays[f"in_{name}"] = a
        args.append(nc.dram_tensor(f"in_{name}", a.shape, mybir.dt.from_np(a.dtype), kind="ExternalInput").ap())
    args.append(nc.dram_tensor("out_0", (1, SEQ, D), F32, kind="ExternalOutput").ap())
    build(nc, *args)
    return _run(nc, [arrays], core_ids=[0]).results[0]["out_0"]
```
